# Optimizing a Trainium2 kernel written in Bass

```python
import math
import jax
import jax.numpy as jnp
from jax import lax
import numpy as np

D_MODEL = 1024
BATCH = 1
SEQ = 128
DEPTH = 2
DEC_BATCH = 1
DEC_SEQ = 512
PAST_LEN = 128

GRID_W = 64
HEAD_DIM = 64
ROPE_BASE = 10000.0
Q_BLOCK = 128
NORM_EPS = 1e-6
NEG_INF = -1e30

DA_HEADS = 4
DA_QK = 32
DA_V = 2 * DA_QK
NA_HEADS = 4
NA_WIN_R = 8
NA_WIN_C = 16
NA_QCOLS = 16
NA_KCOLS = 2 * NA_WIN_C
SW_HEADS = 4
SW_KV_HEADS = 2
SW_WINDOW = 128
SW_BLOCK = SW_WINDOW
MLA_HEADS = 4
MLA_Q_RANK = 256
MLA_KV_RANK = 128
MLA_NOPE = 64
MLA_ROPE = 32
MLA_V = 64
N_BRANCH = 4
BRANCH_WIDTH = D_MODEL // 4
N_EXPERTS = 16
EC_CAPACITY = 2
D_EXPERT = 1024

IN_SIZES = (
    DA_HEADS * 2 * DA_QK, DA_HEADS * 2 * DA_QK, DA_HEADS * DA_V,
    NA_HEADS * HEAD_DIM, NA_HEADS * HEAD_DIM, NA_HEADS * HEAD_DIM,
    SW_HEADS * HEAD_DIM, SW_KV_HEADS * HEAD_DIM, SW_KV_HEADS * HEAD_DIM,
    MLA_Q_RANK, MLA_KV_RANK, MLA_ROPE,
)
IN_DIM = sum(IN_SIZES)

kernel_name = "hybrid_diffusion_prefix_step"

def rms_norm(x, g):
    xf = x.astype(jnp.float32)
    y = xf * lax.rsqrt(jnp.mean(xf * xf, axis=-1, keepdims=True) + NORM_EPS)
    return (y * g.astype(jnp.float32)).astype(x.dtype)

def split_cols(u, sizes):
    parts, off = [], 0
    for s in sizes:
        parts.append(u[..., off:off + s])
        off += s
    return parts

def rope_1d(x, pos):
    half = x.shape[-1] // 2
    freqs = jnp.float32(ROPE_BASE) ** (-jnp.arange(half, dtype=jnp.float32) / half)
    ang = pos.astype(jnp.float32)[:, None] * freqs
    ang = ang.reshape((pos.shape[0],) + (1,) * (x.ndim - 3) + (half,))
    cos, sin = jnp.cos(ang), jnp.sin(ang)
    x1 = x[..., :half].astype(jnp.float32)
    x2 = x[..., half:].astype(jnp.float32)
    return jnp.concatenate([x1 * cos - x2 * sin, x2 * cos + x1 * sin], axis=-1).astype(x.dtype)

def rope_2d(x):
    n = x.shape[1]
    t = jnp.arange(n)
    half = x.shape[-1] // 2
    return jnp.concatenate([rope_1d(x[..., :half], t // GRID_W), rope_1d(x[..., half:], t % GRID_W)], axis=-1)

def sweep_query_blocks(fn, q):
    B, N = q.shape[:2]
    nb = N // Q_BLOCK
    qb = jnp.moveaxis(q.reshape((B, nb, Q_BLOCK) + q.shape[2:]), 1, 0)
    out = jnp.moveaxis(lax.map(fn, qb), 0, 1)
    return out.reshape((B, N) + out.shape[3:])

def dense_attention(q, k, v):
    scale = q.shape[-1] ** -0.5

    def block(qb):
        s = jnp.einsum("bqhd,bkhd->bhqk", qb, k, preferred_element_type=jnp.float32) * scale
        p = jax.nn.softmax(s, axis=-1)
        return jnp.einsum("bhqk,bkhd->bqhd", p.astype(v.dtype), v)

    return sweep_query_blocks(block, q)

def diff_attention(q, k, v, lam):
    scale = DA_QK ** -0.5

    def block(qb):
        s = jnp.einsum("bqhmd,bkhmd->bhmqk", qb, k, preferred_element_type=jnp.float32) * scale
        p = jax.nn.softmax(s, axis=-1)
        w = p[:, :, 0] - lam * p[:, :, 1]
        return jnp.einsum("bhqk,bkhd->bqhd", w.astype(v.dtype), v)

    return sweep_query_blocks(block, q)

def sink_softmax(s, sink):
    sink_col = jnp.broadcast_to(sink.astype(jnp.float32), s.shape[:-1] + (1,))
    return jax.nn.softmax(jnp.concatenate([s, sink_col], axis=-1), axis=-1)[..., :-1]

def gqa_sink_dense(q, k, v, sink):
    B, N, H, d = q.shape
    G = H // SW_KV_HEADS
    qg = q.reshape(B, N, SW_KV_HEADS, G, d)
    s = jnp.einsum("bqhgd,bkhd->bhgqk", qg, k, preferred_element_type=jnp.float32) * d ** -0.5
    p = sink_softmax(s, sink.reshape(SW_KV_HEADS, G, 1, 1))
    o = jnp.einsum("bhgqk,bkhd->bqhgd", p.astype(v.dtype), v)
    return o.reshape(B, N, H, d)

def window_gqa_sink(q, k, v, ck, cv, sink):
    B, N, H, d = q.shape
    KVH = SW_KV_HEADS
    G = H // KVH
    blk = SW_BLOCK
    nb = N // blk
    scale = d ** -0.5
    qb = q.reshape(B, nb, blk, KVH, G, d)

    def band(t):
        tp = jnp.pad(t, ((0, 0), (blk, blk), (0, 0), (0, 0))).reshape(B, nb + 2, blk, KVH, d)
        return jnp.concatenate([tp[:, :-2], tp[:, 1:-1], tp[:, 2:]], axis=2)

    kb, vb = band(k), band(v)
    s_loc = jnp.einsum("bnqhgd,bnkhd->bnhgqk", qb, kb, preferred_element_type=jnp.float32) * scale
    qpos = jnp.arange(nb)[:, None] * blk + jnp.arange(blk)
    kpos = jnp.arange(nb)[:, None] * blk - blk + jnp.arange(3 * blk)
    valid = ((kpos[:, None, :] >= 0) & (kpos[:, None, :] < N)
             & (jnp.abs(qpos[:, :, None] - kpos[:, None, :]) <= SW_WINDOW))
    s_loc = jnp.where(valid[None, :, None, None], s_loc, NEG_INF)
    s_ctx = jnp.einsum("bnqhgd,bphd->bnhgqp", qb, ck, preferred_element_type=jnp.float32) * scale
    p = sink_softmax(jnp.concatenate([s_loc, s_ctx], axis=-1), sink.reshape(KVH, G, 1, 1))
    nl = 3 * blk
    o = (jnp.einsum("bnhgqk,bnkhd->bnqhgd", p[..., :nl].astype(v.dtype), vb)
         + jnp.einsum("bnhgqp,bphd->bnqhgd", p[..., nl:].astype(cv.dtype), cv))
    return o.reshape(B, N, H, d)

def neighbourhood_attention(q, k, v, ck, cv, rpb):
    B, N, H, d = q.shape
    R = N // GRID_W
    WR = min(NA_WIN_R, R)
    ncb = GRID_W // NA_QCOLS
    scale = d ** -0.5
    qg = q.reshape(B, R, ncb, NA_QCOLS, H, d)
    kg = k.reshape(B, R, GRID_W, H, d)
    vg = v.reshape(B, R, GRID_W, H, d)
    rows = jnp.arange(R)
    row_start = jnp.clip(rows - WR // 2, 0, R - WR)
    qcol = jnp.arange(GRID_W).reshape(ncb, NA_QCOLS)
    band_start = jnp.clip(jnp.arange(ncb) * NA_QCOLS - NA_WIN_C // 2, 0, GRID_W - NA_KCOLS)
    kcol = band_start[:, None] + jnp.arange(NA_KCOLS)
    col_start = jnp.clip(qcol - NA_WIN_C // 2, 0, GRID_W - NA_WIN_C)
    col_ok = ((kcol[:, None, :] >= col_start[..., None])
              & (kcol[:, None, :] < col_start[..., None] + NA_WIN_C))
    dc_idx = jnp.clip(kcol[:, None, :] - qcol[:, :, None] + NA_WIN_C - 1, 0, 2 * NA_WIN_C - 2)
    n_loc = WR * NA_KCOLS

    def one_row(args):
        r, rs, q_row = args
        kb = lax.dynamic_slice_in_dim(kg, rs, WR, axis=1)[:, :, kcol]
        vb = lax.dynamic_slice_in_dim(vg, rs, WR, axis=1)[:, :, kcol]
        s_loc = jnp.einsum("bjqhd,brjkhd->bhjqrk", q_row, kb, preferred_element_type=jnp.float32) * scale
        dr_idx = rs + jnp.arange(WR) - r + NA_WIN_R - 1
        bias = rpb[:, dr_idx[None, None, :, None], dc_idx[:, :, None, :]]
        s_loc = jnp.where(col_ok[:, :, None, :], s_loc + bias.astype(jnp.float32), NEG_INF)
        s_loc = s_loc.reshape(B, H, ncb, NA_QCOLS, n_loc)
        s_ctx = jnp.einsum("bjqhd,bphd->bhjqp", q_row, ck, preferred_element_type=jnp.float32) * scale
        p = jax.nn.softmax(jnp.concatenate([s_loc, s_ctx], axis=-1), axis=-1)
        p_loc = p[..., :n_loc].reshape(B, H, ncb, NA_QCOLS, WR, NA_KCOLS)
        return (jnp.einsum("bhjqrk,brjkhd->bjqhd", p_loc.astype(vb.dtype), vb)
                + jnp.einsum("bhjqp,bphd->bjqhd", p[..., n_loc:].astype(cv.dtype), cv))

    out = lax.map(one_row, (rows, row_start, jnp.moveaxis(qg, 1, 0)))
    return jnp.moveaxis(out, 0, 1).reshape(B, N, H, d)

def token_mixing(h, lp, lam_init, ctx):
    B, N, _ = h.shape
    latent = ctx is not None
    u = h @ lp["w_in"]
    a_q, a_k, a_v, b_q, b_k, b_v, c_q, c_k, c_v, d_cq, d_ckv, d_kpe = split_cols(u, IN_SIZES)
    a_q = a_q.reshape(B, N, DA_HEADS, 2, DA_QK)
    a_k = a_k.reshape(B, N, DA_HEADS, 2, DA_QK)
    a_v = a_v.reshape(B, N, DA_HEADS, DA_V)
    b_q = b_q.reshape(B, N, NA_HEADS, HEAD_DIM)
    b_k = b_k.reshape(B, N, NA_HEADS, HEAD_DIM)
    b_v = b_v.reshape(B, N, NA_HEADS, HEAD_DIM)
    c_q = c_q.reshape(B, N, SW_HEADS, HEAD_DIM)
    c_k = c_k.reshape(B, N, SW_KV_HEADS, HEAD_DIM)
    c_v = c_v.reshape(B, N, SW_KV_HEADS, HEAD_DIM)
    d_ckv = rms_norm(d_ckv, lp["mla_kv_norm"])
    q_mla = (rms_norm(d_cq, lp["mla_q_norm"]) @ lp["mla_w_uq"]).reshape(B, N, MLA_HEADS, MLA_NOPE + MLA_ROPE)
    q_nope, q_pe = q_mla[..., :MLA_NOPE], q_mla[..., MLA_NOPE:]

    if latent:
        a_q, a_k, c_q, c_k = rope_2d(a_q), rope_2d(a_k), rope_2d(c_q), rope_2d(c_k)
        q_pe = rope_2d(q_pe)
        d_kpe = rope_2d(d_kpe[:, :, None, :])[:, :, 0]
        ctx_t = ctx
        ck_a, cv_a, ck_b, cv_b, ck_c, cv_c, ck_d, kpe_d = ctx
        ka = jnp.concatenate([ck_a.reshape(B, -1, DA_HEADS, 2, DA_QK), a_k], axis=1)
        va = jnp.concatenate([cv_a, a_v], axis=1)
        o_b = neighbourhood_attention(b_q, b_k, b_v, ck_b, cv_b, lp["na_rpb"])
        o_c = window_gqa_sink(c_q, c_k, c_v, ck_c, cv_c, lp["sw_sink"])
        ckv_all = jnp.concatenate([ck_d, d_ckv], axis=1)
        kpe_all = jnp.concatenate([kpe_d, d_kpe], axis=1)
    else:
        ctx_t = (a_k.reshape(B, N, DA_HEADS, 2 * DA_QK), a_v, b_k, b_v, c_k, c_v, d_ckv, d_kpe)
        ka, va = a_k, a_v
        o_b = dense_attention(b_q, b_k, b_v)
        o_c = gqa_sink_dense(c_q, c_k, c_v, lp["sw_sink"])
        ckv_all, kpe_all = d_ckv, d_kpe

    lq1, lk1, lq2, lk2 = lp["da_lambda"].astype(jnp.float32)
    lam = jnp.exp(jnp.sum(lq1 * lk1)) - jnp.exp(jnp.sum(lq2 * lk2)) + lam_init
    o_a = rms_norm(diff_attention(a_q, ka, va, lam), lp["da_subln"]) * (1.0 - lam_init)

    K = ckv_all.shape[1]
    kv = (ckv_all @ lp["mla_w_ukv"]).reshape(B, K, MLA_HEADS, MLA_NOPE + MLA_V)
    k_mla = jnp.concatenate(
        [kv[..., :MLA_NOPE], jnp.broadcast_to(kpe_all[:, :, None, :], (B, K, MLA_HEADS, MLA_ROPE))], axis=-1)
    o_d = dense_attention(jnp.concatenate([q_nope, q_pe], axis=-1), k_mla, kv[..., MLA_NOPE:])

    gates = jax.nn.sigmoid(h @ lp["w_gate"]).reshape(B, N, N_BRANCH, D_MODEL)
    merged = None
    for i, o in enumerate((o_a, o_b, o_c, o_d)):
        term = gates[:, :, i] * (o.reshape(B, N, BRANCH_WIDTH) @ lp["w_branch"][i])
        merged = term if merged is None else merged + term
    return merged @ lp["w_out"], ctx_t

def expert_choice_ffn(h, w_router, w_g, w_u, w_d):
    B, N, D = h.shape
    T = B * N
    xt = h.reshape(T, D)
    aff = jax.nn.softmax((xt @ w_router).astype(jnp.float32), axis=-1)
    cap = EC_CAPACITY * T // N_EXPERTS
    gate, idx = lax.top_k(aff.T, cap)
    xe = xt[idx]
    hg = jnp.einsum("ecd,edf->ecf", xe, w_g)
    hu = jnp.einsum("ecd,edf->ecf", xe, w_u)
    y = jnp.einsum("ecf,efd->ecd", jax.nn.silu(hg) * hu, w_d)
    y = y * gate[..., None].astype(y.dtype)
    out = jnp.zeros_like(xt).at[idx.reshape(-1)].add(y.reshape(-1, D))
    return out.reshape(B, N, D)

def trunk_layer(x, mod, lp, lam_init, ctx):
    shift1, scale1, gate1, shift2, scale2, gate2 = jnp.split(mod, 6, axis=-1)
    h = rms_norm(x, lp["g_norm1"]) * (1 + scale1) + shift1
    mixed, ctx_t = token_mixing(h, lp, lam_init, ctx)
    x = x + gate1 * mixed
    h = rms_norm(x, lp["g_norm2"]) * (1 + scale2) + shift2
    x = x + gate2 * expert_choice_ffn(h, lp["w_router"], lp["w_e_gate"], lp["w_e_up"], lp["w_e_down"])
    return x, ctx_t

def setup_inputs(seed: int = 0) -> dict:
    key = jax.random.key(seed)
    ks = jax.random.split(key, 40)

    def nrm(i, shape, scale):
        return jax.random.normal(ks[i], shape, jnp.float32) * scale

    D, L, P = D_MODEL, DEPTH, PAST_LEN
    dm = D ** -0.5
    return {
        "x_prompt": nrm(0, (BATCH, SEQ, D), 1.0),
        "x_sample": nrm(1, (DEC_BATCH, DEC_SEQ, D), 1.0),
        "cache_diff_k": nrm(2, (DEC_BATCH, L, P, DA_HEADS, 2 * DA_QK), 1.0),
        "cache_diff_v": nrm(3, (DEC_BATCH, L, P, DA_HEADS, DA_V), 1.0),
        "cache_na_k": nrm(4, (DEC_BATCH, L, P, NA_HEADS, HEAD_DIM), 1.0),
        "cache_na_v": nrm(5, (DEC_BATCH, L, P, NA_HEADS, HEAD_DIM), 1.0),
        "cache_swa_k": nrm(6, (DEC_BATCH, L, P, SW_KV_HEADS, HEAD_DIM), 1.0),
        "cache_swa_v": nrm(7, (DEC_BATCH, L, P, SW_KV_HEADS, HEAD_DIM), 1.0),
        "cache_mla_ckv": nrm(8, (DEC_BATCH, L, P, MLA_KV_RANK), 1.0),
        "cache_mla_kpe": nrm(9, (DEC_BATCH, L, P, MLA_ROPE), 1.0),
        "c": nrm(10, (DEC_BATCH, D), 1.0),
        "c_ctx": nrm(11, (D,), 1.0),
        "w_mod": nrm(12, (L, D, 6 * D), 0.5 * dm),
        "b_mod": nrm(13, (L, 6 * D), 0.02),
        "g_norm1": 1.0 + nrm(14, (L, D), 0.02),
        "g_norm2": 1.0 + nrm(15, (L, D), 0.02),
        "w_in": nrm(16, (L, D, IN_DIM), dm),
        "da_lambda": nrm(17, (L, 4, DA_QK), 0.1),
        "da_subln": 1.0 + nrm(18, (L, DA_V), 0.02),
        "na_rpb": nrm(19, (L, NA_HEADS, 2 * NA_WIN_R - 1, 2 * NA_WIN_C - 1), 0.1),
        "sw_sink": nrm(20, (L, SW_HEADS), 0.5),
        "mla_q_norm": 1.0 + nrm(21, (L, MLA_Q_RANK), 0.02),
        "mla_w_uq": nrm(22, (L, MLA_Q_RANK, MLA_HEADS * (MLA_NOPE + MLA_ROPE)), MLA_Q_RANK ** -0.5),
        "mla_kv_norm": 1.0 + nrm(23, (L, MLA_KV_RANK), 0.02),
        "mla_w_ukv": nrm(24, (L, MLA_KV_RANK, MLA_HEADS * (MLA_NOPE + MLA_V)), MLA_KV_RANK ** -0.5),
        "w_gate": nrm(25, (L, D, N_BRANCH * D), dm),
        "w_branch": nrm(26, (L, N_BRANCH, BRANCH_WIDTH, D), BRANCH_WIDTH ** -0.5),
        "w_out": nrm(27, (L, D, D), dm),
        "w_router": nrm(28, (L, D, N_EXPERTS), dm),
        "w_e_gate": nrm(29, (L, N_EXPERTS, D, D_EXPERT), dm),
        "w_e_up": nrm(30, (L, N_EXPERTS, D, D_EXPERT), dm),
        "w_e_down": nrm(31, (L, N_EXPERTS, D_EXPERT, D), D_EXPERT ** -0.5),
        "g_final": 1.0 + nrm(32, (D,), 0.02),
    }

def reference(x_prompt, x_sample, cache_diff_k, cache_diff_v, cache_na_k, cache_na_v, cache_swa_k,
              cache_swa_v, cache_mla_ckv, cache_mla_kpe, c, c_ctx, w_mod, b_mod, g_norm1, g_norm2, w_in,
              da_lambda, da_subln, na_rpb, sw_sink, mla_q_norm, mla_w_uq, mla_kv_norm, mla_w_ukv, w_gate,
              w_branch, w_out, w_router, w_e_gate, w_e_up, w_e_down, g_final):
    xp, xs = x_prompt, x_sample
    ctx_layers = []
    for l in range(DEPTH):
        lp = {
            "g_norm1": g_norm1[l], "g_norm2": g_norm2[l], "w_in": w_in[l],
            "da_lambda": da_lambda[l], "da_subln": da_subln[l], "na_rpb": na_rpb[l], "sw_sink": sw_sink[l],
            "mla_q_norm": mla_q_norm[l], "mla_w_uq": mla_w_uq[l], "mla_kv_norm": mla_kv_norm[l],
            "mla_w_ukv": mla_w_ukv[l], "w_gate": w_gate[l], "w_branch": w_branch[l], "w_out": w_out[l],
            "w_router": w_router[l], "w_e_gate": w_e_gate[l], "w_e_up": w_e_up[l], "w_e_down": w_e_down[l],
        }
        lam_init = 0.8 - 0.6 * math.exp(-0.3 * l)
        mod_ctx = (jax.nn.silu(c_ctx) @ w_mod[l] + b_mod[l])[None, None, :]
        mod_lat = (jax.nn.silu(c) @ w_mod[l] + b_mod[l])[:, None, :]
        xp, ctx_l = trunk_layer(xp, mod_ctx, lp, lam_init, None)
        ctx_layers.append(ctx_l)
        cached_l = (cache_diff_k[:, l], cache_diff_v[:, l], cache_na_k[:, l], cache_na_v[:, l],
                    cache_swa_k[:, l], cache_swa_v[:, l], cache_mla_ckv[:, l], cache_mla_kpe[:, l])
        xs, _ = trunk_layer(xs, mod_lat, lp, lam_init, cached_l)
    y_prompt = rms_norm(xp, g_final)
    y_sample = rms_norm(xs, g_final)
    new_diff_k = jnp.stack([t[0] for t in ctx_layers], axis=1)
    new_diff_v = jnp.stack([t[1] for t in ctx_layers], axis=1)
    new_na_k = jnp.stack([t[2] for t in ctx_layers], axis=1)
    new_na_v = jnp.stack([t[3] for t in ctx_layers], axis=1)
    new_swa_k = jnp.stack([t[4] for t in ctx_layers], axis=1)
    new_swa_v = jnp.stack([t[5] for t in ctx_layers], axis=1)
    new_mla_ckv = jnp.stack([t[6] for t in ctx_layers], axis=1)
    new_mla_kpe = jnp.stack([t[7] for t in ctx_layers], axis=1)
    return (y_prompt, y_sample, new_diff_k, new_diff_v, new_na_k, new_na_v, new_swa_k, new_swa_v,
            new_mla_ckv, new_mla_kpe)


_drawn_inputs = setup_inputs


def setup_inputs(seed=0):
    import zlib

    import numpy as np

    out = dict(_drawn_inputs(seed))
    spreads = {}
    factors = {'cache_na_k': 3.317,
     'cache_na_v': 2.831,
     'cache_swa_k': 4.411,
     'cache_swa_v': 3.775,
     'cache_mla_ckv': 6.661,
     'cache_mla_kpe': 8.0,
     'g_norm1': 2.873,
     'g_norm2': 6.397,
     'da_lambda': 7.957,
     'da_subln': 8.0,
     'na_rpb': 8.0,
     'sw_sink': 64.0,
     'mla_q_norm': 8.0,
     'mla_kv_norm': 2.703,
     'g_final': 2.73,
     'cache_diff_k': 8.0,
     'cache_diff_v': 8.0}
    for name, (base, spread) in spreads.items():
        noise = np.random.default_rng([zlib.crc32(name.encode()), seed]).standard_normal(out[name].shape)
        drawn = base * np.exp(spread * noise) if base else spread * noise
        out[name] = jnp.asarray(drawn.astype(out[name].dtype))
    for name, factor in factors.items():
        out[name] = (out[name] * factor).astype(out[name].dtype)
    return out
```

```python
import math
from contextlib import ExitStack

import numpy as np
import concourse.bass as bass
from concourse import mybir

F32 = mybir.dt.float32
U32 = mybir.dt.uint32
ALU = mybir.AluOpType
ACT = mybir.ActivationFunctionType
AX = mybir.AxisListType

D, L, P = 1024, 2, 128
NS, NP = 512, 128
T = (NS + NP) // P
TS = NS // P
KD = D // P
GRID_W, HEADS, HD, DQK = 64, 4, 64, 32
NOPE, ROPE_D = 64, 32
DM_ = NOPE + ROPE_D
QR, KVR = 256, 128
NE, DE, CAP_S, CAP_P = 16, 1024, 64, 16
CAP = CAP_S + CAP_P
EPS = 1e-6
IN_DIM = 2464
AQ, AK, AV, BQ, BK, BV, CQ, CK, CV, DCQ, DCKV, DKPE = (
    0, 256, 512, 768, 1024, 1280, 1536, 1792, 1920, 2048, 2304, 2432)
DRQ = DKPE - NOPE
NEG = -1e30
LAM_INIT = [0.8 - 0.6 * math.exp(-0.3 * l) for l in range(L)]
NW = 512
KH = KD // 2
RING = 8
WIN_N = [512, 512, 512, 512, IN_DIM - 2048]
N_MOD = 6 * D // NW
NG_IN, NG_GATE = 5, 8
CH_MOD = 2 * N_MOD * L
CH_DENSE = 2 * NG_IN + 2 * NG_GATE + 4
CH_EXP = 12
CH_LAYER = CH_DENSE + NE * CH_EXP

O_COL = {"A": AQ, "B": BQ, "C": CQ, "D": DCQ}
O_BLOCKS = [AQ, AQ + 128, BQ, BQ + 128, CQ, CQ + 128, DCQ, DCQ + 128]
BLOCKS = [("D", 0), ("D", 1), ("D", 2), ("D", 3), ("A", 0), ("B", 0), ("A", 1), ("B", 1), ("C", 0), ("C", 1)]


def plan_units():
    units, passes = [], 0
    for bi, (br, b) in enumerate(BLOCKS):
        for hh in range(1 if br == "D" else 2):
            for m in range(T):
                head = b if br == "D" else 2 * b + hh
                if m == T - 1:
                    kb = [5]
                elif br == "C":
                    kb = [0] + [1 + j for j in range(max(m - 1, 0), min(m + 2, TS))]
                else:
                    kb = [0, 1, 2, 3, 4]
                n = 2 if br == "A" else 1
                if br == "D":
                    rows = [(0, DM_)]
                elif br == "A":
                    rows = [(64 * hh, 32), (64 * hh + 32, 32)]
                else:
                    rows = [(64 * hh, 64)]
                units.append(dict(bi=bi, br=br, b=b, hh=hh, m=m, head=head, kb=kb, rows=rows,
                                  passes=list(range(passes, passes + n))))
                passes += n
    return units, passes


UNITS, N_PASS = plan_units()
N_UNIT = len(UNITS)
UNIT_OF = {p: i for i, u in enumerate(UNITS) for p in u["passes"]}
FIRST_UNIT = {bi: min(i for i, u in enumerate(UNITS) if u["bi"] == bi) for bi in range(len(BLOCKS))}
LAST_UNIT = {bi: max(i for i, u in enumerate(UNITS) if u["bi"] == bi) for bi in range(len(BLOCKS))}
SCALE = {"A": DQK ** -0.5, "B": HD ** -0.5, "C": HD ** -0.5, "D": DM_ ** -0.5}
PREP_AT = {}
for _bi in range(1, len(BLOCKS)):
    for _g in range(4):
        PREP_AT.setdefault(FIRST_UNIT[_bi - 1] + 1 + _g, []).append((_bi, _g))
A_UNITS = [i for i, u in enumerate(UNITS) if u["br"] == "A"]
B_UNITS = [i for i, u in enumerate(UNITS) if u["br"] == "B"]
N_C = sum(1 for u in UNITS if u["br"] == "C")
C_BEFORE = [sum(1 for u in UNITS[:i] if u["br"] == "C") for i in range(N_UNIT + 1)]
ADDS = [sum(1 for r in range(q) if r // T % 4) for q in range(8 * T + 1)]
A_BEFORE = [sum(1 for a in A_UNITS if a < i) for i in range(N_UNIT + 1)]
TAIL_BEFORE = [sum(1 for u in UNITS[:i] if len(u["kb"]) > 4) for i in range(N_UNIT + 1)]


def segments(u):
    out, col = [], 0
    runs = [(0, 1)] if u["kb"][0] == 0 else []
    rest = [k for k in u["kb"] if k]
    runs.append((rest[0], len(rest)))
    for k0, n in runs:
        a, w = k0 * P, n * P
        while w:
            s = min(w, NW - col % NW)
            out.append((col, a, s))
            col, a, w = col + s, a + s, w - s
    return out


def in_fill(l, c):
    g = CH_MOD + l * CH_LAYER + c
    return g, g % RING, g // RING + 1


def hybrid_step(nc, x_prompt, x_sample, cache_diff_k, cache_diff_v, cache_na_k, cache_na_v, cache_swa_k,
                cache_swa_v, cache_mla_ckv, cache_mla_kpe, c, c_ctx, w_mod, b_mod, g_norm1, g_norm2, w_in,
                da_lambda, da_subln, na_rpb, sw_sink, mla_q_norm, mla_w_uq, mla_kv_norm, mla_w_ukv, w_gate,
                w_branch, w_out, w_router, w_e_gate, w_e_up, w_e_down, g_final,
                k_ident, k_rope, k_mask_na, k_mask_sw,
                y_prompt, y_sample, new_diff_k, new_diff_v, new_na_k, new_na_v, new_swa_k, new_swa_v,
                new_mla_ckv, new_mla_kpe):
    ctx = ExitStack()
    with ctx:
        def sb(name, shape, dt=F32):
            return ctx.enter_context(nc.sbuf_tensor(name, shape, dt))

        def sem(name):
            return ctx.enter_context(nc.semaphore(name))

        x_dram = nc.dram_tensor("x_resid", (T * P, D), F32, kind="Internal").ap()
        xn_dram = nc.dram_tensor("x_normed", (T * P, D), F32, kind="Internal").ap()
        mod_dram = nc.dram_tensor("mod_rows", (L, 2, 6 * D), F32, kind="Internal").ap()
        rpb_dram = nc.dram_tensor("rpb_padded", (L, HEADS * 15, 127), F32, kind="Internal").ap()

        ring = sb("ring", [P, RING, KH, NW])
        hT = sb("hT", [P, KD, T * P])
        WORK_N = T * IN_DIM
        work = sb("work", [P, WORK_N])
        ATT_N = 9952
        att = sb("att", [P, ATT_N])
        u = work[:, :].rearrange("p (m n) -> p m n", m=T)
        merged = work[:, 0:T * D].rearrange("p (m n) -> p m n", m=T)
        mergedT = work[:, T * D:2 * T * D].rearrange("p (k n) -> p k n", k=KD)
        sig = work[:, 10240:11264].rearrange("p (b n) -> p b n", b=2)
        gtmp = work[:, 11264:12288].rearrange("p (b n) -> p b n", b=2)
        xt = work[:, 0:2048].rearrange("p (b n) -> p b n", b=2)
        xn = work[:, 2048:4096].rearrange("p (b n) -> p b n", b=2)
        sq = work[:, 4096:5120]
        xe = work[:, 0:2048].rearrange("p (b n) -> p b n", b=2)
        xeT = work[:, 2048:2048 + 2 * KD * CAP].rearrange("p (b k n) -> p b k n", b=2, k=KD)
        hid = work[:, 4096:5120]
        sil = work[:, 5120:6144].rearrange("p (b n) -> p b n", b=2)
        hidT = work[:, 6144:6144 + KD * CAP].rearrange("p (k n) -> p k n", k=KD)
        ybuf = work[:, 7168:9216].rearrange("p (b n) -> p b n", b=2)
        affT = work[0:NE, 9216:9216 + T * P]
        qT = att[:, 0:1280].rearrange("p (b n) -> p b n", b=2)
        kT = att[:, 1280:2816].rearrange("p (b n) -> p b n", b=2)
        prob = att[:, 2816:5376].rearrange("p (b n) -> p b n", b=4)
        cqT = att[:, 2816:4096].rearrange("p (b n) -> p b n", b=2)
        probT = att[:, 5376:6656].rearrange("p (b n) -> p b n", b=2)
        sqs = att[:, 5376:5632]
        na_tab = att[:, 6656:8448].rearrange("p (h n) -> p h n", h=2)
        c_ka, c_va, c_kb, c_vb = (att[:, 8448 + 256 * i:8704 + 256 * i] for i in range(4))
        c_kc, c_vc, c_ckv = (att[:, 9472 + 128 * i:9600 + 128 * i] for i in range(3))
        c_kpe = att[:, 9856:9952]
        oT = att[:, 0:5120].rearrange("p (k n) -> p k n", k=KD)
        gate1_b = att[:, 5120:7168].rearrange("p (g n) -> p g n", g=2)
        gfin_b = att[:, 7168:8192]

        ckvT = sb("ckvT", [P, 6 * P])
        vmla = sb("vmla", [P, 6, 256])
        mask_sw = sb("mask_sw", [P, 2, P])
        mask_na = sb("mask_na", [P, GRID_W])
        rope = sb("rope", [P, TS, 192])
        ident = sb("ident", [P, P])
        w_uq = sb("w_uq", [P, 2, HEADS * DM_])
        w_ukv = sb("w_ukv", [P, 512])
        wb = sb("wb", [P, 2, NW])
        w_r = sb("w_r", [P, KD, NE])
        qn_b = sb("qn_b", [P, QR])
        kvn_b = sb("kvn_b", [P, KVR])
        lam_b = sb("lam_b", [P, 128])
        sub_b = sb("sub_b", [P, HD])
        sink_b = sb("sink_b", [P, HEADS])
        gate2_b = sb("gate2_b", [P, D])
        rtmp = sb("rtmp", [P, 512])
        rtmp2 = sb("rtmp2", [P, 128])
        rpad = sb("rpad", [HEADS * 15, 127])
        rraw = sb("rraw", [HEADS * 15, 31])
        modcol = sb("modcol", [P, L * 6 * KD * 2])
        amod = sb("amod", [P, L * 2 * KD * 2])
        gn_col = sb("gn_col", [P, L * 2, KD])
        cT = sb("cT", [P, 2, KD])
        csT = sb("csT", [P, KD, 2])
        bm = work[0:2, 10240:11264].rearrange("p (b n) -> p b n", b=2)
        modrow = work[0:2, 11264:12288].rearrange("p (b n) -> p b n", b=2)
        st = sb("st", [P, 160])
        ss, var, sd, rstd = st[:, 0:5], st[:, 5:10], st[:, 10:15], st[:, 15:20]
        s10, v10, r10 = st[:, 20:30], st[:, 30:40], st[:, 40:50]
        s20, v20, r20 = st[:, 50:70], st[:, 70:90], st[:, 90:110]
        mx, negm, sm = st[:, 110:118], st[:, 118:126], st[:, 126:134]
        rinv, cmap, es = st[:, 134:142], st[:, 142:146], st[:, 154:158]
        lam, neglam = st[:, 148:150], st[:, 150:151]
        lg = sb("lg", [P, T, NE])
        lgs = sb("lgs", [P, 2, T])
        top_v = sb("top_v", [NE, CAP])
        top_i = sb("top_i", [NE, CAP], U32)
        top_f = sb("top_f", [NE, CAP])
        gateT = sb("gateT", [CAP, NE + 1])
        idxT = sb("idxT", [CAP, NE + 1], U32)
        gate_c = sb("gate_c", [CAP, 2])
        idx_c = sb("idx_c", [CAP, 2, 2], U32)
        ps = [ctx.enter_context(nc.psum_tensor(f"bank{i}", [P, 1024], F32)) for i in range(4)]

        def bank(i, a=0, b=NW):
            return ps[i // 2][:, NW * (i % 2) + a:NW * (i % 2) + b]

        const_in = sem("const_in")
        ring_full = [sem(f"ring_full{i}") for i in range(RING)]
        ring_used = sem("ring_used")
        wb_full = sem("wb_full")
        small_in = sem("small_in")
        bm_full = [sem(f"bm_full{i}") for i in range(2)]
        cs_ready = sem("cs_ready")
        mod_row, mod_tr, mod_col = sem("mod_row"), sem("mod_tr"), sem("mod_col")
        mod_out = [sem(f"mod_out{i}") for i in range(2)]
        amod_ready = sem("amod_ready")
        x_in = [sem(f"x_in{i}") for i in range(2)]
        var_ready, sd_ready, xn_ready = sem("var_ready"), sem("sd_ready"), sem("xn_ready")
        norm_tr, norm_act, norm_dve = sem("norm_tr"), sem("norm_act"), sem("norm_dve")
        u_full, u_act, u_dve = sem("u_full"), sem("u_act"), sem("u_dve")
        c_var, c_sd, cn_ready = sem("c_var"), sem("c_sd"), sem("cn_ready")
        kpe_ready = sem("kpe_ready")
        rope_a = sem("rope_a")
        kv_out = sem("kv_out")
        x_out, xn_out, y_done = ([sem(f"{n}{i}") for i in range(2)] for n in ("x_out", "xn_out", "y_done"))
        ct_tr, ct_ev = sem("ct_tr"), sem("ct_ev")
        qm_full, qm_ready = sem("qm_full"), sem("qm_ready")
        vm_full, vm_ev = sem("vm_full"), sem("vm_ev")
        lam_z, lam_e, lam_ready = sem("lam_z"), sem("lam_e"), sem("lam_ready")
        prep_tr, prep_ev = sem("prep_tr"), sem("prep_ev")
        s_full, s_max, p_ready, w_ready = sem("s_full"), sem("s_max"), sem("p_ready"), sem("w_ready")
        es_ready = sem("es_ready")
        t_full, t_act, t_dve = sem("t_full"), sem("t_act"), sem("t_dve")
        o_full, o_ev = sem("o_full"), sem("o_ev")
        pad_ready, pad_out, rpb_in = sem("pad_ready"), sem("pad_out"), sem("rpb_in")
        natab_in, natab_ready = sem("natab_in"), sem("natab_ready")
        on_var, on_sd, on_ready = sem("on_var"), sem("on_sd"), sem("on_ready")
        ot_tr, ot_act, ot_dve = sem("ot_tr"), sem("ot_act"), sem("ot_dve")
        g_full, g_sig, g_mul, g_add = sem("g_full"), sem("g_sig"), sem("g_mul"), sem("g_add")
        mt_tr, mt_act, mt_dve = sem("mt_tr"), sem("mt_act"), sem("mt_dve")
        wo_full, x_new = sem("wo_full"), sem("x_new")
        gate1_in, gate2_in, gfin_in = sem("gate1_in"), sem("gate2_in"), sem("gfin_in")
        lg_full, lg_sub, lg_exp, aff_ready = sem("lg_full"), sem("lg_sub"), sem("lg_exp"), sem("aff_ready")
        affT_tr, top_ready, topT_tr, topT_ready = sem("affT_tr"), sem("top_ready"), sem("topT_tr"), sem("topT_ready")
        idx_ready = sem("idx_ready")
        xe_in = [sem(f"xe_in{i}") for i in range(2)]
        xe_tr, xe_ready = sem("xe_tr"), sem("xe_ready")
        silu_ready, hid_ready = sem("silu_ready"), sem("hid_ready")
        hid_tr, hidT_act, hidT_dve = sem("hid_tr"), sem("hidT_act"), sem("hidT_dve")
        y_ready, y_out, added = sem("y_ready"), sem("y_out"), sem("added")
        pe_held, pool_held = sem("pe_held"), sem("pool_held")
        dve_step, pool_step, exp_step = sem("dve_step"), sem("pool_step"), sem("exp_step")

        N_CONST = 6 + 2 * L
        N_SMALL = 18
        N_KV = 8
        BUF = 2

        def tok_in(l, m):
            if l == 0:
                return x_sample[0, m * P:(m + 1) * P, :] if m < TS else x_prompt[0]
            return x_dram[m * P:(m + 1) * P, :]

        def x_fill(q, m):
            return 16 * ((3 if m % 2 == 0 else 2) * q + m // 2 + 1)

        def w_chunk(w, n0, width, kh):
            return w.rearrange("(k p) n -> p k n", p=P)[:, kh * KH:(kh + 1) * KH, n0:n0 + width]

        def u_counts(l, g):
            return 13 * l + g // 2 + 1, 12 * l + (g + 1) // 2

        def k_src(br, b, kb):
            if br == "A":
                return c_ka[:, 128 * b:128 * b + 128] if kb == 0 else u[:, kb - 1, AK + 128 * b:AK + 128 * b + 128]
            if br == "B":
                return c_kb[:, 128 * b:128 * b + 128] if kb == 0 else u[:, kb - 1, BK + 128 * b:BK + 128 * b + 128]
            return c_kc[:, :] if kb == 0 else u[:, kb - 1, CK:CK + 128]

        def v_src(un, kb):
            h = un["head"]
            if un["br"] == "D":
                return vmla[:, kb, 64 * h:64 * h + 64]
            if un["br"] == "C":
                h = h // 2
            cv, off = {"A": (c_va, AV), "B": (c_vb, BV), "C": (c_vc, CV)}[un["br"]]
            return cv[:, 64 * h:64 * h + 64] if kb == 0 else u[:, kb - 1, off + 64 * h:off + 64 * h + 64]

        def gain_col(l, w, k, m):
            a = ((l * 2 + w) * KD + k) * 2 + (1 if m < TS else 0)
            return amod[:, a:a + 1]

        def shift_col(l, w, k, m):
            a = ((l * 6 + 3 * w) * KD + k) * 2 + (1 if m < TS else 0)
            return modcol[:, a:a + 1]

        block = ctx.enter_context(nc.Block())

        @block.sync
        def _(sp):
            sp.dma_start(ident[:, :], k_ident).then_inc(const_in, 16)
            with nc.allow_non_contiguous_dma("columns of small vectors"):
                sp.dma_start(cT[:, 0, :], c_ctx.rearrange("(k p) -> p k", p=P)).then_inc(const_in, 16)
                sp.dma_start(cT[:, 1, :], c[0].rearrange("(k p) -> p k", p=P)).then_inc(const_in, 16)
                for w, g in ((0, g_norm1), (1, g_norm2)):
                    for l in range(L):
                        sp.dma_start(gn_col[:, 2 * l + w, :], g[l].rearrange("(k p) -> p k", p=P)).then_inc(const_in, 16)
            sp.dma_start(rope[:, :, :], k_rope.rearrange("(m p) n -> p m n", p=P)).then_inc(const_in, 16)
            sp.dma_start(mask_na[:, :], k_mask_na).then_inc(const_in, 16)
            sp.dma_start(mask_sw[:, :, :], k_mask_sw).then_inc(const_in, 16)

            def fill(slot, src, used, width=NW):
                if used is not None:
                    sp.wait_ge(ring_used, used)
                sp.dma_start(ring[:, slot, :, 0:width], src).then_inc(ring_full[slot], 16)

            for l in range(L):
                w3 = w_mod[l].rearrange("(k p) n -> p k n", p=P)
                first = 1 if l == 0 else 0
                if first:
                    for j in range(8):
                        fill(j, w3[:, (j % 2) * KH:(j % 2 + 1) * KH, (j // 2) * NW:(j // 2 + 1) * NW], None)
                with sp.Fori(first, N_MOD // 4) as i:
                    for j in range(8):
                        fill(j, w3[:, (j % 2) * KH:(j % 2 + 1) * KH, bass.ds((i * 4 + j // 2) * NW, NW)],
                             i * 8 + (l * 2 * N_MOD + j - RING + 1))
            for l in range(L):
                if l:
                    sp.wait_ge(ot_tr, 2 * T * l)
                    sp.wait_ge(lg_full, l)
                    sp.wait_ge(on_ready, T * l)
                row = lambda a: a.rearrange("(a n) -> a n", a=1)
                small = [
                    (qn_b[:, :], row(mla_q_norm[l]).broadcast_to([P, QR])),
                    (kvn_b[:, :], row(mla_kv_norm[l]).broadcast_to([P, KVR])),
                    (lam_b[:, :], da_lambda[l].rearrange("a n -> (a n)").rearrange("(a n) -> a n", a=1).broadcast_to([P, 128])),
                    (sub_b[:, :], row(da_subln[l]).broadcast_to([P, HD])),
                    (sink_b[:, :], row(sw_sink[l]).broadcast_to([P, HEADS])),
                    (w_uq[:, :, :], mla_w_uq[l].rearrange("(k p) n -> p k n", p=P)),
                    (w_ukv[:, :], mla_w_ukv[l]),
                    (w_r[:, :, :], w_router[l].rearrange("(k p) n -> p k n", p=P)),
                    (rraw[:, :], na_rpb[l].rearrange("h a b -> (h a) b")),
                ]
                for dst, src in small:
                    sp.dma_start(dst, src).then_inc(small_in, 16)
                if l:
                    sp.wait_ge(x_new, T * l)
                for dst, src in [
                    (c_ka, cache_diff_k[0, l].rearrange("t h n -> t (h n)")),
                    (c_va, cache_diff_v[0, l].rearrange("t h n -> t (h n)")),
                    (c_kb, cache_na_k[0, l].rearrange("t h n -> t (h n)")),
                    (c_vb, cache_na_v[0, l].rearrange("t h n -> t (h n)")),
                    (c_kc, cache_swa_k[0, l].rearrange("t h n -> t (h n)")),
                    (c_vc, cache_swa_v[0, l].rearrange("t h n -> t (h n)")),
                    (c_ckv, cache_mla_ckv[0, l]),
                    (c_kpe[:, 0:64], cache_mla_ckv[0, l][:, 0:64]),
                    (c_kpe[:, 64:96], cache_mla_kpe[0, l]),
                ]:
                    sp.dma_start(dst, src).then_inc(small_in, 16)
                n = 0

                def dense(w, n0, width=NW):
                    nonlocal n
                    for kh in range(2):
                        g, slot, _ = in_fill(l, n)
                        fill(slot, w_chunk(w, n0, width, kh), g - RING + 1, width)
                        n += 1

                for j in range(NG_IN):
                    dense(w_in[l], j * NW, WIN_N[j])
                for j in range(NG_GATE):
                    half, br = j // 4, j % 4
                    dense(w_gate[l], br * D + half * NW)
                    if NG_GATE * l + j:
                        sp.wait_ge(g_full, T * (NG_GATE * l + j))
                    sp.dma_start(wb[:, :, :], w_branch[l, br].rearrange("(k p) n -> p k n", p=P)[:, :, half * NW:(half + 1) * NW]).then_inc(wb_full, 16)
                for j in range(2):
                    dense(w_out[l], j * NW)
                g0 = CH_MOD + l * CH_LAYER + CH_DENSE
                with sp.Fori(0, NE // 2) as i:
                    for e in range(2):
                        for j in range(CH_EXP):
                            w = (w_e_gate, w_e_gate, w_e_up, w_e_up, w_e_down, w_e_down)[j // 2]
                            half = j // 2 % 2
                            g = g0 + e * CH_EXP + j
                            src = w[l].rearrange("e (k p) n -> p e k n", p=P)[
                                :, bass.ds(i * 2 + e, 1), (j % 2) * KH:(j % 2 + 1) * KH, half * NW:(half + 1) * NW]
                            fill(g % RING, src.rearrange("p e k n -> p (e k) n"), i * (2 * CH_EXP) + (g - RING + 1))

        @block.tensor
        def _(pe):
            mm, tr = nc.tensor.matmul, nc.tensor.transpose

            def chunk(l, cidx):
                _, slot, k = in_fill(l, cidx)
                pe.wait_ge(ring_full[slot], 16 * k)
                return ring[:, slot, :, :]

            def turn4(dst, src, done):
                for k in range(4):
                    ins = tr(dst(k), src(k), ident[:, :])
                ins.then_inc(done, 1)

            pe.wait_ge(const_in, 16 * N_CONST)
            pe.wait_ge(cs_ready, 2)
            pe.sem_inc(mod_tr, BUF)
            for l in range(L):
                with pe.Fori(0, N_MOD // 4) as i:
                    def rows(j):
                        if j >= 2:
                            pe.wait_ge(mod_row, i * 4 + (l * N_MOD + j - 1 + BUF))
                        for kh in range(2):
                            pe.wait_ge(ring_full[2 * j + kh], i * 16 + 16 * (l * 3 + 1))
                            for k in range(KH):
                                ins = mm(bank(j % 2)[0:2, :], csT[:, kh * KH + k, :], ring[:, 2 * j + kh, k, :],
                                         start=(kh + k == 0), stop=(kh == 1 and k == KH - 1))
                            ins.then_inc(ring_used, 1)

                    def cols(j):
                        pe.wait_ge(mod_row, i * 4 + (l * N_MOD + j + 1 + BUF))
                        pe.wait_ge(mod_col, i * 4 + (l * N_MOD + j - 1 + BUF))
                        pe.sem_inc(pe_held, 1)
                        for b in range(4):
                            ins = tr(bank(2 + j % 2, 2 * b, 2 * b + 2), modrow[:, j % 2, b * P:(b + 1) * P], ident[0:2, 0:2])
                        ins.then_inc(mod_tr, 1)

                    rows(0)
                    rows(1)
                    cols(0)
                    rows(2)
                    cols(1)
                    rows(3)
                    cols(2)
                    cols(3)
            pe.wait_ge(mod_col, L * N_MOD + BUF)

            for l in range(L):
                q1, q2 = 2 * l, 2 * l + 1

                def norm_turn(q, m, banks):
                    t = T * q + m
                    pe.wait_ge(xn_ready, t + 1)
                    if m >= 2:
                        pe.wait_ge(norm_act, t - 1)
                        pe.wait_ge(norm_dve, t - 1)
                    for half in range(2):
                        b = banks + 2 * (m % 2) + half
                        turn4(lambda k: bank(b, k * P, (k + 1) * P),
                              lambda k: xn[:, m % 2, (4 * half + k) * P:(4 * half + k + 1) * P], norm_tr)

                if l:
                    pe.wait_ge(y_ready, NE * l + 1)
                    pe.wait_ge(xe_ready, 2 * (NE + 1) * l)
                for m in range(T):
                    norm_turn(q1, m, 0)

                for g in range(NG_IN * T):
                    n, m = divmod(g, T)
                    if m == 0:
                        w = [chunk(l, 2 * n), chunk(l, 2 * n + 1)]
                    if n == 0:
                        pe.wait_ge(norm_act, T * q1 + m + 1)
                        pe.wait_ge(norm_dve, T * q1 + m + 1)
                    if g >= 4:
                        a, d = u_counts(l, g - 4)
                        pe.wait_ge(u_act, a)
                        pe.wait_ge(u_dve, d)
                    for k in range(KD):
                        ins = mm(bank(4 + g % 4, 0, WIN_N[n]), hT[:, k, m * P:(m + 1) * P], w[k // KH][:, k % KH, 0:WIN_N[n]],
                                 start=(k == 0), stop=(k == KD - 1))
                        if m == T - 1 and k == KH - 1:
                            ins.then_inc(ring_used, 1)
                        if m == 0 and n and k == 0:
                            ins.then_inc(ring_used, 1)
                    ins.then_inc(u_full, 1)

                for m in range(T + 1):
                    if m < T:
                        pe.wait_ge(cn_ready, T * l + m + 1)
                        pe.wait_ge(kpe_ready, TS * l + min(m + 1, TS))
                    else:
                        pe.wait_ge(small_in, 16 * N_SMALL * (l + 1))
                    if m >= 4:
                        pe.wait_ge(ct_ev, 6 * l + m - 3)
                    b = m % 4
                    ins = tr(bank(b, 2 * P, 3 * P), u[:, m, DCKV:DCKV + P] if m < T else c_ckv, ident[:, :])
                    if m == 0:
                        ins.then_inc(ring_used, 1)
                    if m < T:
                        for k in range(2):
                            tr(bank(b, k * P, (k + 1) * P), u[:, m, DCQ + k * P:DCQ + (k + 1) * P], ident[:, :])
                    tr(bank(b, 3 * P, 4 * P)[0:DM_, :], u[:, m, DRQ:DRQ + DM_] if m < T else c_kpe, ident[:, :]).then_inc(ct_tr, 1)
                pe.wait_ge(u_act, 13 * (l + 1))
                pe.wait_ge(u_dve, 12 * (l + 1))
                for m in range(T):
                    pe.wait_ge(ct_ev, 6 * l + m + 1)
                    if m >= 4:
                        pe.wait_ge(qm_ready, T * l + m - 3)
                    for k in range(2):
                        ins = mm(bank(4 + m % 4, 0, HEADS * DM_), cqT[:, k, m * P:(m + 1) * P], w_uq[:, k, :], start=(k == 0), stop=(k == 1))
                    ins.then_inc(qm_full, 1)
                pe.wait_ge(ct_ev, 6 * l + 6)
                for kb in range(6):
                    ins = mm(bank(kb // 2, 256 * (kb % 2), 256 * (kb % 2) + 256), ckvT[:, kb * P:(kb + 1) * P],
                             w_ukv[:, :].rearrange("p (h n) -> p h n", h=HEADS)[:, :, NOPE:NOPE + HD], start=True, stop=True)
                    if kb % 2:
                        ins.then_inc(vm_full, 1)

                def prep(bi, g):
                    br, b = BLOCKS[bi]
                    if 4 * bi + g:
                        pe.wait_ge(prep_ev, 4 * len(BLOCKS) * l + 4 * bi + g)
                    if bi == 0 and g == 0:
                        pe.wait_ge(qm_ready, T * (l + 1))
                        pe.wait_ge(vm_ev, 3 * (l + 1))
                    if br in "AC" and g == 0:
                        pe.wait_ge(rope_a, TS * (l + 1))
                    if g < 2:
                        for i, m in enumerate(range(4) if g == 0 else [4]):
                            if br == "D":
                                src, n = u[:, m, DCQ + DM_ * b:DCQ + DM_ * (b + 1)], DM_
                            else:
                                src, n = u[:, m, O_COL[br] + P * b:O_COL[br] + P * (b + 1)], P
                            ins = tr(bank(7, i * P, (i + 1) * P)[0:n, :], src, ident[:, :])
                    elif br == "D":
                        a, e = (0, 512) if g == 2 else (512, 768)
                        ins = mm(bank(7, 0, e - a)[0:NOPE, :], w_ukv[:, 128 * b:128 * b + NOPE], ckvT[:, a:e], start=True, stop=True)
                    else:
                        for i, kb in enumerate(range(4) if g == 2 else [4, 5]):
                            ins = tr(bank(7, i * P, (i + 1) * P), k_src(br, b, kb), ident[:, :])
                    ins.then_inc(prep_tr, 1)

                def scores(ui):
                    un = UNITS[ui]
                    if ui == FIRST_UNIT[un["bi"]]:
                        pe.wait_ge(prep_ev, 4 * len(BLOCKS) * l + 4 * (un["bi"] + 1))
                    for (r0, rn), p in zip(un["rows"], un["passes"]):
                        if p >= 2:
                            pe.wait_ge(p_ready, N_PASS * l + p - 1)
                        b = un["bi"] % 2
                        for col, a, w in segments(un):
                            ins = mm(ps[p % 2][:, col:col + w], qT[r0:r0 + rn, b, un["m"] * P:(un["m"] + 1) * P],
                                     kT[r0:r0 + rn, b, a:a + w], start=True, stop=True)
                        ins.then_inc(s_full, 1)

                def turn(ui):
                    un = UNITS[ui]
                    if un["br"] == "A":
                        pe.wait_ge(w_ready, len(A_UNITS) * l + A_BEFORE[ui] + 1)
                    else:
                        pe.wait_ge(p_ready, N_PASS * l + un["passes"][0] + 1)
                    if ui:
                        pe.wait_ge(t_act, N_UNIT * l + ui)
                        pe.wait_ge(t_dve, TAIL_BEFORE[N_UNIT] * l + TAIL_BEFORE[ui])
                    for i in range(len(un["kb"])):
                        ins = tr(ps[2][:, i * P:(i + 1) * P], prob[:, un["passes"][0] % 4, i * P:(i + 1) * P], ident[:, :])
                    ins.then_inc(t_full, 1)

                def values(ui):
                    un = UNITS[ui]
                    pe.wait_ge(t_act, N_UNIT * l + ui + 1)
                    pe.wait_ge(t_dve, TAIL_BEFORE[N_UNIT] * l + TAIL_BEFORE[ui + 1])
                    if ui:
                        pe.wait_ge(o_ev, N_UNIT * l + ui)
                    for i, kb in enumerate(un["kb"]):
                        ins = mm(bank(6, 0, HD), probT[:, ui % 2, i * P:(i + 1) * P], v_src(un, kb),
                                 start=(i == 0), stop=(i == len(un["kb"]) - 1))
                    ins.then_inc(o_full, 1)

                for g in range(4):
                    prep(0, g)
                for ui in range(N_UNIT + 2):
                    if ui < N_UNIT:
                        scores(ui)
                    if 1 <= ui <= N_UNIT:
                        turn(ui - 1)
                    if ui >= 2:
                        values(ui - 2)
                    for bi, g in PREP_AT.get(ui, []):
                        prep(bi, g)

                pe.wait_ge(o_ev, N_UNIT * (l + 1))
                for m in range(T):
                    pe.wait_ge(on_ready, T * l + m + 1)
                    if m >= 2:
                        pe.wait_ge(ot_act, T * l + m - 1)
                        pe.wait_ge(ot_dve, T * l + m - 1)
                    for half in range(2):
                        turn4(lambda k: bank(2 * (m % 2) + half, k * P, (k + 1) * P),
                              lambda k: u[:, m, O_BLOCKS[4 * half + k]:O_BLOCKS[4 * half + k] + P], ot_tr)
                pe.wait_ge(ot_act, T * (l + 1))
                pe.wait_ge(ot_dve, T * (l + 1))

                for j in range(NG_GATE):
                    br = j % 4
                    w = [chunk(l, 2 * NG_IN + 2 * j), chunk(l, 2 * NG_IN + 2 * j + 1)]
                    pe.wait_ge(wb_full, 16 * (NG_GATE * l + j + 1))
                    for m in range(T):
                        q = T * j + m
                        if q >= 2:
                            pe.wait_ge(g_mul, NG_GATE * T * l + q - 1)
                        for k in range(KD):
                            ins = mm(bank(q % 2), hT[:, k, m * P:(m + 1) * P], w[k // KH][:, k % KH, :], start=(k == 0), stop=(k == KD - 1))
                            if m == T - 1 and k in (KH - 1, KD - 1):
                                ins.then_inc(ring_used, 1)
                        for k in range(2):
                            ins = mm(bank(2 + q % 2), oT[:, 2 * br + k, m * P:(m + 1) * P], wb[:, k, :], start=(k == 0), stop=(k == 1))
                        ins.then_inc(g_full, 1)

                for m in range(T):
                    pe.wait_ge(g_add, 6 * T * l + 5 * T + m + 1)
                    if m >= 2:
                        pe.wait_ge(mt_act, T * l + m - 1)
                        pe.wait_ge(mt_dve, T * l + m - 1)
                    for half in range(2):
                        turn4(lambda k: bank(4 + 2 * (m % 2) + half, k * P, (k + 1) * P),
                              lambda k: merged[:, m, (4 * half + k) * P:(4 * half + k + 1) * P], mt_tr)
                pe.wait_ge(g_mul, NG_GATE * T * (l + 1))

                def out_proj(m):
                    pe.wait_ge(mt_act, T * l + m + 1)
                    pe.wait_ge(mt_dve, T * l + m + 1)
                    if m >= 2:
                        pe.wait_ge(x_new, T * l + m - 1)
                    for half in range(2):
                        if m == 0:
                            w_o.extend([chunk(l, CH_DENSE - 4 + 2 * half), chunk(l, CH_DENSE - 4 + 2 * half + 1)])
                        for k in range(KD):
                            ins = mm(bank(2 * (m % 2) + half), mergedT[:, k, m * P:(m + 1) * P], w_o[2 * half + k // KH][:, k % KH, :],
                                     start=(k == 0), stop=(k == KD - 1))
                            if m == T - 1 and k % KH == KH - 1 and (half == 0 or k < KH):
                                ins.then_inc(ring_used, 1)
                    ins.then_inc(wo_full, 1)

                w_o = []
                for m in range(T + 1):
                    if m < T:
                        out_proj(m)
                    if m == 1:
                        pe.wait_ge(mt_act, T * (l + 1))
                        pe.wait_ge(mt_dve, T * (l + 1))
                    if m >= 1:
                        norm_turn(q2, m - 1, 4)

                pe.wait_ge(norm_act, T * (q2 + 1))
                pe.wait_ge(norm_dve, T * (q2 + 1))
                pe.wait_ge(x_new, T * (l + 1))
                for m in range(T):
                    for k in range(KD):
                        ins = mm(bank(0, NE * m, NE * (m + 1)), hT[:, k, m * P:(m + 1) * P], w_r[:, k, :], start=(k == 0), stop=(k == KD - 1))
                        if m == 0 and k == 0:
                            ins.then_inc(ring_used, 1)
                ins.then_inc(lg_full, 1)
                pe.wait_ge(aff_ready, l + 1)
                for m in range(T):
                    ins = tr(bank(1 + m // 4, (m % 4) * P, (m % 4 + 1) * P)[0:NE, :], lg[:, m, :], ident[:, :])
                ins.then_inc(affT_tr, 1)
                pe.wait_ge(top_ready, l + 1)
                tr(bank(3, 0, NE)[0:CAP, :], top_v[:, :], ident[0:NE, 0:NE])
                tr(bank(3, NE, 2 * NE)[0:CAP, :], top_f[:, :], ident[0:NE, 0:NE]).then_inc(topT_tr, 1)

                def rows_turn(b, fills):
                    pe.wait_ge(xe_in[b], fills)
                    for half in range(2):
                        for k in range(4):
                            kk = 4 * half + k
                            ins = tr(bank(6 + half, k * CAP, (k + 1) * CAP), xe[0:CAP, b, kk * P:(kk + 1) * P], ident[0:CAP, 0:CAP])
                        ins.then_inc(xe_tr, 1)

                pe.wait_ge(topT_ready, l + 1)
                rows_turn(0, 16 * (9 * l + 1))
                g0 = CH_MOD + l * CH_LAYER + CH_DENSE
                with pe.Fori(0, NE // 2) as i:
                    for e in range(2):
                        n_exp = i * 2 + (NE * l + e)
                        n_prep = i * 2 + ((NE + 1) * l + e)

                        def part(j, b, stat):
                            g = g0 + e * CH_EXP + j
                            pe.wait_ge(ring_full[g % RING], i * (16 * 2 * CH_EXP // RING) + 16 * (g // RING + 1))
                            for k in range(KH):
                                kk = (j % 2) * KH + k
                                ins = mm(bank(b)[0:CAP, :], stat(kk), ring[:, g % RING, k, :], start=(kk == 0), stop=(kk == KD - 1))
                            ins.then_inc(ring_used, 1)

                        pe.wait_ge(xe_ready, n_prep * 2 + 2)
                        for j in range(4):
                            part(j, j // 2, lambda kk: xeT[:, e, kk, :])
                        rows_turn(1 - e, i * 16 + 16 * (8 * l + 1) if e == 0 else i * 16 + 16 * (9 * l + 2))
                        for j in range(4, 8):
                            part(j, j // 2, lambda kk: xeT[:, e, kk, :])
                        pe.wait_ge(xe_ready, n_prep * 2 + 4)
                        for half in range(2):
                            pe.wait_ge(hid_ready, n_exp * 2 + (half + 1 + BUF))
                            for k in range(4):
                                kk = 4 * half + k
                                ins = tr(bank(6 + half, k * CAP, (k + 1) * CAP), hid[0:CAP, kk * P:(kk + 1) * P], ident[0:CAP, 0:CAP])
                            ins.then_inc(hid_tr, 1)
                        pe.wait_ge(hidT_act, n_exp + 1)
                        pe.wait_ge(hidT_dve, n_exp + 1)
                        pe.wait_ge(y_ready, n_exp + 1)
                        for j in range(8, 12):
                            part(j, j // 2, lambda kk: hidT[:, kk, :])

        @block.scalar
        def _(act):
            A = nc.scalar.activation

            act.wait_ge(const_in, 16 * N_CONST)
            for b in range(2):
                act.sem_inc(mod_out[b], 16)
            for g in range(2):
                A(csT[:, :, g], cT[:, g, :], ACT.Silu).then_inc(cs_ready, 1)
            for l in range(L):
                with act.Fori(0, N_MOD // 4) as i:
                    for j in range(4):
                        act.wait_ge(mod_row, i * 4 + (l * N_MOD + j - 1 + BUF))
                        act.dma_start(bm[:, j % 2, :], b_mod[l:l + 1, bass.ds((i * 4 + j) * NW, NW)].broadcast_to([2, NW])).then_inc(bm_full[j % 2], 16)
                        act.wait_ge(mod_row, i * 4 + (l * N_MOD + j + 1 + BUF))
                        act.dma_start(mod_dram[l][:, bass.ds((i * 4 + j) * NW, NW)], modrow[:, j % 2, :]).then_inc(mod_out[j % 2], 16)
            act.wait_ge(amod_ready, 2 * L)

            for l in range(L):
                q1, q2 = 2 * l, 2 * l + 1

                def std(q, m):
                    t = T * q + m
                    act.wait_ge(var_ready, t + 1)
                    A(sd[:, m:m + 1], var[:, m:m + 1], ACT.Sqrt).then_inc(sd_ready, 1)

                def modulate(q, m, banks):
                    t = T * q + m
                    act.wait_ge(norm_tr, 2 * t + 1)
                    for k in range(4):
                        ins = A(hT[:, k, m * P:(m + 1) * P], bank(banks + 2 * (m % 2), k * P, (k + 1) * P), ACT.Identity,
                                bias=shift_col(l, q % 2, k, m), scale=gain_col(l, q % 2, k, m))
                    ins.then_inc(norm_act, 1)

                std(q1, 0)
                for m in range(T):
                    if m + 1 < T:
                        std(q1, m + 1)
                    modulate(q1, m, 0)

                for g in range(0, NG_IN * T, 2):
                    n, m = divmod(g, T)
                    act.wait_ge(u_full, NG_IN * T * l + g + 1)
                    A(u[:, m, n * NW:n * NW + WIN_N[n]], bank(4 + g % 4, 0, WIN_N[n]), ACT.Copy).then_inc(u_act, 1)

                act.wait_ge(c_var, l + 1)
                A(r10, v10, ACT.Sqrt).then_inc(c_sd, 1)
                for m in range(T + 1):
                    act.wait_ge(ct_tr, 6 * l + m + 1)
                    b = m % 4
                    at = (m + 1) * P if m < T else 0
                    if m < T:
                        A(cqT[:, :, m * P:(m + 1) * P], bank(b, 0, 2 * P).rearrange("p (k n) -> p k n", k=2), ACT.Copy)
                    A(ckvT[:, at:at + P], bank(b, 2 * P, 3 * P), ACT.Copy)
                    for z in range(2):
                        ins = A(kT[NOPE:DM_, z, at:at + P], bank(b, 3 * P, 4 * P)[NOPE:DM_, :], ACT.Copy)
                    ins.then_inc(ct_ev, 1)
                for z in range(3):
                    act.wait_ge(vm_full, 3 * l + z + 1)
                    A(vmla[:, 2 * z:2 * z + 2, :], bank(z).rearrange("p (k n) -> p k n", k=2), ACT.Copy).then_inc(vm_ev, 1)
                act.wait_ge(lam_z, l + 1)
                A(lam, lam, ACT.Exp).then_inc(lam_e, 1)

                def prep_out(bi, g):
                    br, b = BLOCKS[bi]
                    z = bi % 2
                    act.wait_ge(prep_tr, 4 * len(BLOCKS) * l + 4 * bi + g + 1)
                    a, e = ((0, 512), (512, 640), (0, 512), (512, 768))[g]
                    n = e - a
                    if g < 2:
                        r = DM_ if br == "D" else P
                        ins = A(qT[0:r, z, a:e], bank(7, 0, n)[0:r, :], ACT.Copy)
                    elif br == "C":
                        A(kT[0:64, z, a:e], bank(7, 0, n)[64 * b:64 * b + 64, :], ACT.Copy)
                        ins = A(kT[64:128, z, a:e], bank(7, 0, n)[64 * b:64 * b + 64, :], ACT.Copy)
                    else:
                        r = NOPE if br == "D" else P
                        ins = A(kT[0:r, z, a:e], bank(7, 0, n)[0:r, :], ACT.Copy)
                    ins.then_inc(prep_ev, 1)

                for g in range(4):
                    prep_out(0, g)
                for ui in range(N_UNIT + 2):
                    if ui < N_UNIT:
                        un = UNITS[ui]
                        w = len(un["kb"]) * P
                        for p in un["passes"]:
                            act.wait_ge(s_max, N_PASS * l + p + 1)
                            if p >= 4:
                                act.wait_ge(t_full, N_UNIT * l + UNIT_OF[p - 4] + 1)
                            A(prob[:, p % 4, 0:w], ps[p % 2][:, 0:w], ACT.Exp, bias=negm[:, p % 8:p % 8 + 1],
                              scale=SCALE[un["br"]], accum_out=sm[:, p % 8:p % 8 + 1]).then_inc(p_ready, 1)
                        if un["br"] == "C":
                            p, h = un["passes"][0], un["head"]
                            A(es[:, ui % 4:ui % 4 + 1], sink_b[:, h:h + 1], ACT.Exp, bias=negm[:, p % 8:p % 8 + 1],
                              scale=SCALE["C"]).then_inc(es_ready, 1)
                    if 1 <= ui <= N_UNIT:
                        v = ui - 1
                        w = min(len(UNITS[v]["kb"]), 4) * P
                        act.wait_ge(t_full, N_UNIT * l + v + 1)
                        if v >= 2:
                            act.wait_ge(o_full, N_UNIT * l + v - 1)
                        A(probT[:, v % 2, 0:w], ps[2][:, 0:w], ACT.Copy).then_inc(t_act, 1)
                    for bi, g in PREP_AT.get(ui, []):
                        prep_out(bi, g)

                act.wait_ge(on_var, l + 1)
                A(r20, v20, ACT.Sqrt).then_inc(on_sd, 1)
                for m in range(T):
                    act.wait_ge(ot_tr, 2 * (T * l + m) + 1)
                    A(oT[:, 0:4, m * P:(m + 1) * P], bank(2 * (m % 2)).rearrange("p (k n) -> p k n", k=4), ACT.Copy).then_inc(ot_act, 1)

                for q in range(NG_GATE * T):
                    act.wait_ge(g_full, NG_GATE * T * l + q + 1)
                    if q >= 2:
                        act.wait_ge(g_mul, NG_GATE * T * l + q - 1)
                    A(sig[:, q % 2, :], bank(q % 2), ACT.Sigmoid).then_inc(g_sig, 1)
                for m in range(T):
                    act.wait_ge(mt_tr, 2 * (T * l + m) + 1)
                    A(mergedT[:, 0:4, m * P:(m + 1) * P], bank(4 + 2 * (m % 2)).rearrange("p (k n) -> p k n", k=4), ACT.Copy).then_inc(mt_act, 1)

                std(q2, 0)
                for m in range(T):
                    if m + 1 < T:
                        std(q2, m + 1)
                    modulate(q2, m, 4)

                act.wait_ge(lg_sub, l + 1)
                A(lg[:, :, :], lg[:, :, :], ACT.Exp).then_inc(lg_exp, 1)

                g0 = CH_MOD + l * CH_LAYER + CH_DENSE
                with act.Fori(0, NE // 2) as i:
                    for e in range(2):
                        n_exp = i * 2 + (NE * l + e)
                        for half in range(2):
                            act.wait_ge(ring_used, i * (2 * CH_EXP) + (g0 + e * CH_EXP + 2 * half + 2))
                            act.wait_ge(hid_ready, n_exp * 2 + BUF)
                            A(sil[0:CAP, half, :], bank(half)[0:CAP, :], ACT.Silu).then_inc(silu_ready, 1)
                        act.wait_ge(hid_tr, n_exp * 2 + 1)
                        A(hidT[:, 0:4, :], bank(6, 0, 4 * CAP).rearrange("p (k n) -> p k n", k=4), ACT.Copy).then_inc(hidT_act, 1)

            for m in range(T):
                act.wait_ge(var_ready, T * 2 * L + m + 1)
                A(sd[:, m:m + 1], var[:, m:m + 1], ACT.Sqrt).then_inc(sd_ready, 1)

        @block.vector
        def _(dve):
            V = nc.vector
            steps = [0]

            def then(ins):
                steps[0] += 1
                ins.then_inc(dve_step, 1)
                dve.wait_ge(dve_step, steps[0])

            def backwards(ap):
                dims = [list(d) for d in ap.ap]
                step, n = dims[-1]
                return bass.AP(ap.tensor, ap.offset + step * (n - 1), dims[:-1] + [[-step, n]])

            def rope_tile(X, cos, sin, tmp, heads, q):
                t = tmp.rearrange("p (h a j q) -> p h a j q", h=heads, a=2, j=2)
                for j in range(2):
                    s = sin.rearrange("p (o a j q) -> p o a j q", o=1, a=2, j=2)[:, :, :, j, :].broadcast_to([P, heads, 2, q])
                    then(V.tensor_tensor(t[:, :, :, j, :], X[:, :, :, 1 - j, :], s, ALU.mult))
                flat = X.rearrange("p h a j q -> p h (a j q)")
                cc = cos.rearrange("p (o n) -> p o n", o=1).broadcast_to([P, heads, 4 * q])
                then(V.tensor_tensor(flat, flat, cc, ALU.mult))
                return V.tensor_tensor(flat, flat, tmp.rearrange("p (h n) -> p h n", h=heads), ALU.add)

            then(V.memset(rpad[:, :], 0.0))
            dve.wait_ge(const_in, 16 * N_CONST)
            dve.sem_inc(mod_row, BUF)
            dve.sem_inc(mod_col, BUF)
            dve.sem_inc(hid_ready, BUF)
            dve.sem_inc(y_ready, 1)
            for l in range(L):
                with dve.Fori(0, N_MOD // 4) as i:
                    def row(j):
                        q0 = l * N_MOD + j
                        dve.wait_ge(ring_used, i * 8 + 2 * (q0 + 1))
                        dve.wait_ge(bm_full[j % 2], i * 32 + 16 * (q0 // 2 + 1))
                        dve.wait_ge(mod_tr, i * 4 + (q0 - 1 + BUF))
                        dve.wait_ge(mod_out[j % 2], i * 32 + 16 * (q0 // 2 + 1))
                        V.tensor_tensor(modrow[:, j % 2, :], bank(j % 2)[0:2, :], bm[:, j % 2, :], ALU.add).then_inc(mod_row, 1)

                    def col(j):
                        q0 = l * N_MOD + j
                        dve.wait_ge(mod_tr, i * 4 + (q0 + 1 + BUF))
                        V.tensor_copy(modcol[:, bass.ds(i * 32 + q0 * 8, 8)], bank(2 + j % 2, 0, 8)).then_inc(mod_col, 1)

                    row(0)
                    row(1)
                    col(0)
                    row(2)
                    col(1)
                    row(3)
                    col(2)
                    col(3)
            dve.wait_ge(mod_col, L * N_MOD + BUF)
            for l in range(L):
                for w in range(2):
                    a = (l * 6 + 1 + 3 * w) * KD * 2
                    V.scalar_tensor_tensor(
                        out=amod[:, (l * 2 + w) * KD * 2:(l * 2 + w + 1) * KD * 2].rearrange("p (k g) -> p k g", g=2),
                        in0=modcol[:, a:a + KD * 2].rearrange("p (k g) -> p k g", g=2), scalar=1.0,
                        in1=gn_col[:, l * 2 + w, :].rearrange("p (k o) -> p k o", o=1).broadcast_to([P, KD, 2]),
                        op0=ALU.add, op1=ALU.mult).then_inc(amod_ready, 1)
            dve.wait_ge(amod_ready, 2 * L)

            def stats(q, m, last=False):
                t = T * q + m
                then(V.tensor_tensor_reduce(sq, xt[:, m % 2, :], xt[:, m % 2, :], 1.0, 0.0, ALU.mult, ALU.add, ss[:, m:m + 1]))
                V.tensor_scalar(var[:, m:m + 1], ss[:, m:m + 1], 1.0 / D, EPS, ALU.mult, ALU.add).then_inc(var_ready, 1)
                dve.wait_ge(sd_ready, t + 1)
                then(V.reciprocal(rstd[:, m:m + 1], sd[:, m:m + 1]))
                if m >= 2 and not last:
                    dve.wait_ge(norm_tr, 2 * (t - 1))
                    if q % 2:
                        dve.wait_ge(xn_out[m % 2], x_fill(q // 2, m) - 16)
                if last:
                    if m >= 2:
                        dve.wait_ge(y_done[m % 2], 16 * (m // 2))
                    V.scalar_tensor_tensor(out=xn[:, m % 2, :], in0=xt[:, m % 2, :], scalar=rstd[:, m:m + 1], in1=gfin_b,
                                           op0=ALU.mult, op1=ALU.mult).then_inc(xn_ready, 1)
                else:
                    V.tensor_scalar(xn[:, m % 2, :], xt[:, m % 2, :], rstd[:, m:m + 1], None, ALU.mult).then_inc(xn_ready, 1)

            def modulate(l, q, m, banks):
                t = T * q + m
                dve.wait_ge(norm_tr, 2 * t + 2)
                for k in range(4, 8):
                    ins = V.tensor_scalar(hT[:, k, m * P:(m + 1) * P], bank(banks + 2 * (m % 2) + 1, (k - 4) * P, (k - 3) * P),
                                          gain_col(l, q % 2, k, m), shift_col(l, q % 2, k, m), ALU.mult, ALU.add)
                ins.then_inc(norm_dve, 1)

            for l in range(L):
                q1, q2 = 2 * l, 2 * l + 1
                for m in range(T + 1):
                    if m < T:
                        dve.wait_ge(x_in[m % 2], x_fill(q1, m))
                        stats(q1, m)
                    if m >= 1:
                        modulate(l, q1, m - 1, 0)

                for g in range(1, NG_IN * T, 2):
                    n, m = divmod(g, T)
                    dve.wait_ge(u_full, NG_IN * T * l + g + 1)
                    V.tensor_copy(u[:, m, n * NW:n * NW + WIN_N[n]], bank(4 + g % 4, 0, WIN_N[n])).then_inc(u_dve, 1)

                dve.wait_ge(small_in, 16 * N_SMALL * (l + 1))
                for m in range(T):
                    a, d = u_counts(l, 4 * T + m)
                    dve.wait_ge(u_act, a)
                    dve.wait_ge(u_dve, d)
                    then(V.tensor_tensor_reduce(sqs, u[:, m, DCQ:DCQ + QR], u[:, m, DCQ:DCQ + QR], 1.0, 0.0, ALU.mult, ALU.add, s10[:, 2 * m:2 * m + 1]))
                    then(V.tensor_tensor_reduce(sqs[:, 0:KVR], u[:, m, DCKV:DCKV + KVR], u[:, m, DCKV:DCKV + KVR], 1.0, 0.0, ALU.mult, ALU.add, s10[:, 2 * m + 1:2 * m + 2]))
                then(V.tensor_scalar(v10[:, 0:10:2], s10[:, 0:10:2], 1.0 / QR, EPS, ALU.mult, ALU.add))
                V.tensor_scalar(v10[:, 1:10:2], s10[:, 1:10:2], 1.0 / KVR, EPS, ALU.mult, ALU.add).then_inc(c_var, 1)
                for m in range(TS):
                    X = u[:, m, DKPE:DKPE + 32].rearrange("p (h a j q) -> p h a j q", h=1, a=2, j=2)
                    rope_tile(X, rope[:, m, 0:32], rope[:, m, 32:64], rtmp2[:, 0:32], 1, 8).then_inc(kpe_ready, 1)
                    dve.wait_ge(kpe_ready, TS * l + m + 1)
                dve.wait_ge(c_sd, l + 1)
                then(V.reciprocal(r10, r10))
                for m in range(T):
                    V.scalar_tensor_tensor(out=u[:, m, DCQ:DCQ + QR], in0=u[:, m, DCQ:DCQ + QR], scalar=r10[:, 2 * m:2 * m + 1],
                                           in1=qn_b[:, :], op0=ALU.mult, op1=ALU.mult)
                    V.scalar_tensor_tensor(out=u[:, m, DCKV:DCKV + KVR], in0=u[:, m, DCKV:DCKV + KVR], scalar=r10[:, 2 * m + 1:2 * m + 2],
                                           in1=kvn_b[:, :], op0=ALU.mult, op1=ALU.mult).then_inc(cn_ready, 1)

                then(V.tensor_tensor_reduce(rtmp2[:, 0:32], lam_b[:, 0:32], lam_b[:, 32:64], 1.0, 0.0, ALU.mult, ALU.add, lam[:, 0:1]))
                V.tensor_tensor_reduce(rtmp2[:, 32:64], lam_b[:, 64:96], lam_b[:, 96:128], 1.0, 0.0, ALU.mult, ALU.add, lam[:, 1:2]).then_inc(lam_z, 1)
                then(V.tensor_scalar(sub_b[:, :], sub_b[:, :], 1.0 - LAM_INIT[l], None, ALU.mult))
                then(V.tensor_scalar(sink_b[:, :], sink_b[:, :], 1.0 / SCALE["C"], None, ALU.mult))
                if l:
                    dve.wait_ge(pad_out, 16 * l)
                V.tensor_scalar(rpad[:, 48:79], backwards(rraw[:, :]), 1.0 / SCALE["B"], None, ALU.mult).then_inc(pad_ready, 1)

                for m in range(T):
                    dve.wait_ge(qm_full, T * l + m + 1)
                    if m == T - 1:
                        dve.wait_ge(kv_out, 16 * N_KV * (l + 1))
                    src = bank(4 + m % 4, 0, HEADS * DM_)
                    dst = u[:, m, DCQ:DCQ + HEADS * DM_]
                    if m == T - 1:
                        V.tensor_copy(dst, src).then_inc(qm_ready, 1)
                        continue
                    then(V.tensor_copy(dst, src))
                    X = dst.rearrange("p (h n) -> p h n", h=HEADS)[:, :, NOPE:DM_].rearrange("p h (a j q) -> p h a j q", a=2, j=2)
                    rope_tile(X, rope[:, m, 0:32], rope[:, m, 32:64], rtmp2[:, 0:128], HEADS, 8).then_inc(qm_ready, 1)
                    dve.wait_ge(qm_ready, T * l + m + 1)
                dve.wait_ge(lam_e, l + 1)
                then(V.tensor_tensor(neglam, lam[:, 1:2], lam[:, 0:1], ALU.subtract))
                then(V.tensor_scalar(neglam, neglam, LAM_INIT[l], None, ALU.subtract))

                for ui in range(N_UNIT + 2):
                    if ui < N_UNIT:
                        un = UNITS[ui]
                        br, m, w = un["br"], un["m"], len(un["kb"]) * P
                        if br == "B" and ui == FIRST_UNIT[un["bi"]]:
                            dve.wait_ge(natab_in, 64 * (2 * l + un["b"] + 1))
                            for h in range(2):
                                tab = na_tab[:, h, :].rearrange("p (j n) -> p j n", n=GRID_W)
                                msk = mask_na[:, :].rearrange("p (o n) -> p o n", o=1).broadcast_to([P, 14, GRID_W])
                                then(V.tensor_tensor(tab, tab, msk, ALU.add))
                        for p in un["passes"]:
                            dve.wait_ge(s_full, N_PASS * l + p + 1)
                            S = ps[p % 2]
                            if br == "B" and m < TS:
                                j0 = (6 - 2 * m) * GRID_W
                                loc = S[:, P:5 * P].rearrange("p (r n) -> p r n", n=GRID_W)
                                then(V.tensor_tensor(loc, loc, backwards(na_tab[:, un["hh"], j0:j0 + 4 * P].rearrange("p (r n) -> p r n", n=GRID_W)), ALU.add))
                            if br == "C" and m < TS:
                                if m > 0:
                                    then(V.tensor_tensor(S[:, P:2 * P], S[:, P:2 * P], mask_sw[:, 0, :], ALU.add))
                                if m < TS - 1:
                                    then(V.tensor_tensor(S[:, w - P:w], S[:, w - P:w], mask_sw[:, 1, :], ALU.add))
                            c8 = p % 8
                            then(V.tensor_reduce(mx[:, c8:c8 + 1], S[:, 0:w], AX.X, ALU.max))
                            if br == "C":
                                h = un["head"]
                                V.tensor_scalar(negm[:, c8:c8 + 1], mx[:, c8:c8 + 1], sink_b[:, h:h + 1], -SCALE[br], ALU.max, ALU.mult).then_inc(s_max, 1)
                            else:
                                V.tensor_scalar(negm[:, c8:c8 + 1], mx[:, c8:c8 + 1], -SCALE[br], None, ALU.mult).then_inc(s_max, 1)
                    if 1 <= ui <= N_UNIT:
                        v = ui - 1
                        un = UNITS[v]
                        w = len(un["kb"]) * P
                        if un["br"] == "A":
                            p1, p2 = un["passes"]
                            r = v % 8
                            dve.wait_ge(p_ready, N_PASS * l + p2 + 1)
                            then(V.reciprocal(cmap[:, v % 4:v % 4 + 1], sm[:, p2 % 8:p2 % 8 + 1]))
                            then(V.scalar_tensor_tensor(out=cmap[:, v % 4:v % 4 + 1], in0=cmap[:, v % 4:v % 4 + 1], scalar=neglam,
                                                        in1=sm[:, p1 % 8:p1 % 8 + 1], op0=ALU.mult, op1=ALU.mult))
                            V.scalar_tensor_tensor(out=prob[:, p1 % 4, 0:w], in0=prob[:, p2 % 4, 0:w], scalar=cmap[:, v % 4:v % 4 + 1],
                                                   in1=prob[:, p1 % 4, 0:w], op0=ALU.mult, op1=ALU.add).then_inc(w_ready, 1)
                        if len(un["kb"]) > 4:
                            dve.wait_ge(t_full, N_UNIT * l + v + 1)
                            if v >= 2:
                                dve.wait_ge(o_full, N_UNIT * l + v - 1)
                            V.tensor_copy(probT[:, v % 2, 4 * P:5 * P], ps[2][:, 4 * P:5 * P]).then_inc(t_dve, 1)
                    if ui >= 2:
                        v = ui - 2
                        un = UNITS[v]
                        p, r = un["passes"][0] % 8, v % 8
                        dve.wait_ge(p_ready, N_PASS * l + un["passes"][-1] + 1)
                        if un["br"] == "C":
                            dve.wait_ge(es_ready, N_C * l + C_BEFORE[v] + 1)
                            then(V.tensor_tensor(sm[:, p:p + 1], sm[:, p:p + 1], es[:, v % 4:v % 4 + 1], ALU.add))
                        then(V.reciprocal(rinv[:, r:r + 1], sm[:, p:p + 1]))
                        dve.wait_ge(o_full, N_UNIT * l + v + 1)
                        col = O_COL[un["br"]] + HD * un["head"]
                        V.tensor_scalar(u[:, un["m"], col:col + HD], bank(6, 0, HD), rinv[:, r:r + 1], None, ALU.mult).then_inc(o_ev, 1)

                dve.wait_ge(o_ev, N_UNIT * (l + 1))
                for m in range(T):
                    then(V.tensor_tensor(sqs, u[:, m, AQ:AQ + 256], u[:, m, AQ:AQ + 256], ALU.mult))
                    then(V.tensor_reduce(s20[:, 4 * m:4 * m + 4], sqs.rearrange("p (h n) -> p h n", h=HEADS), AX.X, ALU.add))
                V.tensor_scalar(v20, s20, 1.0 / HD, EPS, ALU.mult, ALU.add).then_inc(on_var, 1)
                dve.wait_ge(on_sd, l + 1)
                then(V.reciprocal(r20, r20))
                for m in range(T):
                    o = u[:, m, AQ:AQ + 256].rearrange("p (h n) -> p h n", h=HEADS)
                    rs = r20[:, 4 * m:4 * m + 4].rearrange("p (h o) -> p h o", o=1).broadcast_to([P, HEADS, HD])
                    gs = sub_b[:, :].rearrange("p (o n) -> p o n", o=1).broadcast_to([P, HEADS, HD])
                    then(V.tensor_tensor(o, o, rs, ALU.mult))
                    V.tensor_tensor(o, o, gs, ALU.mult).then_inc(on_ready, 1)
                for m in range(T):
                    dve.wait_ge(ot_tr, 2 * (T * l + m) + 2)
                    V.tensor_copy(oT[:, 4:8, m * P:(m + 1) * P], bank(2 * (m % 2) + 1).rearrange("p (k n) -> p k n", k=4)).then_inc(ot_dve, 1)

                for q in range(NG_GATE * T):
                    j, m = divmod(q, T)
                    half, br = divmod(j, 4)
                    dve.wait_ge(g_sig, NG_GATE * T * l + q + 1)
                    if br == 0:
                        if j == 0 and m == 0:
                            dve.wait_ge(ot_tr, 2 * T * (l + 1))
                        dst = merged[:, m, half * NW:(half + 1) * NW]
                    else:
                        dst = gtmp[:, q % 2, :]
                        if ADDS[q - 1]:
                            dve.wait_ge(g_add, 6 * T * l + ADDS[q - 1])
                    V.tensor_tensor(dst, sig[:, q % 2, :], bank(2 + q % 2), ALU.mult).then_inc(g_mul, 1)
                for m in range(T):
                    dve.wait_ge(mt_tr, 2 * (T * l + m) + 2)
                    V.tensor_copy(mergedT[:, 4:8, m * P:(m + 1) * P], bank(4 + 2 * (m % 2) + 1).rearrange("p (k n) -> p k n", k=4)).then_inc(mt_dve, 1)

                dve.wait_ge(gate1_in, 32 * (l + 1))
                for m in range(T + 1):
                    if m < T:
                        dve.wait_ge(wo_full, T * l + m + 1)
                        dve.wait_ge(x_in[m % 2], x_fill(q2, m))
                        then(V.tensor_tensor(sq, ps[m % 2][:, :], gate1_b[:, 1 if m < TS else 0, :], ALU.mult))
                        V.tensor_tensor(xt[:, m % 2, :], xt[:, m % 2, :], sq, ALU.add).then_inc(x_new, 1)
                        dve.wait_ge(x_new, T * l + m + 1)
                        stats(q2, m)
                    if m >= 1:
                        modulate(l, q2, m - 1, 4)

                dve.wait_ge(lg_full, l + 1)
                z = bank(0, 0, T * NE).rearrange("p (m e) -> p m e", m=T)
                col = lambda i: lgs[:, i, :].rearrange("p (m o) -> p m o", o=1).broadcast_to([P, T, NE])
                then(V.tensor_reduce(lgs[:, 0, :], z, AX.X, ALU.max))
                V.tensor_tensor(lg[:, :, :], z, col(0), ALU.subtract).then_inc(lg_sub, 1)
                dve.wait_ge(lg_exp, l + 1)
                then(V.tensor_reduce(lgs[:, 1, :], lg[:, :, :], AX.X, ALU.add))
                then(V.reciprocal(lgs[:, 1, :], lgs[:, 1, :]))
                V.tensor_tensor(lg[:, :, :], lg[:, :, :], col(1), ALU.mult).then_inc(aff_ready, 1)
                dve.wait_ge(affT_tr, l + 1)
                then(V.tensor_copy(affT[:, 0:NS], bank(1)[0:NE, :]))
                then(V.tensor_copy(affT[:, NS:NS + NP], bank(2, 0, NP)[0:NE, :]))
                for a, n, r0, rounds in ((0, NS, 0, CAP_S // 8), (NS, NP, CAP_S, CAP_P // 8)):
                    for r in range(rounds):
                        v8 = slice(r0 + 8 * r, r0 + 8 * r + 8)
                        src = affT[:, a:a + n]
                        then(V.max(top_v[:, v8], src))
                        then(V.max_index(top_i[:, v8], top_v[:, v8], src))
                        if r < rounds - 1:
                            then(V.match_replace(src, top_v[:, v8], src, -1.0))
                then(V.tensor_copy(top_f[:, 0:CAP_S], top_i[:, 0:CAP_S]))
                V.tensor_scalar(top_f[:, CAP_S:CAP], top_i[:, CAP_S:CAP], float(NS), None, ALU.add).then_inc(top_ready, 1)
                dve.wait_ge(topT_tr, l + 1)
                then(V.tensor_copy(gateT[:, 0:NE], bank(3, 0, NE)[0:CAP, :]))
                then(V.tensor_copy(gateT[:, NE:NE + 1], bank(3, 0, 1)[0:CAP, :]))
                then(V.tensor_copy(idxT[:, 0:NE], bank(3, NE, 2 * NE)[0:CAP, :]))
                V.tensor_copy(idxT[:, NE:NE + 1], bank(3, NE, NE + 1)[0:CAP, :]).then_inc(topT_ready, 1)
                dve.wait_ge(topT_ready, l + 1)
                then(V.tensor_copy(gate_c[:, 0:1], gateT[:, 0:1]))
                V.tensor_copy(idx_c[:, 0, 0:1], idxT[:, 0:1]).then_inc(idx_ready, 1)

                def exp_then(ins, count):
                    ins.then_inc(exp_step, 1)
                    dve.wait_ge(exp_step, count)

                def rows_in(b, turned, base):
                    for half in range(2):
                        dve.wait_ge(xe_tr, turned + (half + 1))
                        ks = slice(4 * half, 4 * half + 4)
                        views = []
                        for g, c0, c1 in ((1, 0, CAP_S), (0, CAP_S, CAP)):
                            def wide(t, o):
                                return t[:, o:o + 2 * KD].rearrange("p (k g) -> p k g", g=2)[:, ks, g:g + 1].broadcast_to([P, 4, c1 - c0])
                            views.append((bank(6 + half, 0, 4 * CAP).rearrange("p (k n) -> p k n", k=4)[:, :, c0:c1],
                                          xeT[:, b, ks, c0:c1], wide(amod, (l * 2 + 1) * KD * 2), wide(modcol, (l * 6 + 3) * KD * 2)))
                        (s0, d0, a0, h0), (s1, d1, a1, h1) = views
                        V.tensor_tensor(d0, s0, a0, ALU.mult)
                        exp_then(V.tensor_tensor(d1, s1, a1, ALU.mult), base + (half + 1))
                        V.tensor_tensor(d0, d0, h0, ALU.add)
                        V.tensor_tensor(d1, d1, h1, ALU.add).then_inc(xe_ready, 1)

                rows_in(0, 2 * (NE + 1) * l, 2 * (NE + 1) * l)
                g0 = CH_MOD + l * CH_LAYER + CH_DENSE
                with dve.Fori(0, NE // 2) as i:
                    for e in range(2):
                        n_exp = i * 2 + (NE * l + e)
                        n_prep = i * 2 + ((NE + 1) * l + e)
                        c_exp = g0 + e * CH_EXP
                        dve.wait_ge(added, n_exp + BUF)
                        if e == 0:
                            V.tensor_copy(gate_c[:, 1:2], gateT[:, bass.ds(i * 2 + 1, 1)])
                        else:
                            V.tensor_copy(gate_c[:, 0:1], gateT[:, bass.ds(i * 2 + 2, 1)])
                        V.tensor_copy(idx_c[:, 1 - e, 0:1], idxT[:, bass.ds(i * 2 + (e + 1), 1)]).then_inc(idx_ready, 1)
                        rows_in(1 - e, n_prep * 2 + 2, n_prep * 2 + 2)
                        for half in range(2):
                            dve.wait_ge(silu_ready, n_exp * 2 + (half + 1))
                            dve.wait_ge(ring_used, i * (2 * CH_EXP) + (c_exp + 4 + 2 * half + 2))
                            V.tensor_tensor(hid[0:CAP, half * NW:(half + 1) * NW], sil[0:CAP, half, :], bank(2 + half)[0:CAP, :], ALU.mult).then_inc(hid_ready, 1)
                        dve.wait_ge(hid_tr, n_exp * 2 + 2)
                        V.tensor_copy(hidT[:, 4:8, :], bank(7, 0, 4 * CAP).rearrange("p (k n) -> p k n", k=4)).then_inc(hidT_dve, 1)
                        for half in range(2):
                            dve.wait_ge(ring_used, i * (2 * CH_EXP) + (c_exp + 8 + 2 * half + 2))
                            ins = V.scalar_tensor_tensor(out=ybuf[0:CAP, e, half * NW:(half + 1) * NW], in0=bank(4 + half)[0:CAP, :],
                                                         scalar=gate_c[:, e:e + 1], in1=gate2_b[0:CAP, half * NW:(half + 1) * NW],
                                                         op0=ALU.mult, op1=ALU.mult)
                        ins.then_inc(y_ready, 1)

            dve.wait_ge(gfin_in, 16)
            for m in range(T):
                dve.wait_ge(x_in[m % 2], x_fill(2 * L, m))
                stats(2 * L, m, last=True)

        @block.gpsimd
        def _(pool):
            G = nc.gpsimd
            steps = [0]

            def then(ins):
                steps[0] += 1
                ins.then_inc(pool_step, 1)
                pool.wait_ge(pool_step, steps[0])

            def rope_tile(X, cos, sin, tmp, heads, q):
                t = tmp.rearrange("p (h a j q) -> p h a j q", h=heads, a=2, j=2)
                for j in range(2):
                    s = sin.rearrange("p (o a j q) -> p o a j q", o=1, a=2, j=2)[:, :, :, j, :].broadcast_to([P, heads, 2, q])
                    then(G.tensor_tensor(t[:, :, :, j, :], X[:, :, :, 1 - j, :], s, ALU.mult))
                flat = X.rearrange("p h a j q -> p h (a j q)")
                cc = cos.rearrange("p (o n) -> p o n", o=1).broadcast_to([P, heads, 4 * q])
                then(G.tensor_tensor(flat, flat, cc, ALU.mult))
                return G.tensor_tensor(flat, flat, tmp.rearrange("p (h n) -> p h n", h=heads), ALU.add)

            pool.sem_inc(added, BUF)
            for b in range(2):
                pool.wait_ge(mod_out[b], 16 * (L * N_MOD // 2 + 1))
            pool.wait_ge(const_in, 16 * N_CONST)

            for l in range(L):
                q1, q2 = 2 * l, 2 * l + 1
                if l:
                    pool.wait_ge(y_out, 16 * NE * l)
                    pool.wait_ge(xe_tr, 2 * (NE + 1) * l)
                for m in range(T):
                    if m >= 2:
                        pool.wait_ge(xn_ready, T * q1 + m - 1)
                    pool.dma_start(xt[:, m % 2, :], tok_in(l, m)).then_inc(x_in[m % 2], 16)

                for m in range(TS):
                    a, d = u_counts(l, 4 * T + m)
                    pool.wait_ge(u_act, a)
                    pool.wait_ge(u_dve, d)
                    for c0, heads, d4, t0 in ((AQ, 16, 8, 0), (CQ, 6, 16, 64)):
                        w = heads * 4 * d4
                        X = u[:, m, c0:c0 + w].rearrange("p (h a j q) -> p h a j q", h=heads, a=2, j=2)
                        ins = rope_tile(X, rope[:, m, t0:t0 + 4 * d4], rope[:, m, t0 + 4 * d4:t0 + 8 * d4], rtmp[:, 0:w], heads, d4)
                        if heads == 16:
                            then(ins)
                    ins.then_inc(rope_a, 1)
                    pool.wait_ge(rope_a, TS * l + m + 1)

                pool.wait_ge(u_act, 13 * (l + 1))
                pool.wait_ge(u_dve, 12 * (l + 1))
                pool.wait_ge(cn_ready, T * (l + 1))
                for dst, c0, h, n in ((new_diff_k, AK, HEADS, 64), (new_diff_v, AV, HEADS, 64), (new_na_k, BK, HEADS, 64),
                                      (new_na_v, BV, HEADS, 64), (new_swa_k, CK, 2, 64), (new_swa_v, CV, 2, 64)):
                    pool.dma_start(dst[0, l].rearrange("t h n -> t (h n)"), u[:, T - 1, c0:c0 + h * n]).then_inc(kv_out, 16)
                pool.dma_start(new_mla_ckv[0, l], u[:, T - 1, DCKV:DCKV + KVR]).then_inc(kv_out, 16)
                pool.dma_start(new_mla_kpe[0, l], u[:, T - 1, DKPE:DKPE + ROPE_D]).then_inc(kv_out, 16)

                pool.wait_ge(pad_ready, l + 1)
                pool.dma_start(rpb_dram[l], rpad[:, :]).then_inc(pad_out, 16)
                pool.wait_ge(pad_out, 16 * (l + 1))
                for b in range(2):
                    if b:
                        last = UNITS[LAST_UNIT[BLOCKS.index(("B", 0))]]["passes"][-1]
                        pool.wait_ge(s_max, N_PASS * l + last + 1)
                    for h in range(2):
                        for r in range(2):
                            off = ((l * HEADS + 2 * b + h) * 15 + 1 - r) * 127
                            src = bass.AP(rpb_dram.tensor, off, [[1, GRID_W], [127, 14], [1, GRID_W]])
                            pool.dma_start(na_tab[64 * r:64 * r + 64, h, :].rearrange("p (j n) -> p j n", n=GRID_W), src).then_inc(natab_in, 16)

                pool.wait_ge(on_ready, T * (l + 1))
                for g in range(2):
                    pool.dma_start(gate1_b[:, g, :], mod_dram[l, g:g + 1, 2 * D:3 * D].broadcast_to([P, D])).then_inc(gate1_in, 16)
                pool.dma_start(gate2_b[0:CAP_S, :], mod_dram[l, 1:2, 5 * D:6 * D].broadcast_to([CAP_S, D])).then_inc(gate2_in, 16)
                pool.dma_start(gate2_b[CAP_S:CAP, :], mod_dram[l, 0:1, 5 * D:6 * D].broadcast_to([CAP_P, D])).then_inc(gate2_in, 16)

                n = 0
                for q in range(NG_GATE * T):
                    j, m = divmod(q, T)
                    if j % 4 == 0:
                        continue
                    pool.wait_ge(g_mul, NG_GATE * T * l + q + 1)
                    if n >= T:
                        pool.wait_ge(g_add, 6 * T * l + n - T + 1)
                    dst = merged[:, m, (j // 4) * NW:(j // 4 + 1) * NW]
                    G.tensor_tensor(dst, dst, gtmp[:, q % 2, :], ALU.add).then_inc(g_add, 1)
                    n += 1

                pool.wait_ge(mt_tr, 2 * T * (l + 1))
                for m in range(2):
                    pool.dma_start(xt[:, m % 2, :], tok_in(l, m)).then_inc(x_in[m % 2], 16)
                for m in range(T):
                    pool.wait_ge(x_new, T * l + m + 1)
                    pool.dma_start(x_dram[m * P:(m + 1) * P, :], xt[:, m % 2, :]).then_inc(x_out[m % 2], 16)
                    pool.wait_ge(xn_ready, T * q2 + m + 1)
                    pool.dma_start(xn_dram[m * P:(m + 1) * P, :], xn[:, m % 2, :]).then_inc(xn_out[m % 2], 16)
                    if m + 2 < T:
                        pool.wait_ge(x_out[m % 2], x_fill(l, m))
                        pool.dma_start(xt[:, m % 2, :], tok_in(l, m + 2)).then_inc(x_in[m % 2], 16)

                for b in range(2):
                    pool.wait_ge(x_out[b], x_fill(l, 4 - b))
                    pool.wait_ge(xn_out[b], x_fill(l, 4 - b))

                def gather(b, ready):
                    pool.wait_ge(idx_ready, ready)
                    pool.sem_inc(pool_held, 1)
                    pool.indirect_dma_start(out=xe[0:CAP, b, :], out_offset=None, in_=xn_dram,
                                            in_offset=bass.IndirectOffsetOnAxis(ap=idx_c[:, b, 0:1], axis=0)).then_inc(xe_in[b], 16)

                gather(0, (NE + 1) * l + 1)
                pool.wait_ge(gate2_in, 32 * (l + 1))
                with pool.Fori(0, NE // 2) as i:
                    for e in range(2):
                        n_exp = i * 2 + (NE * l + e)
                        gather(1 - e, i * 2 + ((NE + 1) * l + e + 2))
                        pool.wait_ge(y_ready, n_exp + 2)
                        pool.sem_inc(pool_held, 1)
                        pool.indirect_dma_start(out=x_dram, out_offset=bass.IndirectOffsetOnAxis(ap=idx_c[:, e, 0:1], axis=0),
                                                in_=ybuf[0:CAP, e, :], in_offset=None, compute_op=ALU.add).then_inc(y_out, 16)
                        pool.wait_ge(y_out, n_exp * 16 + 16)
                        pool.sem_inc(added, 1)

            pool.dma_start(gfin_b, g_final.rearrange("(a n) -> a n", a=1).broadcast_to([P, D])).then_inc(gfin_in, 16)
            pool.wait_ge(y_out, 16 * NE * L)
            pool.wait_ge(xe_tr, 2 * (NE + 1) * L)
            q = 2 * L
            for m in range(T + 1):
                if m < T:
                    if m >= 2:
                        pool.wait_ge(xn_ready, T * q + m - 1)
                    pool.dma_start(xt[:, m % 2, :], tok_in(L, m)).then_inc(x_in[m % 2], 16)
                if m >= 1:
                    v = m - 1
                    pool.wait_ge(xn_ready, T * q + v + 1)
                    dst = y_sample[0, v * P:(v + 1) * P, :] if v < TS else y_prompt[0]
                    pool.dma_start(dst, xn[:, v % 2, :]).then_inc(y_done[v % 2], 16)
            pool.wait_ge(kv_out, 16 * N_KV * L)
            for b in range(2):
                pool.wait_ge(y_done[b], 16 * (3 - b))


_INS = ["x_prompt", "x_sample", "cache_diff_k", "cache_diff_v", "cache_na_k", "cache_na_v", "cache_swa_k",
        "cache_swa_v", "cache_mla_ckv", "cache_mla_kpe", "c", "c_ctx", "w_mod", "b_mod", "g_norm1", "g_norm2", "w_in",
        "da_lambda", "da_subln", "na_rpb", "sw_sink", "mla_q_norm", "mla_w_uq", "mla_kv_norm", "mla_w_ukv", "w_gate",
        "w_branch", "w_out", "w_router", "w_e_gate", "w_e_up", "w_e_down", "g_final"]
_OUTS = [(1, NP, D), (1, NS, D), (1, L, NP, 4, 64), (1, L, NP, 4, 64), (1, L, NP, 4, 64), (1, L, NP, 4, 64),
         (1, L, NP, 2, 64), (1, L, NP, 2, 64), (1, L, NP, KVR), (1, L, NP, ROPE_D)]


def position_tables():
    t = np.arange(NS)
    parts = []
    for d4 in (8, 16):
        f = np.float32(10000.0) ** (-np.arange(d4, dtype=np.float32) / np.float32(d4))
        cos, sin = [], []
        for pos in (t // GRID_W, t % GRID_W):
            ang = pos.astype(np.float32)[:, None] * f.astype(np.float32)
            cc, s = np.cos(ang), np.sin(ang)
            cos += [cc, cc]
            sin += [-s, s]
        parts += cos + sin
    rope = np.concatenate(parts, axis=1).astype(np.float32)
    qc, kc = np.arange(GRID_W)[:, None], np.arange(GRID_W)[None, :]
    start = np.clip(qc - 8, 0, GRID_W - 16)
    na = np.where((kc >= start) & (kc < start + 16), 0.0, NEG).astype(np.float32)
    q, k = np.arange(P)[:, None], np.arange(P)[None, :]
    sw = np.stack([np.where(k >= q, 0.0, NEG), np.where(k <= q, 0.0, NEG)], axis=1).astype(np.float32)
    return np.eye(P, dtype=np.float32), rope, np.ascontiguousarray(np.concatenate([na, na], axis=0)[:, ::-1]), sw


def kernel(**inputs):
    import concourse.bacc as _bacc
    from concourse.bass_utils import run_bass_kernel_spmd as _run

    nc = _bacc.Bacc("TRN2", target_bir_lowering=False, num_devices=1)
    arrays, args = {}, []
    given = [(n, np.ascontiguousarray(inputs[n])) for n in _INS]
    given += list(zip(["k_ident", "k_rope", "k_mask_na", "k_mask_sw"], position_tables()))
    for name, a in given:
        arrays[f"in_{name}"] = a
        args.append(nc.dram_tensor(f"in_{name}", a.shape, mybir.dt.from_np(a.dtype), kind="ExternalInput").ap())
    for i, shape in enumerate(_OUTS):
        args.append(nc.dram_tensor(f"out_{i}", shape, F32, kind="ExternalOutput").ap())
    hybrid_step(nc, *args)
    r = _run(nc, [arrays], core_ids=[0])
    return tuple(r.results[0][f"out_{i}"] for i in range(len(_OUTS)))
```

```python
import math
from contextlib import ExitStack

import numpy as np
import concourse.bass as bass
from concourse import mybir

F32 = mybir.dt.float32
F32R = mybir.dt.float32r
U32 = mybir.dt.uint32
ALU = mybir.AluOpType
ACT = mybir.ActivationFunctionType
AX = mybir.AxisListType

D, L, P = 1024, 2, 128
NS, NP = 512, 128
T = (NS + NP) // P
TS = NS // P
KD = D // P
GRID_W, HEADS, HD, DQK = 64, 4, 64, 32
NOPE, ROPE_D = 64, 32
DM_ = NOPE + ROPE_D
QR, KVR = 256, 128
NE, DE, CAP_S, CAP_P = 16, 1024, 64, 16
CAP = CAP_S + CAP_P
EPS = 1e-6
IN_DIM = 2464
AQ, AK, AV, BQ, BK, BV, CQ, CK, CV, DCQ, DCKV, DKPE = (
    0, 256, 512, 768, 1024, 1280, 1536, 1792, 1920, 2048, 2304, 2432)
DRQ = DKPE - NOPE
NEG = -1e30
LAM_INIT = [0.8 - 0.6 * math.exp(-0.3 * l) for l in range(L)]
NW = 512
KC = 2
NQ = KD // KC
RING = 8
HIGH = 4
WIN_N = [512, 512, 512, 512, IN_DIM - 2048]
N_MOD = 6 * D // NW
NG_IN, NG_GATE = 5, 8
CH_MOD = NQ * N_MOD * L
CH_IN, CH_GATE = NQ * NG_IN, (NQ + 1) * NG_GATE
CH_DENSE = CH_IN + CH_GATE + 2 * NQ
CH_EXP = 6 * NQ
CH_LAYER = CH_DENSE + NE * CH_EXP
N_CHUNKS = CH_MOD + L * CH_LAYER
SIG = 6

O_COL = {"A": AQ, "B": BQ, "C": CQ, "D": DCQ}
O_BLOCKS = [AQ, AQ + 128, BQ, BQ + 128, CQ, CQ + 128, DCQ, DCQ + 128]
BLOCKS = [("D", 0), ("D", 1), ("D", 2), ("D", 3), ("A", 0), ("B", 0), ("A", 1), ("B", 1), ("C", 0), ("C", 1)]


def plan_units():
    units, passes = [], 0
    for bi, (br, b) in enumerate(BLOCKS):
        for hh in range(1 if br == "D" else 2):
            for m in range(T):
                head = b if br == "D" else 2 * b + hh
                if m == T - 1:
                    kb = [5]
                elif br == "C":
                    kb = [0] + [1 + j for j in range(max(m - 1, 0), min(m + 2, TS))]
                else:
                    kb = [0, 1, 2, 3, 4]
                n = 2 if br == "A" else 1
                if br == "D":
                    rows = [(0, DM_)]
                elif br == "A":
                    rows = [(64 * hh, 32), (64 * hh + 32, 32)]
                else:
                    rows = [(64 * hh, 64)]
                units.append(dict(bi=bi, br=br, b=b, hh=hh, m=m, head=head, kb=kb, rows=rows,
                                  passes=list(range(passes, passes + n))))
                passes += n
    return units, passes


UNITS, N_PASS = plan_units()
N_UNIT = len(UNITS)
UNIT_OF = {p: i for i, u in enumerate(UNITS) for p in u["passes"]}
FIRST_UNIT = {bi: min(i for i, u in enumerate(UNITS) if u["bi"] == bi) for bi in range(len(BLOCKS))}
LAST_UNIT = {bi: max(i for i, u in enumerate(UNITS) if u["bi"] == bi) for bi in range(len(BLOCKS))}
SCALE = {"A": DQK ** -0.5, "B": HD ** -0.5, "C": HD ** -0.5, "D": DM_ ** -0.5}
PREP_AT = {}
for _bi in range(1, len(BLOCKS)):
    for _g in range(4):
        PREP_AT.setdefault(FIRST_UNIT[_bi - 1] + 1 + _g, []).append((_bi, _g))
A_UNITS = [i for i, u in enumerate(UNITS) if u["br"] == "A"]
B_UNITS = [i for i, u in enumerate(UNITS) if u["br"] == "B"]
N_C = sum(1 for u in UNITS if u["br"] == "C")
C_BEFORE = [sum(1 for u in UNITS[:i] if u["br"] == "C") for i in range(N_UNIT + 1)]
ADDS = [sum(1 for r in range(q) if r // T % 4) for q in range(8 * T + 1)]
A_BEFORE = [sum(1 for a in A_UNITS if a < i) for i in range(N_UNIT + 1)]
TAIL_BEFORE = [sum(1 for u in UNITS[:i] if len(u["kb"]) > 4) for i in range(N_UNIT + 1)]


def segments(u):
    out, col = [], 0
    runs = [(0, 1)] if u["kb"][0] == 0 else []
    rest = [k for k in u["kb"] if k]
    runs.append((rest[0], len(rest)))
    for k0, n in runs:
        a, w = k0 * P, n * P
        while w:
            s = min(w, NW - col % NW)
            out.append((col, a, s))
            col, a, w = col + s, a + s, w - s
    return out


def chunk_no(l, c):
    return CH_MOD + l * CH_LAYER + c


def width_of(g):
    c = (g - CH_MOD) % CH_LAYER
    return WIN_N[-1] if CH_MOD <= g < N_CHUNKS and CH_IN - NQ <= c < CH_IN else NW


def by_pool(g):
    l, c = divmod(g - CH_MOD, CH_LAYER)
    return g >= CH_MOD and g % 4 == 3 and (c >= CH_DENSE or (c < HIGH and l > 0))


LOW_POOL = [sum(map(by_pool, range(g + 1))) for g in range(N_CHUNKS + HIGH)]
LOW_DVE = [g + 1 - LOW_POOL[g] for g in range(N_CHUNKS + HIGH)]


def hybrid_step(nc, x_prompt, x_sample, cache_diff_k, cache_diff_v, cache_na_k, cache_na_v, cache_swa_k,
                cache_swa_v, cache_mla_ckv, cache_mla_kpe, c, c_ctx, w_mod, b_mod, g_norm1, g_norm2, w_in,
                da_lambda, da_subln, na_rpb, sw_sink, mla_q_norm, mla_w_uq, mla_kv_norm, mla_w_ukv, w_gate,
                w_branch, w_out, w_router, w_e_gate, w_e_up, w_e_down, g_final,
                k_ident, k_rope, k_mask_na, k_mask_sw,
                y_prompt, y_sample, new_diff_k, new_diff_v, new_na_k, new_na_v, new_swa_k, new_swa_v,
                new_mla_ckv, new_mla_kpe):
    ctx = ExitStack()
    with ctx:
        def sb(name, shape, dt=F32):
            return ctx.enter_context(nc.sbuf_tensor(name, shape, dt))

        def sem(name):
            return ctx.enter_context(nc.semaphore(name))

        x_dram = nc.dram_tensor("x_resid", (T * P, D), F32, kind="Internal").ap()
        xn_dram = nc.dram_tensor("x_normed", (T * P, D), F32, kind="Internal").ap()
        mod_dram = nc.dram_tensor("mod_rows", (L, 2, 6 * D), F32, kind="Internal").ap()
        rpb_dram = nc.dram_tensor("rpb_padded", (L, HEADS * 15, 127), F32, kind="Internal").ap()

        def over(name, shape, base, first):
            return nc.alloc_sbuf_tensor_at(name, shape, F32R, offset=(base + 31) // 32 * 32 + 4 * first)

        ring_at = nc.sbuf_base
        ring = sb("ring", [P, RING, KC, NW])
        low = over("low", [P, RING, KC, NW], ring_at, 0)
        high = sb("high", [P, HIGH, KC, NW], F32R)
        hT = [sb("hT_high", [P, KD, T * P], F32R), sb("hT_low", [P, KD, T * P], F32R)]
        WORK_N = T * IN_DIM
        work_at = nc.sbuf_base
        work = sb("work", [P, WORK_N])
        ATT_N = 2 * KD * T * P
        att_at = nc.sbuf_base
        att = sb("att", [P, ATT_N])
        u = work[:, :].rearrange("p (m n) -> p m n", m=T)
        merged = work[:, 0:T * D].rearrange("p (m n) -> p m n", m=T)
        mergedT = [over("mergedT_high", [P, KD, T * P], work_at, 5120), over("mergedT_low", [P, KD, T * P], att_at, 0)]
        sig = work[:, 5120:5120 + SIG * NW].rearrange("p (b n) -> p b n", b=SIG)
        gtmp = work[:, 11264:12288].rearrange("p (b n) -> p b n", b=2)
        xt = work[:, 0:T * D].rearrange("p (b n) -> p b n", b=T)
        xn_work = work[:, 5120:7168].rearrange("p (b n) -> p b n", b=2)
        xn_att = att[:, 8192:10240].rearrange("p (b n) -> p b n", b=2)
        sq = work[:, 10240:11264]
        xe = work[:, 0:2048].rearrange("p (b n) -> p b n", b=2)
        xeT = [over("xeT_high", [P, 2, KD, CAP], work_at, 2048), over("xeT_low", [P, 2, KD, CAP], work_at, 3328)]
        hid = work[:, 4608:5632]
        sil = work[:, 5632:6656].rearrange("p (b n) -> p b n", b=2)
        hidT = [over("hidT_high", [P, KD, CAP], work_at, 6656), over("hidT_low", [P, KD, CAP], work_at, 7296)]
        ybuf = work[:, 7936:9984].rearrange("p (b n) -> p b n", b=2)
        affT = work[0:NE, 10240:10240 + T * P]
        qT = att[:, 0:1280].rearrange("p (b n) -> p b n", b=2)
        kT = att[:, 1280:2816].rearrange("p (b n) -> p b n", b=2)
        prob = att[:, 2816:5376].rearrange("p (b n) -> p b n", b=4)
        cqT = att[:, 2816:4096].rearrange("p (b n) -> p b n", b=2)
        probT = att[:, 5376:6656].rearrange("p (b n) -> p b n", b=2)
        sqs = att[:, 5376:5632]
        na_tab = att[:, 6656:8448].rearrange("p (h n) -> p h n", h=2)
        c_ka, c_va, c_kb, c_vb = (att[:, 8448 + 256 * i:8704 + 256 * i] for i in range(4))
        c_kc, c_vc, c_ckv = (att[:, 9472 + 128 * i:9600 + 128 * i] for i in range(3))
        c_kpe = att[:, 9856:9952]
        oT = [over("oT_high", [P, KD, T * P], att_at, 0), over("oT_low", [P, KD, T * P], att_at, 5120)]
        gate1_b = att[:, 5120:7168].rearrange("p (g n) -> p g n", g=2)
        gate2_b = att[:, 7168:8192]
        gfin_b = att[:, 8192:9216]

        ckvT = sb("ckvT", [P, 6 * P])
        vmla = sb("vmla", [P, 6, 256])
        mask_sw = sb("mask_sw", [P, 2, P])
        mask_na = sb("mask_na", [P, GRID_W])
        rope = sb("rope", [P, TS, 192])
        ident = sb("ident", [P, P])
        w_uq = sb("w_uq", [P, 2, HEADS * DM_])
        w_ukv = sb("w_ukv", [P, 512])
        w_r = sb("w_r", [P, KD, NE])
        w_r2 = [sb("w_r_high", [P, KD, NE], F32R), sb("w_r_low", [P, KD, NE], F32R)]
        qn_b = sb("qn_b", [P, QR])
        kvn_b = sb("kvn_b", [P, KVR])
        lam_b = sb("lam_b", [P, 128])
        sub_b = sb("sub_b", [P, HD])
        sink_b = sb("sink_b", [P, HEADS])
        rtmp = sb("rtmp", [P, 512])
        rtmp2 = sb("rtmp2", [P, 128])
        rpad = sb("rpad", [HEADS * 15, 127])
        rraw = sb("rraw", [HEADS * 15, 31])
        modcol = sb("modcol", [P, L * 6 * KD * 2])
        amod = sb("amod", [P, L * 2 * KD * 2])
        gn_col = sb("gn_col", [P, L * 2, KD])
        cT = sb("cT", [P, 2, KD])
        csf = sb("csf", [P, KD, 2])
        csT = [sb("csT_high", [P, KD, 2], F32R), sb("csT_low", [P, KD, 2], F32R)]
        bm = work[0:2, 10240:11264].rearrange("p (b n) -> p b n", b=2)
        modrow = work[0:2, 11264:12288].rearrange("p (b n) -> p b n", b=2)
        st = sb("st", [P, 160])
        ss, var, sd, rstd = st[:, 0:5], st[:, 5:10], st[:, 10:15], st[:, 15:20]
        s10, v10, r10 = st[:, 20:30], st[:, 30:40], st[:, 40:50]
        s20, v20, r20 = st[:, 50:70], st[:, 70:90], st[:, 90:110]
        mx, negm, sm = st[:, 110:118], st[:, 118:126], st[:, 126:134]
        rinv, cmap, es = st[:, 134:142], st[:, 142:146], st[:, 154:158]
        lam, neglam = st[:, 148:150], st[:, 150:151]
        lg = sb("lg", [P, T, NE])
        lgs = sb("lgs", [P, 2, T])
        top_v = sb("top_v", [NE, CAP])
        top_i = sb("top_i", [NE, CAP], U32)
        top_f = sb("top_f", [NE, CAP])
        gateT = sb("gateT", [CAP, NE + 1])
        idxT = sb("idxT", [CAP, NE + 1], U32)
        gate_c = sb("gate_c", [CAP, 2])
        idx_c = sb("idx_c", [CAP, 2, 2], U32)
        ps = [ctx.enter_context(nc.psum_tensor(f"bank{i}", [P, 1024], F32)) for i in range(4)]

        def bank(i, a=0, b=NW):
            return ps[i // 2][:, NW * (i % 2) + a:NW * (i % 2) + b]

        const_in = sem("const_in")
        ring_full = [sem(f"ring_full{i}") for i in range(RING)]
        ring_used = sem("ring_used")
        high_done, low_dve, low_pool = sem("high_done"), sem("low_dve"), sem("low_pool")
        small_in = sem("small_in")
        bm_full = [sem(f"bm_full{i}") for i in range(2)]
        cs_ready = sem("cs_ready")
        mod_row, mod_tr, mod_col = sem("mod_row"), sem("mod_tr"), sem("mod_col")
        mod_out = [sem(f"mod_out{i}") for i in range(2)]
        amod_ready = sem("amod_ready")
        x_in = [sem(f"x_in{i}") for i in range(T)]
        mod_done = sem("mod_done")
        var_ready, sd_ready, xn_ready = sem("var_ready"), sem("sd_ready"), sem("xn_ready")
        norm_tr, norm_high, norm_low = sem("norm_tr"), sem("norm_high"), sem("norm_low")
        u_full, u_act, u_dve = sem("u_full"), sem("u_act"), sem("u_dve")
        c_var, c_sd, cn_ready = sem("c_var"), sem("c_sd"), sem("cn_ready")
        kpe_ready = sem("kpe_ready")
        rope_a = sem("rope_a")
        kv_out = sem("kv_out")
        x_out = sem("x_out")
        xn_out, y_done = ([sem(f"{n}{i}") for i in range(2)] for n in ("xn_out", "y_done"))
        ct_tr, ct_ev = sem("ct_tr"), sem("ct_ev")
        qm_full, qm_ready = sem("qm_full"), sem("qm_ready")
        vm_full, vm_ev = sem("vm_full"), sem("vm_ev")
        lam_z, lam_e, lam_ready = sem("lam_z"), sem("lam_e"), sem("lam_ready")
        prep_tr, prep_ev = sem("prep_tr"), sem("prep_ev")
        s_full, s_max, p_ready, w_ready = sem("s_full"), sem("s_max"), sem("p_ready"), sem("w_ready")
        es_ready = sem("es_ready")
        t_full, t_act, t_dve = sem("t_full"), sem("t_act"), sem("t_dve")
        o_full, o_ev = sem("o_full"), sem("o_ev")
        pad_ready, pad_out, rpb_in = sem("pad_ready"), sem("pad_out"), sem("rpb_in")
        natab_in, natab_ready = sem("natab_in"), sem("natab_ready")
        on_var, on_sd, on_ready = sem("on_var"), sem("on_sd"), sem("on_ready")
        ot_tr, ot_high, ot_low = sem("ot_tr"), sem("ot_high"), sem("ot_low")
        gate_full, b_full = sem("gate_full"), sem("b_full")
        g_sig, g_mul, g_add = sem("g_sig"), sem("g_mul"), sem("g_add")
        mt_tr, mt_high, mt_low = sem("mt_tr"), sem("mt_high"), sem("mt_low")
        wo_full, wo_half, x_new = sem("wo_full"), sem("wo_half"), sem("x_new")
        gate1_in, gate2_in, gfin_in = sem("gate1_in"), sem("gate2_in"), sem("gfin_in")
        lg_full, lg_sub, lg_exp, aff_ready = sem("lg_full"), sem("lg_sub"), sem("lg_exp"), sem("aff_ready")
        affT_tr, top_ready, topT_tr, topT_ready = sem("affT_tr"), sem("top_ready"), sem("topT_tr"), sem("topT_ready")
        idx_ready = sem("idx_ready")
        xe_in = [sem(f"xe_in{i}") for i in range(2)]
        xe_tr, xe_mod, xe_high, xe_ready = sem("xe_tr"), sem("xe_mod"), sem("xe_high"), sem("xe_ready")
        wr_high, wr_ready = sem("wr_high"), sem("wr_ready")
        silu_ready, hid_ready = sem("silu_ready"), sem("hid_ready")
        hid_tr, hidT_high, hidT_low = sem("hid_tr"), sem("hidT_high"), sem("hidT_low")
        y_ready, y_out, added = sem("y_ready"), sem("y_out"), sem("added")
        pe_held, pool_held = sem("pe_held"), sem("pool_held")
        dve_step, pool_step, exp_step = sem("dve_step"), sem("pool_step"), sem("exp_step")

        N_CONST = 6 + 2 * L
        N_SMALL = 18
        N_KV = 8
        BUF = 2

        def tok_in(l, m):
            if l == 0:
                return x_sample[0, m * P:(m + 1) * P, :] if m < TS else x_prompt[0]
            return x_dram[m * P:(m + 1) * P, :]

        def xn_of(q):
            return xn_att if q % 2 and q < 2 * L else xn_work

        def xn_store(l, m):
            return 16 * ((3 if m % 2 == 0 else 2) * l + m // 2 + 1)

        def w_chunk(w, n0, width, kq):
            return w.rearrange("(k p) n -> p k n", p=P)[:, kq * KC:(kq + 1) * KC, n0:n0 + width]

        def three(out, lhs, rhs_high, rhs_low, start, stop):
            nc.tensor.matmul(out, lhs[0], rhs_high, start=start, stop=False)
            nc.tensor.matmul(out, lhs[0], rhs_low, start=False, stop=False)
            return nc.tensor.matmul(out, lhs[1], rhs_high, start=False, stop=stop)

        def u_counts(l, g):
            return 13 * l + g // 2 + 1, 12 * l + (g + 1) // 2

        def k_src(br, b, kb):
            if br == "A":
                return c_ka[:, 128 * b:128 * b + 128] if kb == 0 else u[:, kb - 1, AK + 128 * b:AK + 128 * b + 128]
            if br == "B":
                return c_kb[:, 128 * b:128 * b + 128] if kb == 0 else u[:, kb - 1, BK + 128 * b:BK + 128 * b + 128]
            return c_kc[:, :] if kb == 0 else u[:, kb - 1, CK:CK + 128]

        def v_src(un, kb):
            h = un["head"]
            if un["br"] == "D":
                return vmla[:, kb, 64 * h:64 * h + 64]
            if un["br"] == "C":
                h = h // 2
            cv, off = {"A": (c_va, AV), "B": (c_vb, BV), "C": (c_vc, CV)}[un["br"]]
            return cv[:, 64 * h:64 * h + 64] if kb == 0 else u[:, kb - 1, off + 64 * h:off + 64 * h + 64]

        def gain_col(l, w, k, m):
            a = ((l * 2 + w) * KD + k) * 2 + (1 if m < TS else 0)
            return amod[:, a:a + 1]

        def shift_col(l, w, k, m):
            a = ((l * 6 + 3 * w) * KD + k) * 2 + (1 if m < TS else 0)
            return modcol[:, a:a + 1]

        block = ctx.enter_context(nc.Block())

        @block.sync
        def _(sp):
            sp.dma_start(ident[:, :], k_ident).then_inc(const_in, 16)
            with nc.allow_non_contiguous_dma("columns of small vectors"):
                sp.dma_start(cT[:, 0, :], c_ctx.rearrange("(k p) -> p k", p=P)).then_inc(const_in, 16)
                sp.dma_start(cT[:, 1, :], c[0].rearrange("(k p) -> p k", p=P)).then_inc(const_in, 16)
                for w, g in ((0, g_norm1), (1, g_norm2)):
                    for l in range(L):
                        sp.dma_start(gn_col[:, 2 * l + w, :], g[l].rearrange("(k p) -> p k", p=P)).then_inc(const_in, 16)
            sp.dma_start(rope[:, :, :], k_rope.rearrange("(m p) n -> p m n", p=P)).then_inc(const_in, 16)
            sp.dma_start(mask_na[:, :], k_mask_na).then_inc(const_in, 16)
            sp.dma_start(mask_sw[:, :, :], k_mask_sw).then_inc(const_in, 16)

            def fill(slot, src, used, width=NW):
                if used is not None:
                    sp.wait_ge(ring_used, used)
                sp.dma_start(ring[:, slot, :, 0:width], src).then_inc(ring_full[slot], 16)

            for l in range(L):
                w3 = w_mod[l].rearrange("(k p) n -> p k n", p=P)
                if l == 0:
                    for j in range(RING):
                        fill(j, w_chunk(w_mod[0], j // NQ * NW, NW, j % NQ), None)
                with sp.Fori(1 if l == 0 else 0, N_MOD // 2) as i:
                    for j in range(2 * NQ):
                        fill(j, w3[:, (j % NQ) * KC:(j % NQ + 1) * KC, bass.ds((i * 2 + j // NQ) * NW, NW)],
                             i * (2 * NQ) + (l * NQ * N_MOD + j - RING + 1))
            for l in range(L):
                if l:
                    sp.wait_ge(ot_tr, 2 * T * l)
                    sp.wait_ge(lg_full, l)
                    sp.wait_ge(on_ready, T * l)
                row = lambda a: a.rearrange("(a n) -> a n", a=1)
                small = [
                    (qn_b[:, :], row(mla_q_norm[l]).broadcast_to([P, QR])),
                    (kvn_b[:, :], row(mla_kv_norm[l]).broadcast_to([P, KVR])),
                    (lam_b[:, :], da_lambda[l].rearrange("a n -> (a n)").rearrange("(a n) -> a n", a=1).broadcast_to([P, 128])),
                    (sub_b[:, :], row(da_subln[l]).broadcast_to([P, HD])),
                    (sink_b[:, :], row(sw_sink[l]).broadcast_to([P, HEADS])),
                    (w_uq[:, :, :], mla_w_uq[l].rearrange("(k p) n -> p k n", p=P)),
                    (w_ukv[:, :], mla_w_ukv[l]),
                    (w_r[:, :, :], w_router[l].rearrange("(k p) n -> p k n", p=P)),
                    (rraw[:, :], na_rpb[l].rearrange("h a b -> (h a) b")),
                ]
                for dst, src in small:
                    sp.dma_start(dst, src).then_inc(small_in, 16)
                if l:
                    sp.wait_ge(xe_tr, 2 * (NE + 1) * (l - 1) + 2)
                for dst, src in [
                    (c_ka, cache_diff_k[0, l].rearrange("t h n -> t (h n)")),
                    (c_va, cache_diff_v[0, l].rearrange("t h n -> t (h n)")),
                    (c_kb, cache_na_k[0, l].rearrange("t h n -> t (h n)")),
                    (c_vb, cache_na_v[0, l].rearrange("t h n -> t (h n)")),
                    (c_kc, cache_swa_k[0, l].rearrange("t h n -> t (h n)")),
                    (c_vc, cache_swa_v[0, l].rearrange("t h n -> t (h n)")),
                    (c_ckv, cache_mla_ckv[0, l]),
                    (c_kpe[:, 0:64], cache_mla_ckv[0, l][:, 0:64]),
                    (c_kpe[:, 64:96], cache_mla_kpe[0, l]),
                ]:
                    sp.dma_start(dst, src).then_inc(small_in, 16)
                n = 0

                def dense(w, n0, width=NW, chunks=NQ):
                    nonlocal n
                    for kq in range(chunks):
                        g = chunk_no(l, n)
                        fill(g % RING, w_chunk(w, n0, width, kq), g - RING + 1, width)
                        n += 1

                for j in range(NG_IN):
                    dense(w_in[l], j * NW, WIN_N[j])
                for j in range(NG_GATE):
                    half, br = j // 4, j % 4
                    dense(w_gate[l], br * D + half * NW)
                    dense(w_branch[l, br], half * NW, chunks=1)
                for j in range(2):
                    dense(w_out[l], j * NW)
                g0 = chunk_no(l, CH_DENSE)
                with sp.Fori(0, NE // 2) as i:
                    for e in range(2):
                        for j in range(CH_EXP):
                            w = (w_e_gate, w_e_gate, w_e_up, w_e_up, w_e_down, w_e_down)[j // NQ]
                            half, kq = j // NQ % 2, j % NQ
                            g = g0 + e * CH_EXP + j
                            src = w[l].rearrange("e (k p) n -> p e k n", p=P)[
                                :, bass.ds(i * 2 + e, 1), kq * KC:(kq + 1) * KC, half * NW:(half + 1) * NW]
                            fill(g % RING, src.rearrange("p e k n -> p (e k) n"), i * (2 * CH_EXP) + (g - RING + 1))
            for j in range(HIGH):
                g = N_CHUNKS + j
                fill(g % RING, w_chunk(w_e_down[L - 1, NE - 1], 0, NW, j), g - RING + 1)

        @block.tensor
        def _(pe):
            mm, tr = nc.tensor.matmul, nc.tensor.transpose

            def split_done(g, i=None):
                s, n = (low_pool, LOW_POOL[g]) if by_pool(g) else (low_dve, LOW_DVE[g])
                if i is None:
                    pe.wait_ge(s, n)
                else:
                    pe.wait_ge(s, i * (2 * CH_EXP // 4 * (1 if by_pool(g) else 3)) + n)

            def turn4(dst, src, done):
                for k in range(4):
                    ins = tr(dst(k), src(k), ident[:, :])
                ins.then_inc(done, 1)

            pe.wait_ge(const_in, 16 * N_CONST)
            pe.wait_ge(cs_ready, 4)
            pe.sem_inc(mod_tr, BUF)
            for l in range(L):
                with pe.Fori(0, N_MOD // 2) as i:
                    def rows(j):
                        for kq in range(NQ):
                            c = NQ * j + kq
                            pe.wait_ge(low_dve, i * (2 * NQ) + (l * NQ * N_MOD + c + 1))
                            for k in range(KC):
                                kk = kq * KC + k
                                ins = three(bank(j)[0:2, :], [t[:, kk, :] for t in csT], high[:, c % HIGH, k, :], low[:, c % RING, k, :],
                                            kk == 0, kk == KD - 1)
                            ins.then_inc(ring_used, 1)

                    def cols(j):
                        pe.wait_ge(mod_row, i * 2 + (l * N_MOD + j + 1 + BUF))
                        pe.wait_ge(mod_col, i * 2 + (l * N_MOD + j - 1 + BUF))
                        pe.sem_inc(pe_held, 1)
                        for b in range(4):
                            ins = tr(bank(2 + j, 2 * b, 2 * b + 2), modrow[:, j, b * P:(b + 1) * P], ident[0:2, 0:2])
                        ins.then_inc(mod_tr, 1)

                    rows(0)
                    rows(1)
                    cols(0)
                    cols(1)
            pe.wait_ge(mod_col, L * N_MOD + BUF)

            for l in range(L):
                q1, q2 = 2 * l, 2 * l + 1

                def norm_turn(q, m, banks):
                    t = T * q + m
                    pe.wait_ge(xn_ready, t + 1)
                    if m >= 2:
                        pe.wait_ge(norm_low, 2 * (t - 1))
                    for half in range(2):
                        b = banks + 2 * (m % 2) + half
                        turn4(lambda k: bank(b, k * P, (k + 1) * P),
                              lambda k: xn_of(q)[:, m % 2, (4 * half + k) * P:(4 * half + k + 1) * P], norm_tr)

                if l:
                    pe.wait_ge(y_ready, NE * l + 1)
                    pe.wait_ge(xe_ready, 2 * (NE + 1) * l)
                for m in range(T):
                    norm_turn(q1, m, 4)

                for n in range(NG_IN):
                    for kq in range(NQ):
                        g = chunk_no(l, NQ * n + kq)
                        split_done(g)
                        for m in range(T):
                            q = T * n + m
                            if n == 0 and kq == 0:
                                pe.wait_ge(norm_low, 2 * (T * q1 + m + 1))
                            if kq == 0 and q >= 8:
                                a, d = u_counts(l, q - 8)
                                pe.wait_ge(u_act, a)
                                pe.wait_ge(u_dve, d)
                            for k in range(KC):
                                kk = kq * KC + k
                                ins = three(bank(q % 8, 0, WIN_N[n]), [t[:, kk, m * P:(m + 1) * P] for t in hT],
                                            high[:, g % HIGH, k, 0:WIN_N[n]], low[:, g % RING, k, 0:WIN_N[n]], kk == 0, kk == KD - 1)
                            if kq == NQ - 1 and m < T - 1:
                                ins.then_inc(u_full, 1)
                        ins.then_inc(ring_used, 1)

                pe.wait_ge(u_act, 13 * (l + 1))
                pe.wait_ge(u_dve, 12 * (l + 1))
                for m in range(T + 1):
                    if m < T:
                        pe.wait_ge(cn_ready, T * l + m + 1)
                        pe.wait_ge(kpe_ready, TS * l + min(m + 1, TS))
                    else:
                        pe.wait_ge(small_in, 16 * N_SMALL * (l + 1))
                    if m >= 4:
                        pe.wait_ge(ct_ev, 6 * l + m - 3)
                    b = m % 4
                    tr(bank(b, 2 * P, 3 * P), u[:, m, DCKV:DCKV + P] if m < T else c_ckv, ident[:, :])
                    if m < T:
                        for k in range(2):
                            tr(bank(b, k * P, (k + 1) * P), u[:, m, DCQ + k * P:DCQ + (k + 1) * P], ident[:, :])
                    tr(bank(b, 3 * P, 4 * P)[0:DM_, :], u[:, m, DRQ:DRQ + DM_] if m < T else c_kpe, ident[:, :]).then_inc(ct_tr, 1)
                for m in range(T):
                    pe.wait_ge(ct_ev, 6 * l + m + 1)
                    if m >= 4:
                        pe.wait_ge(qm_ready, T * l + m - 3)
                    for k in range(2):
                        ins = mm(bank(4 + m % 4, 0, HEADS * DM_), cqT[:, k, m * P:(m + 1) * P], w_uq[:, k, :], start=(k == 0), stop=(k == 1))
                    ins.then_inc(qm_full, 1)
                pe.wait_ge(ct_ev, 6 * l + 6)
                for kb in range(6):
                    ins = mm(bank(kb // 2, 256 * (kb % 2), 256 * (kb % 2) + 256), ckvT[:, kb * P:(kb + 1) * P],
                             w_ukv[:, :].rearrange("p (h n) -> p h n", h=HEADS)[:, :, NOPE:NOPE + HD], start=True, stop=True)
                    if kb % 2:
                        ins.then_inc(vm_full, 1)

                def prep(bi, g):
                    br, b = BLOCKS[bi]
                    if 4 * bi + g:
                        pe.wait_ge(prep_ev, 4 * len(BLOCKS) * l + 4 * bi + g)
                    if bi == 0 and g == 0:
                        pe.wait_ge(qm_ready, T * (l + 1))
                        pe.wait_ge(vm_ev, 3 * (l + 1))
                    if br in "AC" and g == 0:
                        pe.wait_ge(rope_a, TS * (l + 1))
                    if g < 2:
                        for i, m in enumerate(range(4) if g == 0 else [4]):
                            if br == "D":
                                src, n = u[:, m, DCQ + DM_ * b:DCQ + DM_ * (b + 1)], DM_
                            else:
                                src, n = u[:, m, O_COL[br] + P * b:O_COL[br] + P * (b + 1)], P
                            ins = tr(bank(7, i * P, (i + 1) * P)[0:n, :], src, ident[:, :])
                    elif br == "D":
                        a, e = (0, 512) if g == 2 else (512, 768)
                        ins = mm(bank(7, 0, e - a)[0:NOPE, :], w_ukv[:, 128 * b:128 * b + NOPE], ckvT[:, a:e], start=True, stop=True)
                    else:
                        for i, kb in enumerate(range(4) if g == 2 else [4, 5]):
                            ins = tr(bank(7, i * P, (i + 1) * P), k_src(br, b, kb), ident[:, :])
                    ins.then_inc(prep_tr, 1)

                def scores(ui):
                    un = UNITS[ui]
                    if ui == FIRST_UNIT[un["bi"]]:
                        pe.wait_ge(prep_ev, 4 * len(BLOCKS) * l + 4 * (un["bi"] + 1))
                    for (r0, rn), p in zip(un["rows"], un["passes"]):
                        if p >= 2:
                            pe.wait_ge(p_ready, N_PASS * l + p - 1)
                        b = un["bi"] % 2
                        for col, a, w in segments(un):
                            ins = mm(ps[p % 2][:, col:col + w], qT[r0:r0 + rn, b, un["m"] * P:(un["m"] + 1) * P],
                                     kT[r0:r0 + rn, b, a:a + w], start=True, stop=True)
                        ins.then_inc(s_full, 1)

                def turn(ui):
                    un = UNITS[ui]
                    if un["br"] == "A":
                        pe.wait_ge(w_ready, len(A_UNITS) * l + A_BEFORE[ui] + 1)
                    else:
                        pe.wait_ge(p_ready, N_PASS * l + un["passes"][0] + 1)
                    if ui:
                        pe.wait_ge(t_act, N_UNIT * l + ui)
                        pe.wait_ge(t_dve, TAIL_BEFORE[N_UNIT] * l + TAIL_BEFORE[ui])
                    for i in range(len(un["kb"])):
                        ins = tr(ps[2][:, i * P:(i + 1) * P], prob[:, un["passes"][0] % 4, i * P:(i + 1) * P], ident[:, :])
                    ins.then_inc(t_full, 1)

                def values(ui):
                    un = UNITS[ui]
                    pe.wait_ge(t_act, N_UNIT * l + ui + 1)
                    pe.wait_ge(t_dve, TAIL_BEFORE[N_UNIT] * l + TAIL_BEFORE[ui + 1])
                    if ui:
                        pe.wait_ge(o_ev, N_UNIT * l + ui)
                    for i, kb in enumerate(un["kb"]):
                        ins = mm(bank(6, 0, HD), probT[:, ui % 2, i * P:(i + 1) * P], v_src(un, kb),
                                 start=(i == 0), stop=(i == len(un["kb"]) - 1))
                    ins.then_inc(o_full, 1)

                for g in range(4):
                    prep(0, g)
                for ui in range(N_UNIT + 2):
                    if ui < N_UNIT:
                        scores(ui)
                    if 1 <= ui <= N_UNIT:
                        turn(ui - 1)
                    if ui >= 2:
                        values(ui - 2)
                    for bi, g in PREP_AT.get(ui, []):
                        prep(bi, g)

                pe.wait_ge(o_ev, N_UNIT * (l + 1))
                for m in range(T):
                    pe.wait_ge(on_ready, T * l + m + 1)
                    if m >= 2:
                        pe.wait_ge(ot_low, 2 * (T * l + m - 1))
                    for half in range(2):
                        turn4(lambda k: bank(2 * (m % 2) + half, k * P, (k + 1) * P),
                              lambda k: u[:, m, O_BLOCKS[4 * half + k]:O_BLOCKS[4 * half + k] + P], ot_tr)
                pe.wait_ge(ot_low, 2 * T * (l + 1))

                for j in range(NG_GATE):
                    for kq in range(NQ + 1):
                        g = chunk_no(l, CH_IN + (NQ + 1) * j + kq)
                        split_done(g)
                        for m in range(T):
                            q = T * j + m
                            if kq == 0 and q >= SIG:
                                pe.wait_ge(g_sig, NG_GATE * T * l + q - SIG + 1)
                            if kq == NQ and q >= 2:
                                pe.wait_ge(g_mul, NG_GATE * T * l + q - 1)
                            for k in range(KC):
                                kk = kq * KC + k
                                if kq < NQ:
                                    ins = three(bank(q % SIG), [t[:, kk, m * P:(m + 1) * P] for t in hT],
                                                high[:, g % HIGH, k, :], low[:, g % RING, k, :], kk == 0, kk == KD - 1)
                                else:
                                    ins = three(bank(6 + q % 2), [t[:, KC * (j % 4) + k, m * P:(m + 1) * P] for t in oT],
                                                high[:, g % HIGH, k, :], low[:, g % RING, k, :], k == 0, k == KC - 1)
                            if m < T - 1 and kq == NQ - 1:
                                ins.then_inc(gate_full, 1)
                            if m < T - 1 and kq == NQ:
                                ins.then_inc(b_full, 1)
                        ins.then_inc(ring_used, 1)

                pe.wait_ge(g_mul, NG_GATE * T * (l + 1))
                for m in range(T):
                    pe.wait_ge(g_add, 6 * T * l + 5 * T + m + 1)
                    if m >= 2:
                        pe.wait_ge(mt_low, 2 * (T * l + m - 1))
                    for half in range(2):
                        turn4(lambda k: bank(4 + 2 * (m % 2) + half, k * P, (k + 1) * P),
                              lambda k: merged[:, m, (4 * half + k) * P:(4 * half + k + 1) * P], mt_tr)

                for half in range(2):
                    for kq in range(NQ):
                        g = chunk_no(l, CH_DENSE - 2 * NQ + NQ * half + kq)
                        split_done(g)
                        for m in range(T):
                            q = T * half + m
                            if half == 0 and kq == 0:
                                pe.wait_ge(mt_low, 2 * (T * l + m + 1))
                                if m == 4:
                                    pe.wait_ge(mt_low, 2 * T * (l + 1))
                            if kq == 0 and q >= 8:
                                pe.wait_ge(wo_half, T * l + q - 7)
                            for k in range(KC):
                                kk = kq * KC + k
                                ins = three(bank(q % 8), [t[:, kk, m * P:(m + 1) * P] for t in mergedT],
                                            high[:, g % HIGH, k, :], low[:, g % RING, k, :], kk == 0, kk == KD - 1)
                            if kq == NQ - 1 and m < T - 1:
                                ins.then_inc(wo_full, 1)
                        ins.then_inc(ring_used, 1)
                pe.wait_ge(wo_half, T * (l + 1))
                for m in range(T):
                    norm_turn(q2, m, 2)

                pe.wait_ge(norm_low, 2 * T * (q2 + 1))
                pe.wait_ge(x_new, T * (l + 1))
                pe.wait_ge(wr_ready, l + 1)
                for m in range(T):
                    for k in range(KD):
                        ins = three(bank(0, NE * m, NE * (m + 1)), [t[:, k, m * P:(m + 1) * P] for t in hT],
                                    w_r2[0][:, k, :], w_r2[1][:, k, :], k == 0, k == KD - 1)
                ins.then_inc(lg_full, 1)
                pe.wait_ge(aff_ready, l + 1)
                for m in range(T):
                    ins = tr(bank(1 + m // 4, (m % 4) * P, (m % 4 + 1) * P)[0:NE, :], lg[:, m, :], ident[:, :])
                ins.then_inc(affT_tr, 1)
                pe.wait_ge(top_ready, l + 1)
                tr(bank(3, 0, NE)[0:CAP, :], top_v[:, :], ident[0:NE, 0:NE])
                tr(bank(3, NE, 2 * NE)[0:CAP, :], top_f[:, :], ident[0:NE, 0:NE]).then_inc(topT_tr, 1)

                def rows_turn(b, fills):
                    pe.wait_ge(xe_in[b], fills)
                    for half in range(2):
                        for k in range(4):
                            kk = 4 * half + k
                            ins = tr(bank(6 + half, k * CAP, (k + 1) * CAP), xe[0:CAP, b, kk * P:(kk + 1) * P], ident[0:CAP, 0:CAP])
                        ins.then_inc(xe_tr, 1)

                pe.wait_ge(topT_ready, l + 1)
                rows_turn(0, 16 * (9 * l + 1))
                g0 = chunk_no(l, CH_DENSE)
                with pe.Fori(0, NE // 2) as i:
                    for e in range(2):
                        n_exp = i * 2 + (NE * l + e)
                        n_prep = i * 2 + ((NE + 1) * l + e)

                        def part(j, stat):
                            g = g0 + e * CH_EXP + j
                            split_done(g, i)
                            for k in range(KC):
                                kk = (j % NQ) * KC + k
                                ins = three(bank(j // NQ)[0:CAP, :], stat(kk), high[:, g % HIGH, k, :], low[:, g % RING, k, :], kk == 0, kk == KD - 1)
                            ins.then_inc(ring_used, 1)

                        pe.wait_ge(xe_ready, n_prep * 2 + 2)
                        for j in range(2 * NQ):
                            part(j, lambda kk: [t[:, e, kk, :] for t in xeT])
                        rows_turn(1 - e, i * 16 + 16 * (8 * l + 1) if e == 0 else i * 16 + 16 * (9 * l + 2))
                        for j in range(2 * NQ, 4 * NQ):
                            part(j, lambda kk: [t[:, e, kk, :] for t in xeT])
                        pe.wait_ge(xe_ready, n_prep * 2 + 4)
                        for half in range(2):
                            pe.wait_ge(hid_ready, n_exp * 2 + (half + 1 + BUF))
                            for k in range(4):
                                kk = 4 * half + k
                                ins = tr(bank(6 + half, k * CAP, (k + 1) * CAP), hid[0:CAP, kk * P:(kk + 1) * P], ident[0:CAP, 0:CAP])
                            ins.then_inc(hid_tr, 1)
                        pe.wait_ge(y_ready, n_exp + 1)
                        for j in range(4 * NQ, 6 * NQ):
                            if j in (4 * NQ, 4 * NQ + 2):
                                pe.wait_ge(hidT_low, n_exp * 2 + (2 if j > 4 * NQ else 1))
                            part(j, lambda kk: [t[:, kk, :] for t in hidT])

        @block.scalar
        def _(act):
            A = nc.scalar.activation

            def split_high(g, i=None):
                if i is None:
                    act.wait_ge(ring_full[g % RING], 16 * (g // RING + 1))
                    if g >= HIGH:
                        act.wait_ge(ring_used, g - HIGH + 1)
                else:
                    act.wait_ge(ring_full[g % RING], i * (16 * 2 * CH_EXP // RING) + 16 * (g // RING + 1))
                    act.wait_ge(ring_used, i * (2 * CH_EXP) + (g - HIGH + 1))
                w = width_of(g)
                A(high[:, g % HIGH, :, 0:w], ring[:, g % RING, :, 0:w], ACT.Copy).then_inc(high_done, 1)

            def high_part(dst, src, done):
                return A(dst, src.rearrange("p (k n) -> p k n", k=4), ACT.Copy).then_inc(done, 1)

            act.wait_ge(const_in, 16 * N_CONST)
            for b in range(2):
                act.sem_inc(mod_out[b], 16)
            for g in range(2):
                A(csf[:, :, g], cT[:, g, :], ACT.Silu).then_inc(cs_ready, 1)
            act.wait_ge(cs_ready, 2)
            A(csT[0][:, :, :], csf[:, :, :], ACT.Copy).then_inc(cs_ready, 1)
            for g in range(HIGH):
                split_high(g)
            for l in range(L):
                with act.Fori(0, N_MOD // 2) as i:
                    for j in range(2):
                        act.wait_ge(mod_row, i * 2 + (l * N_MOD + j - 1 + BUF))
                        act.dma_start(bm[:, j, :], b_mod[l:l + 1, bass.ds((i * 2 + j) * NW, NW)].broadcast_to([2, NW])).then_inc(bm_full[j], 16)
                        for kq in range(NQ):
                            g = l * NQ * N_MOD + NQ * j + kq + HIGH
                            act.wait_ge(ring_full[g % RING], i * 16 + 16 * (g // RING + 1))
                            act.wait_ge(ring_used, i * (2 * NQ) + (g - HIGH + 1))
                            A(high[:, g % HIGH, :, :], ring[:, g % RING, :, :], ACT.Copy).then_inc(high_done, 1)
                        act.wait_ge(mod_row, i * 2 + (l * N_MOD + j + 1 + BUF))
                        act.dma_start(mod_dram[l][:, bass.ds((i * 2 + j) * NW, NW)], modrow[:, j, :]).then_inc(mod_out[j], 16)
            act.wait_ge(amod_ready, 2 * L)

            for l in range(L):
                q1, q2 = 2 * l, 2 * l + 1

                def std(q, m):
                    t = T * q + m
                    act.wait_ge(var_ready, t + 1)
                    A(sd[:, m:m + 1], var[:, m:m + 1], ACT.Sqrt).then_inc(sd_ready, 1)

                def modulate(q, m, banks):
                    t = T * q + m
                    for half in range(2):
                        act.wait_ge(norm_tr, 2 * t + half + 1)
                        b = banks + 2 * (m % 2) + half
                        for k in range(4):
                            kk = 4 * half + k
                            ins = A(bank(b, k * P, (k + 1) * P), bank(b, k * P, (k + 1) * P), ACT.Identity,
                                    bias=shift_col(l, q % 2, kk, m), scale=gain_col(l, q % 2, kk, m))
                        ins.then_inc(mod_done, 1)
                        act.wait_ge(mod_done, 2 * t + half + 1)
                        high_part(hT[0][:, 4 * half:4 * half + 4, m * P:(m + 1) * P], bank(b), norm_high)

                std(q1, 0)
                for m in range(T):
                    if m + 1 < T:
                        std(q1, m + 1)
                    modulate(q1, m, 4)

                for n in range(NG_IN):
                    for kq in range(NQ):
                        g = chunk_no(l, NQ * n + kq)
                        if kq == NQ - 1:
                            for m in range(T):
                                q = T * n + m
                                if q % 2 == 0:
                                    if m < T - 1:
                                        act.wait_ge(u_full, (T - 1) * (NG_IN * l + n) + m + 1)
                                    else:
                                        act.wait_ge(ring_used, g + 1)
                                    A(u[:, m, n * NW:n * NW + WIN_N[n]], bank(q % 8, 0, WIN_N[n]), ACT.Copy).then_inc(u_act, 1)
                        split_high(g + HIGH)

                act.wait_ge(c_var, l + 1)
                A(r10, v10, ACT.Sqrt).then_inc(c_sd, 1)
                for m in range(T + 1):
                    act.wait_ge(ct_tr, 6 * l + m + 1)
                    b = m % 4
                    at = (m + 1) * P if m < T else 0
                    if m < T:
                        A(cqT[:, :, m * P:(m + 1) * P], bank(b, 0, 2 * P).rearrange("p (k n) -> p k n", k=2), ACT.Copy)
                    A(ckvT[:, at:at + P], bank(b, 2 * P, 3 * P), ACT.Copy)
                    for z in range(2):
                        ins = A(kT[NOPE:DM_, z, at:at + P], bank(b, 3 * P, 4 * P)[NOPE:DM_, :], ACT.Copy)
                    ins.then_inc(ct_ev, 1)
                for z in range(3):
                    act.wait_ge(vm_full, 3 * l + z + 1)
                    A(vmla[:, 2 * z:2 * z + 2, :], bank(z).rearrange("p (k n) -> p k n", k=2), ACT.Copy).then_inc(vm_ev, 1)
                act.wait_ge(lam_z, l + 1)
                A(lam, lam, ACT.Exp).then_inc(lam_e, 1)

                def prep_out(bi, g):
                    br, b = BLOCKS[bi]
                    z = bi % 2
                    act.wait_ge(prep_tr, 4 * len(BLOCKS) * l + 4 * bi + g + 1)
                    a, e = ((0, 512), (512, 640), (0, 512), (512, 768))[g]
                    n = e - a
                    if g < 2:
                        r = DM_ if br == "D" else P
                        ins = A(qT[0:r, z, a:e], bank(7, 0, n)[0:r, :], ACT.Copy)
                    elif br == "C":
                        A(kT[0:64, z, a:e], bank(7, 0, n)[64 * b:64 * b + 64, :], ACT.Copy)
                        ins = A(kT[64:128, z, a:e], bank(7, 0, n)[64 * b:64 * b + 64, :], ACT.Copy)
                    else:
                        r = NOPE if br == "D" else P
                        ins = A(kT[0:r, z, a:e], bank(7, 0, n)[0:r, :], ACT.Copy)
                    ins.then_inc(prep_ev, 1)

                for g in range(4):
                    prep_out(0, g)
                for ui in range(N_UNIT + 2):
                    if ui < N_UNIT:
                        un = UNITS[ui]
                        w = len(un["kb"]) * P
                        for p in un["passes"]:
                            act.wait_ge(s_max, N_PASS * l + p + 1)
                            if p >= 4:
                                act.wait_ge(t_full, N_UNIT * l + UNIT_OF[p - 4] + 1)
                            A(prob[:, p % 4, 0:w], ps[p % 2][:, 0:w], ACT.Exp, bias=negm[:, p % 8:p % 8 + 1],
                              scale=SCALE[un["br"]], accum_out=sm[:, p % 8:p % 8 + 1]).then_inc(p_ready, 1)
                        if un["br"] == "C":
                            p, h = un["passes"][0], un["head"]
                            A(es[:, ui % 4:ui % 4 + 1], sink_b[:, h:h + 1], ACT.Exp, bias=negm[:, p % 8:p % 8 + 1],
                              scale=SCALE["C"]).then_inc(es_ready, 1)
                    if 1 <= ui <= N_UNIT:
                        v = ui - 1
                        w = min(len(UNITS[v]["kb"]), 4) * P
                        act.wait_ge(t_full, N_UNIT * l + v + 1)
                        if v >= 2:
                            act.wait_ge(o_full, N_UNIT * l + v - 1)
                        A(probT[:, v % 2, 0:w], ps[2][:, 0:w], ACT.Copy).then_inc(t_act, 1)
                    for bi, g in PREP_AT.get(ui, []):
                        prep_out(bi, g)

                act.wait_ge(on_var, l + 1)
                A(r20, v20, ACT.Sqrt).then_inc(on_sd, 1)
                for m in range(T):
                    for half in range(2):
                        act.wait_ge(ot_tr, 2 * (T * l + m) + half + 1)
                        high_part(oT[0][:, 4 * half:4 * half + 4, m * P:(m + 1) * P], bank(2 * (m % 2) + half), ot_high)

                for j in range(NG_GATE):
                    for kq in range(NQ + 1):
                        g = chunk_no(l, CH_IN + (NQ + 1) * j + kq)
                        if kq == NQ - 1:
                            for m in range(T):
                                q = T * j + m
                                if m < T - 1:
                                    act.wait_ge(gate_full, (T - 1) * (NG_GATE * l + j) + m + 1)
                                else:
                                    act.wait_ge(ring_used, g + 1)
                                if q >= SIG:
                                    act.wait_ge(g_mul, NG_GATE * T * l + q - SIG + 1)
                                A(sig[:, q % SIG, :], bank(q % SIG), ACT.Sigmoid).then_inc(g_sig, 1)
                        split_high(g + HIGH)
                for m in range(T):
                    for half in range(2):
                        act.wait_ge(mt_tr, 2 * (T * l + m) + half + 1)
                        high_part(mergedT[0][:, 4 * half:4 * half + 4, m * P:(m + 1) * P], bank(4 + 2 * (m % 2) + half), mt_high)
                A(w_r2[0][:, :, :], w_r[:, :, :], ACT.Copy).then_inc(wr_high, 1)

                for c in range(CH_DENSE - 2 * NQ, CH_DENSE):
                    split_high(chunk_no(l, c) + HIGH)

                std(q2, 0)
                for m in range(T):
                    if m + 1 < T:
                        std(q2, m + 1)
                    modulate(q2, m, 2)

                act.wait_ge(lg_sub, l + 1)
                A(lg[:, :, :], lg[:, :, :], ACT.Exp).then_inc(lg_exp, 1)

                g0 = chunk_no(l, CH_DENSE)

                def rows_high(b, mods):
                    for half in range(2):
                        act.wait_ge(xe_mod, mods + (half + 1))
                        high_part(xeT[0][:, b, 4 * half:4 * half + 4, :], bank(6 + half, 0, 4 * CAP), xe_high)

                rows_high(0, 2 * (NE + 1) * l)
                with act.Fori(0, NE // 2) as i:
                    for e in range(2):
                        n_exp = i * 2 + (NE * l + e)
                        n_prep = i * 2 + ((NE + 1) * l + e)
                        for j in range(CH_EXP):
                            g = g0 + e * CH_EXP + j
                            if j in (NQ, 2 * NQ):
                                half = j // NQ - 1
                                act.wait_ge(ring_used, i * (2 * CH_EXP) + (g0 + e * CH_EXP + j))
                                act.wait_ge(hid_ready, n_exp * 2 + BUF)
                                A(sil[0:CAP, half, :], bank(half)[0:CAP, :], ACT.Silu).then_inc(silu_ready, 1)
                            if j == 2 * NQ + 1:
                                rows_high(1 - e, n_prep * 2 + 2)
                            split_high(g + HIGH, i)
                            if j == 4 * NQ - 1:
                                for half in range(2):
                                    act.wait_ge(hid_tr, n_exp * 2 + (half + 1))
                                    high_part(hidT[0][:, 4 * half:4 * half + 4, :], bank(6 + half, 0, 4 * CAP), hidT_high)

            for m in range(T):
                act.wait_ge(var_ready, T * 2 * L + m + 1)
                A(sd[:, m:m + 1], var[:, m:m + 1], ACT.Sqrt).then_inc(sd_ready, 1)

        @block.vector
        def _(dve):
            V = nc.vector
            steps = [0]

            def then(ins):
                steps[0] += 1
                ins.then_inc(dve_step, 1)
                dve.wait_ge(dve_step, steps[0])

            def split_low(g):
                if by_pool(g):
                    return
                dve.wait_ge(high_done, g + 1)
                w = width_of(g)
                V.tensor_tensor(low[:, g % RING, :, 0:w], ring[:, g % RING, :, 0:w], high[:, g % HIGH, :, 0:w].bitcast(F32),
                                ALU.subtract).then_inc(low_dve, 1)

            def low_part(dst, src, top, done):
                V.tensor_tensor(dst, src.rearrange("p (k n) -> p k n", k=4), top.bitcast(F32), ALU.subtract).then_inc(done, 1)

            def backwards(ap):
                dims = [list(d) for d in ap.ap]
                step, n = dims[-1]
                return bass.AP(ap.tensor, ap.offset + step * (n - 1), dims[:-1] + [[-step, n]])

            def rope_tile(X, cos, sin, tmp, heads, q):
                t = tmp.rearrange("p (h a j q) -> p h a j q", h=heads, a=2, j=2)
                for j in range(2):
                    s = sin.rearrange("p (o a j q) -> p o a j q", o=1, a=2, j=2)[:, :, :, j, :].broadcast_to([P, heads, 2, q])
                    then(V.tensor_tensor(t[:, :, :, j, :], X[:, :, :, 1 - j, :], s, ALU.mult))
                flat = X.rearrange("p h a j q -> p h (a j q)")
                cc = cos.rearrange("p (o n) -> p o n", o=1).broadcast_to([P, heads, 4 * q])
                then(V.tensor_tensor(flat, flat, cc, ALU.mult))
                return V.tensor_tensor(flat, flat, tmp.rearrange("p (h n) -> p h n", h=heads), ALU.add)

            then(V.memset(rpad[:, :], 0.0))
            dve.wait_ge(const_in, 16 * N_CONST)
            dve.sem_inc(mod_row, BUF)
            dve.sem_inc(mod_col, BUF)
            dve.sem_inc(hid_ready, BUF)
            dve.sem_inc(y_ready, 1)
            dve.wait_ge(cs_ready, 3)
            V.tensor_tensor(csT[1][:, :, :], csf[:, :, :], csT[0][:, :, :].bitcast(F32), ALU.subtract).then_inc(cs_ready, 1)
            for g in range(HIGH):
                split_low(g)
            for l in range(L):
                with dve.Fori(0, N_MOD // 2) as i:
                    for j in range(2):
                        q0 = l * N_MOD + j
                        for kq in range(NQ):
                            g = l * NQ * N_MOD + NQ * j + kq + HIGH
                            dve.wait_ge(high_done, i * (2 * NQ) + (g + 1))
                            V.tensor_tensor(low[:, g % RING, :, :], ring[:, g % RING, :, :], high[:, g % HIGH, :, :].bitcast(F32),
                                            ALU.subtract).then_inc(low_dve, 1)
                        dve.wait_ge(ring_used, i * (2 * NQ) + (NQ * q0 + NQ))
                        dve.wait_ge(bm_full[j], i * 16 + 16 * (l * (N_MOD // 2) + 1))
                        dve.wait_ge(mod_tr, i * 2 + (q0 - 1 + BUF))
                        dve.wait_ge(mod_out[j], i * 16 + 16 * (l * (N_MOD // 2) + 1))
                        V.tensor_tensor(modrow[:, j, :], bank(j)[0:2, :], bm[:, j, :], ALU.add).then_inc(mod_row, 1)
                    for j in range(2):
                        q0 = l * N_MOD + j
                        dve.wait_ge(mod_tr, i * 2 + (q0 + 1 + BUF))
                        V.tensor_copy(modcol[:, bass.ds(i * 16 + q0 * 8, 8)], bank(2 + j, 0, 8)).then_inc(mod_col, 1)
            dve.wait_ge(mod_col, L * N_MOD + BUF)
            for l in range(L):
                for w in range(2):
                    a = (l * 6 + 1 + 3 * w) * KD * 2
                    V.scalar_tensor_tensor(
                        out=amod[:, (l * 2 + w) * KD * 2:(l * 2 + w + 1) * KD * 2].rearrange("p (k g) -> p k g", g=2),
                        in0=modcol[:, a:a + KD * 2].rearrange("p (k g) -> p k g", g=2), scalar=1.0,
                        in1=gn_col[:, l * 2 + w, :].rearrange("p (k o) -> p k o", o=1).broadcast_to([P, KD, 2]),
                        op0=ALU.add, op1=ALU.mult).then_inc(amod_ready, 1)
            dve.wait_ge(amod_ready, 2 * L)

            def stats(q, m, last=False):
                t = T * q + m
                then(V.tensor_tensor_reduce(sq, xt[:, m, :], xt[:, m, :], 1.0, 0.0, ALU.mult, ALU.add, ss[:, m:m + 1]))
                V.tensor_scalar(var[:, m:m + 1], ss[:, m:m + 1], 1.0 / D, EPS, ALU.mult, ALU.add).then_inc(var_ready, 1)
                dve.wait_ge(sd_ready, t + 1)
                then(V.reciprocal(rstd[:, m:m + 1], sd[:, m:m + 1]))
                if m >= 2 and not last:
                    dve.wait_ge(norm_tr, 2 * (t - 1))
                    if q % 2:
                        dve.wait_ge(xn_out[m % 2], xn_store(q // 2, m) - 16)
                if last:
                    if m >= 2:
                        dve.wait_ge(y_done[m % 2], 16 * (m // 2))
                    V.scalar_tensor_tensor(out=xn_of(q)[:, m % 2, :], in0=xt[:, m, :], scalar=rstd[:, m:m + 1], in1=gfin_b,
                                           op0=ALU.mult, op1=ALU.mult).then_inc(xn_ready, 1)
                else:
                    V.tensor_scalar(xn_of(q)[:, m % 2, :], xt[:, m, :], rstd[:, m:m + 1], None, ALU.mult).then_inc(xn_ready, 1)

            def norm_lows(q, m, banks):
                t = T * q + m
                for half in range(2):
                    ks = slice(4 * half, 4 * half + 4)
                    dve.wait_ge(norm_high, 2 * t + half + 1)
                    low_part(hT[1][:, ks, m * P:(m + 1) * P], bank(banks + 2 * (m % 2) + half), hT[0][:, ks, m * P:(m + 1) * P], norm_low)

            for l in range(L):
                q1, q2 = 2 * l, 2 * l + 1
                for m in range(T + 1):
                    if m < T:
                        dve.wait_ge(x_in[m], 16 * (q1 + 1))
                        stats(q1, m)
                    if m >= 1:
                        norm_lows(q1, m - 1, 4)

                for n in range(NG_IN):
                    for kq in range(NQ):
                        g = chunk_no(l, NQ * n + kq)
                        if kq == NQ - 1:
                            for m in range(T):
                                q = T * n + m
                                if q % 2:
                                    if m < T - 1:
                                        dve.wait_ge(u_full, (T - 1) * (NG_IN * l + n) + m + 1)
                                    else:
                                        dve.wait_ge(ring_used, g + 1)
                                    V.tensor_copy(u[:, m, n * NW:n * NW + WIN_N[n]], bank(q % 8, 0, WIN_N[n])).then_inc(u_dve, 1)
                        split_low(g + HIGH)

                dve.wait_ge(small_in, 16 * N_SMALL * (l + 1))
                for m in range(T):
                    a, d = u_counts(l, 4 * T + m)
                    dve.wait_ge(u_act, a)
                    dve.wait_ge(u_dve, d)
                    then(V.tensor_tensor_reduce(sqs, u[:, m, DCQ:DCQ + QR], u[:, m, DCQ:DCQ + QR], 1.0, 0.0, ALU.mult, ALU.add, s10[:, 2 * m:2 * m + 1]))
                    then(V.tensor_tensor_reduce(sqs[:, 0:KVR], u[:, m, DCKV:DCKV + KVR], u[:, m, DCKV:DCKV + KVR], 1.0, 0.0, ALU.mult, ALU.add, s10[:, 2 * m + 1:2 * m + 2]))
                then(V.tensor_scalar(v10[:, 0:10:2], s10[:, 0:10:2], 1.0 / QR, EPS, ALU.mult, ALU.add))
                V.tensor_scalar(v10[:, 1:10:2], s10[:, 1:10:2], 1.0 / KVR, EPS, ALU.mult, ALU.add).then_inc(c_var, 1)
                for m in range(TS):
                    X = u[:, m, DKPE:DKPE + 32].rearrange("p (h a j q) -> p h a j q", h=1, a=2, j=2)
                    rope_tile(X, rope[:, m, 0:32], rope[:, m, 32:64], rtmp2[:, 0:32], 1, 8).then_inc(kpe_ready, 1)
                    dve.wait_ge(kpe_ready, TS * l + m + 1)
                dve.wait_ge(c_sd, l + 1)
                then(V.reciprocal(r10, r10))
                for m in range(T):
                    V.scalar_tensor_tensor(out=u[:, m, DCQ:DCQ + QR], in0=u[:, m, DCQ:DCQ + QR], scalar=r10[:, 2 * m:2 * m + 1],
                                           in1=qn_b[:, :], op0=ALU.mult, op1=ALU.mult)
                    V.scalar_tensor_tensor(out=u[:, m, DCKV:DCKV + KVR], in0=u[:, m, DCKV:DCKV + KVR], scalar=r10[:, 2 * m + 1:2 * m + 2],
                                           in1=kvn_b[:, :], op0=ALU.mult, op1=ALU.mult).then_inc(cn_ready, 1)

                then(V.tensor_tensor_reduce(rtmp2[:, 0:32], lam_b[:, 0:32], lam_b[:, 32:64], 1.0, 0.0, ALU.mult, ALU.add, lam[:, 0:1]))
                V.tensor_tensor_reduce(rtmp2[:, 32:64], lam_b[:, 64:96], lam_b[:, 96:128], 1.0, 0.0, ALU.mult, ALU.add, lam[:, 1:2]).then_inc(lam_z, 1)
                then(V.tensor_scalar(sub_b[:, :], sub_b[:, :], 1.0 - LAM_INIT[l], None, ALU.mult))
                then(V.tensor_scalar(sink_b[:, :], sink_b[:, :], 1.0 / SCALE["C"], None, ALU.mult))
                if l:
                    dve.wait_ge(pad_out, 16 * l)
                V.tensor_scalar(rpad[:, 48:79], backwards(rraw[:, :]), 1.0 / SCALE["B"], None, ALU.mult).then_inc(pad_ready, 1)

                for m in range(T):
                    dve.wait_ge(qm_full, T * l + m + 1)
                    if m == T - 1:
                        dve.wait_ge(kv_out, 16 * N_KV * (l + 1))
                    src = bank(4 + m % 4, 0, HEADS * DM_)
                    dst = u[:, m, DCQ:DCQ + HEADS * DM_]
                    if m == T - 1:
                        V.tensor_copy(dst, src).then_inc(qm_ready, 1)
                        continue
                    then(V.tensor_copy(dst, src))
                    X = dst.rearrange("p (h n) -> p h n", h=HEADS)[:, :, NOPE:DM_].rearrange("p h (a j q) -> p h a j q", a=2, j=2)
                    rope_tile(X, rope[:, m, 0:32], rope[:, m, 32:64], rtmp2[:, 0:128], HEADS, 8).then_inc(qm_ready, 1)
                    dve.wait_ge(qm_ready, T * l + m + 1)
                dve.wait_ge(lam_e, l + 1)
                then(V.tensor_tensor(neglam, lam[:, 1:2], lam[:, 0:1], ALU.subtract))
                then(V.tensor_scalar(neglam, neglam, LAM_INIT[l], None, ALU.subtract))

                for ui in range(N_UNIT + 2):
                    if ui < N_UNIT:
                        un = UNITS[ui]
                        br, m, w = un["br"], un["m"], len(un["kb"]) * P
                        if br == "B" and ui == FIRST_UNIT[un["bi"]]:
                            dve.wait_ge(natab_in, 64 * (2 * l + un["b"] + 1))
                            for h in range(2):
                                tab = na_tab[:, h, :].rearrange("p (j n) -> p j n", n=GRID_W)
                                msk = mask_na[:, :].rearrange("p (o n) -> p o n", o=1).broadcast_to([P, 14, GRID_W])
                                then(V.tensor_tensor(tab, tab, msk, ALU.add))
                        for p in un["passes"]:
                            dve.wait_ge(s_full, N_PASS * l + p + 1)
                            S = ps[p % 2]
                            if br == "B" and m < TS:
                                j0 = (6 - 2 * m) * GRID_W
                                loc = S[:, P:5 * P].rearrange("p (r n) -> p r n", n=GRID_W)
                                then(V.tensor_tensor(loc, loc, backwards(na_tab[:, un["hh"], j0:j0 + 4 * P].rearrange("p (r n) -> p r n", n=GRID_W)), ALU.add))
                            if br == "C" and m < TS:
                                if m > 0:
                                    then(V.tensor_tensor(S[:, P:2 * P], S[:, P:2 * P], mask_sw[:, 0, :], ALU.add))
                                if m < TS - 1:
                                    then(V.tensor_tensor(S[:, w - P:w], S[:, w - P:w], mask_sw[:, 1, :], ALU.add))
                            c8 = p % 8
                            then(V.tensor_reduce(mx[:, c8:c8 + 1], S[:, 0:w], AX.X, ALU.max))
                            if br == "C":
                                h = un["head"]
                                V.tensor_scalar(negm[:, c8:c8 + 1], mx[:, c8:c8 + 1], sink_b[:, h:h + 1], -SCALE[br], ALU.max, ALU.mult).then_inc(s_max, 1)
                            else:
                                V.tensor_scalar(negm[:, c8:c8 + 1], mx[:, c8:c8 + 1], -SCALE[br], None, ALU.mult).then_inc(s_max, 1)
                    if 1 <= ui <= N_UNIT:
                        v = ui - 1
                        un = UNITS[v]
                        w = len(un["kb"]) * P
                        if un["br"] == "A":
                            p1, p2 = un["passes"]
                            r = v % 8
                            dve.wait_ge(p_ready, N_PASS * l + p2 + 1)
                            then(V.reciprocal(cmap[:, v % 4:v % 4 + 1], sm[:, p2 % 8:p2 % 8 + 1]))
                            then(V.scalar_tensor_tensor(out=cmap[:, v % 4:v % 4 + 1], in0=cmap[:, v % 4:v % 4 + 1], scalar=neglam,
                                                        in1=sm[:, p1 % 8:p1 % 8 + 1], op0=ALU.mult, op1=ALU.mult))
                            V.scalar_tensor_tensor(out=prob[:, p1 % 4, 0:w], in0=prob[:, p2 % 4, 0:w], scalar=cmap[:, v % 4:v % 4 + 1],
                                                   in1=prob[:, p1 % 4, 0:w], op0=ALU.mult, op1=ALU.add).then_inc(w_ready, 1)
                        if len(un["kb"]) > 4:
                            dve.wait_ge(t_full, N_UNIT * l + v + 1)
                            if v >= 2:
                                dve.wait_ge(o_full, N_UNIT * l + v - 1)
                            V.tensor_copy(probT[:, v % 2, 4 * P:5 * P], ps[2][:, 4 * P:5 * P]).then_inc(t_dve, 1)
                    if ui >= 2:
                        v = ui - 2
                        un = UNITS[v]
                        p, r = un["passes"][0] % 8, v % 8
                        dve.wait_ge(p_ready, N_PASS * l + un["passes"][-1] + 1)
                        if un["br"] == "C":
                            dve.wait_ge(es_ready, N_C * l + C_BEFORE[v] + 1)
                            then(V.tensor_tensor(sm[:, p:p + 1], sm[:, p:p + 1], es[:, v % 4:v % 4 + 1], ALU.add))
                        then(V.reciprocal(rinv[:, r:r + 1], sm[:, p:p + 1]))
                        dve.wait_ge(o_full, N_UNIT * l + v + 1)
                        col = O_COL[un["br"]] + HD * un["head"]
                        V.tensor_scalar(u[:, un["m"], col:col + HD], bank(6, 0, HD), rinv[:, r:r + 1], None, ALU.mult).then_inc(o_ev, 1)

                dve.wait_ge(o_ev, N_UNIT * (l + 1))
                for m in range(T):
                    then(V.tensor_tensor(sqs, u[:, m, AQ:AQ + 256], u[:, m, AQ:AQ + 256], ALU.mult))
                    then(V.tensor_reduce(s20[:, 4 * m:4 * m + 4], sqs.rearrange("p (h n) -> p h n", h=HEADS), AX.X, ALU.add))
                V.tensor_scalar(v20, s20, 1.0 / HD, EPS, ALU.mult, ALU.add).then_inc(on_var, 1)
                dve.wait_ge(on_sd, l + 1)
                then(V.reciprocal(r20, r20))
                for m in range(T):
                    o = u[:, m, AQ:AQ + 256].rearrange("p (h n) -> p h n", h=HEADS)
                    rs = r20[:, 4 * m:4 * m + 4].rearrange("p (h o) -> p h o", o=1).broadcast_to([P, HEADS, HD])
                    gs = sub_b[:, :].rearrange("p (o n) -> p o n", o=1).broadcast_to([P, HEADS, HD])
                    then(V.tensor_tensor(o, o, rs, ALU.mult))
                    V.tensor_tensor(o, o, gs, ALU.mult).then_inc(on_ready, 1)
                for m in range(T):
                    for half in range(2):
                        ks = slice(4 * half, 4 * half + 4)
                        dve.wait_ge(ot_high, 2 * (T * l + m) + half + 1)
                        low_part(oT[1][:, ks, m * P:(m + 1) * P], bank(2 * (m % 2) + half), oT[0][:, ks, m * P:(m + 1) * P], ot_low)

                for j in range(NG_GATE):
                    half, br = divmod(j, 4)
                    for kq in range(NQ + 1):
                        g = chunk_no(l, CH_IN + (NQ + 1) * j + kq)
                        if kq == NQ:
                            for m in range(T):
                                q = T * j + m
                                dve.wait_ge(g_sig, NG_GATE * T * l + q + 1)
                                if m < T - 1:
                                    dve.wait_ge(b_full, (T - 1) * (NG_GATE * l + j) + m + 1)
                                else:
                                    dve.wait_ge(ring_used, g + 1)
                                if br == 0:
                                    dst = merged[:, m, half * NW:(half + 1) * NW]
                                else:
                                    dst = gtmp[:, q % 2, :]
                                    if ADDS[q - 1]:
                                        dve.wait_ge(g_add, 6 * T * l + ADDS[q - 1])
                                V.tensor_tensor(dst, sig[:, q % SIG, :], bank(6 + q % 2), ALU.mult).then_inc(g_mul, 1)
                        split_low(g + HIGH)
                for m in range(T):
                    for half in range(2):
                        ks = slice(4 * half, 4 * half + 4)
                        dve.wait_ge(mt_high, 2 * (T * l + m) + half + 1)
                        low_part(mergedT[1][:, ks, m * P:(m + 1) * P], bank(4 + 2 * (m % 2) + half), mergedT[0][:, ks, m * P:(m + 1) * P], mt_low)
                dve.wait_ge(wr_high, l + 1)
                V.tensor_tensor(w_r2[1][:, :, :], w_r[:, :, :], w_r2[0][:, :, :].bitcast(F32), ALU.subtract).then_inc(wr_ready, 1)

                def residual(half, m, g):
                    cols = slice(half * NW, (half + 1) * NW)
                    if m < T - 1:
                        dve.wait_ge(wo_full, (T - 1) * (2 * l + half) + m + 1)
                    else:
                        dve.wait_ge(ring_used, g + 1)
                    dve.wait_ge(x_in[m], 16 * (q2 + 1))
                    then(V.tensor_tensor(sq[:, 0:NW], bank((T * half + m) % 8), gate1_b[:, 1 if m < TS else 0, cols], ALU.mult))
                    return V.tensor_tensor(xt[:, m, cols], xt[:, m, cols], sq[:, 0:NW], ALU.add)

                for half in range(2):
                    for kq in range(NQ):
                        g = chunk_no(l, CH_DENSE - 2 * NQ + NQ * half + kq)
                        if kq == NQ - 1 and half == 0:
                            dve.wait_ge(gate1_in, 32 * (l + 1))
                            for m in range(T):
                                residual(0, m, g).then_inc(wo_half, 1)
                                dve.wait_ge(wo_half, T * l + m + 1)
                        if kq < NQ - 1 or half == 0:
                            split_low(g + HIGH)
                for m in range(T + 1):
                    if m < T:
                        residual(1, m, g).then_inc(x_new, 1)
                        dve.wait_ge(x_new, T * l + m + 1)
                        if m == T - 1:
                            split_low(g + HIGH)
                        stats(q2, m)
                    if m >= 1:
                        norm_lows(q2, m - 1, 2)

                dve.wait_ge(lg_full, l + 1)
                z = bank(0, 0, T * NE).rearrange("p (m e) -> p m e", m=T)
                col = lambda i: lgs[:, i, :].rearrange("p (m o) -> p m o", o=1).broadcast_to([P, T, NE])
                then(V.tensor_reduce(lgs[:, 0, :], z, AX.X, ALU.max))
                V.tensor_tensor(lg[:, :, :], z, col(0), ALU.subtract).then_inc(lg_sub, 1)
                dve.wait_ge(lg_exp, l + 1)
                then(V.tensor_reduce(lgs[:, 1, :], lg[:, :, :], AX.X, ALU.add))
                then(V.reciprocal(lgs[:, 1, :], lgs[:, 1, :]))
                V.tensor_tensor(lg[:, :, :], lg[:, :, :], col(1), ALU.mult).then_inc(aff_ready, 1)
                dve.wait_ge(affT_tr, l + 1)
                then(V.tensor_copy(affT[:, 0:NS], bank(1)[0:NE, :]))
                then(V.tensor_copy(affT[:, NS:NS + NP], bank(2, 0, NP)[0:NE, :]))
                for a, n, r0, rounds in ((0, NS, 0, CAP_S // 8), (NS, NP, CAP_S, CAP_P // 8)):
                    for r in range(rounds):
                        v8 = slice(r0 + 8 * r, r0 + 8 * r + 8)
                        src = affT[:, a:a + n]
                        then(V.max(top_v[:, v8], src))
                        then(V.max_index(top_i[:, v8], top_v[:, v8], src))
                        if r < rounds - 1:
                            then(V.match_replace(src, top_v[:, v8], src, -1.0))
                then(V.tensor_copy(top_f[:, 0:CAP_S], top_i[:, 0:CAP_S]))
                V.tensor_scalar(top_f[:, CAP_S:CAP], top_i[:, CAP_S:CAP], float(NS), None, ALU.add).then_inc(top_ready, 1)
                dve.wait_ge(topT_tr, l + 1)
                then(V.tensor_copy(gateT[:, 0:NE], bank(3, 0, NE)[0:CAP, :]))
                then(V.tensor_copy(gateT[:, NE:NE + 1], bank(3, 0, 1)[0:CAP, :]))
                then(V.tensor_copy(idxT[:, 0:NE], bank(3, NE, 2 * NE)[0:CAP, :]))
                V.tensor_copy(idxT[:, NE:NE + 1], bank(3, NE, NE + 1)[0:CAP, :]).then_inc(topT_ready, 1)
                dve.wait_ge(topT_ready, l + 1)
                then(V.tensor_copy(gate_c[:, 0:1], gateT[:, 0:1]))
                V.tensor_copy(idx_c[:, 0, 0:1], idxT[:, 0:1]).then_inc(idx_ready, 1)

                def exp_then(ins, count):
                    ins.then_inc(exp_step, 1)
                    dve.wait_ge(exp_step, count)

                def rows_mod(b, turned, base):
                    for half in range(2):
                        dve.wait_ge(xe_tr, turned + (half + 1))
                        ks = slice(4 * half, 4 * half + 4)
                        views = []
                        for g, c0, c1 in ((1, 0, CAP_S), (0, CAP_S, CAP)):
                            def wide(t, o):
                                return t[:, o:o + 2 * KD].rearrange("p (k g) -> p k g", g=2)[:, ks, g:g + 1].broadcast_to([P, 4, c1 - c0])
                            views.append((bank(6 + half, 0, 4 * CAP).rearrange("p (k n) -> p k n", k=4)[:, :, c0:c1],
                                          wide(amod, (l * 2 + 1) * KD * 2), wide(modcol, (l * 6 + 3) * KD * 2)))
                        (s0, a0, h0), (s1, a1, h1) = views
                        V.tensor_tensor(s0, s0, a0, ALU.mult)
                        exp_then(V.tensor_tensor(s1, s1, a1, ALU.mult), base + (half + 1))
                        V.tensor_tensor(s0, s0, h0, ALU.add)
                        V.tensor_tensor(s1, s1, h1, ALU.add).then_inc(xe_mod, 1)

                def rows_low(b, highs):
                    for half in range(2):
                        ks = slice(4 * half, 4 * half + 4)
                        dve.wait_ge(xe_high, highs + (half + 1))
                        low_part(xeT[1][:, b, ks, :], bank(6 + half, 0, 4 * CAP), xeT[0][:, b, ks, :], xe_ready)

                def y_half(half, e, i):
                    dve.wait_ge(ring_used, i * (2 * CH_EXP) + (chunk_no(l, CH_DENSE) + e * CH_EXP + (5 + half) * NQ))
                    return V.scalar_tensor_tensor(out=ybuf[0:CAP, e, half * NW:(half + 1) * NW], in0=bank(4 + half)[0:CAP, :],
                                                  scalar=gate_c[:, e:e + 1], in1=gate2_b[0:CAP, half * NW:(half + 1) * NW],
                                                  op0=ALU.mult, op1=ALU.mult)

                rows_mod(0, 2 * (NE + 1) * l, 2 * (NE + 1) * l)
                rows_low(0, 2 * (NE + 1) * l)
                g0 = chunk_no(l, CH_DENSE)
                with dve.Fori(0, NE // 2) as i:
                    for e in range(2):
                        n_exp = i * 2 + (NE * l + e)
                        n_prep = i * 2 + ((NE + 1) * l + e)
                        for j in range(CH_EXP):
                            g = g0 + e * CH_EXP + j
                            if j == 2:
                                dve.wait_ge(added, n_exp + BUF)
                                V.tensor_copy(gate_c[:, 1 - e:2 - e], gateT[:, bass.ds(i * 2 + (e + 1), 1)])
                                V.tensor_copy(idx_c[:, 1 - e, 0:1], idxT[:, bass.ds(i * 2 + (e + 1), 1)]).then_inc(idx_ready, 1)
                            if j == 2 * NQ + 1:
                                rows_mod(1 - e, n_prep * 2 + 2, n_prep * 2 + 2)
                            if j == 2 * NQ + 2:
                                rows_low(1 - e, n_prep * 2 + 2)
                            if j in (3 * NQ, 4 * NQ):
                                half = j // NQ - 3
                                dve.wait_ge(silu_ready, n_exp * 2 + (half + 1))
                                dve.wait_ge(ring_used, i * (2 * CH_EXP) + (g0 + e * CH_EXP + j))
                                V.tensor_tensor(hid[0:CAP, half * NW:(half + 1) * NW], sil[0:CAP, half, :], bank(2 + half)[0:CAP, :], ALU.mult).then_inc(hid_ready, 1)
                            if j == 4 * NQ:
                                for half in range(2):
                                    ks = slice(4 * half, 4 * half + 4)
                                    dve.wait_ge(hidT_high, n_exp * 2 + (half + 1))
                                    low_part(hidT[1][:, ks, :], bank(6 + half, 0, 4 * CAP), hidT[0][:, ks, :], hidT_low)
                            if j == 5 * NQ:
                                y_half(0, e, i)
                            if not by_pool(g + HIGH):
                                dve.wait_ge(high_done, i * (2 * CH_EXP) + (g + HIGH + 1))
                                V.tensor_tensor(low[:, (g + HIGH) % RING, :, :], ring[:, (g + HIGH) % RING, :, :],
                                                high[:, g % HIGH, :, :].bitcast(F32), ALU.subtract).then_inc(low_dve, 1)
                        y_half(1, e, i).then_inc(y_ready, 1)

            dve.wait_ge(gfin_in, 16)
            for m in range(T):
                dve.wait_ge(x_in[m], 16 * (2 * L + 1))
                stats(2 * L, m, last=True)

        @block.gpsimd
        def _(pool):
            G = nc.gpsimd
            steps = [0]

            def then(ins):
                steps[0] += 1
                ins.then_inc(pool_step, 1)
                pool.wait_ge(pool_step, steps[0])

            def rope_tile(X, cos, sin, tmp, heads, q):
                t = tmp.rearrange("p (h a j q) -> p h a j q", h=heads, a=2, j=2)
                for j in range(2):
                    s = sin.rearrange("p (o a j q) -> p o a j q", o=1, a=2, j=2)[:, :, :, j, :].broadcast_to([P, heads, 2, q])
                    then(G.tensor_tensor(t[:, :, :, j, :], X[:, :, :, 1 - j, :], s, ALU.mult))
                flat = X.rearrange("p h a j q -> p h (a j q)")
                cc = cos.rearrange("p (o n) -> p o n", o=1).broadcast_to([P, heads, 4 * q])
                then(G.tensor_tensor(flat, flat, cc, ALU.mult))
                return G.tensor_tensor(flat, flat, tmp.rearrange("p (h n) -> p h n", h=heads), ALU.add)

            pool.sem_inc(added, BUF)
            for b in range(2):
                pool.wait_ge(mod_out[b], 16 * (L * N_MOD // 2 + 1))
            pool.wait_ge(const_in, 16 * N_CONST)

            for l in range(L):
                q1, q2 = 2 * l, 2 * l + 1
                if l:
                    pool.wait_ge(y_out, 16 * NE * l)
                    pool.wait_ge(xe_tr, 2 * (NE + 1) * l)
                for m in range(T):
                    pool.dma_start(xt[:, m, :], tok_in(l, m)).then_inc(x_in[m], 16)

                for m in range(TS):
                    a, d = u_counts(l, 4 * T + m)
                    pool.wait_ge(u_act, a)
                    pool.wait_ge(u_dve, d)
                    for c0, heads, d4, t0 in ((AQ, 16, 8, 0), (CQ, 6, 16, 64)):
                        w = heads * 4 * d4
                        X = u[:, m, c0:c0 + w].rearrange("p (h a j q) -> p h a j q", h=heads, a=2, j=2)
                        ins = rope_tile(X, rope[:, m, t0:t0 + 4 * d4], rope[:, m, t0 + 4 * d4:t0 + 8 * d4], rtmp[:, 0:w], heads, d4)
                        if heads == 16:
                            then(ins)
                    ins.then_inc(rope_a, 1)
                    pool.wait_ge(rope_a, TS * l + m + 1)

                pool.wait_ge(u_act, 13 * (l + 1))
                pool.wait_ge(u_dve, 12 * (l + 1))
                pool.wait_ge(cn_ready, T * (l + 1))
                for dst, c0, h, n in ((new_diff_k, AK, HEADS, 64), (new_diff_v, AV, HEADS, 64), (new_na_k, BK, HEADS, 64),
                                      (new_na_v, BV, HEADS, 64), (new_swa_k, CK, 2, 64), (new_swa_v, CV, 2, 64)):
                    pool.dma_start(dst[0, l].rearrange("t h n -> t (h n)"), u[:, T - 1, c0:c0 + h * n]).then_inc(kv_out, 16)
                pool.dma_start(new_mla_ckv[0, l], u[:, T - 1, DCKV:DCKV + KVR]).then_inc(kv_out, 16)
                pool.dma_start(new_mla_kpe[0, l], u[:, T - 1, DKPE:DKPE + ROPE_D]).then_inc(kv_out, 16)

                pool.wait_ge(pad_ready, l + 1)
                pool.dma_start(rpb_dram[l], rpad[:, :]).then_inc(pad_out, 16)
                pool.wait_ge(pad_out, 16 * (l + 1))
                for b in range(2):
                    if b:
                        last = UNITS[LAST_UNIT[BLOCKS.index(("B", 0))]]["passes"][-1]
                        pool.wait_ge(s_max, N_PASS * l + last + 1)
                    for h in range(2):
                        for r in range(2):
                            off = ((l * HEADS + 2 * b + h) * 15 + 1 - r) * 127
                            src = bass.AP(rpb_dram.tensor, off, [[1, GRID_W], [127, 14], [1, GRID_W]])
                            pool.dma_start(na_tab[64 * r:64 * r + 64, h, :].rearrange("p (j n) -> p j n", n=GRID_W), src).then_inc(natab_in, 16)

                n = 0
                for q in range(NG_GATE * T):
                    j, m = divmod(q, T)
                    if j % 4 == 0:
                        continue
                    pool.wait_ge(g_mul, NG_GATE * T * l + q + 1)
                    if n >= T:
                        pool.wait_ge(g_add, 6 * T * l + n - T + 1)
                    dst = merged[:, m, (j // 4) * NW:(j // 4 + 1) * NW]
                    G.tensor_tensor(dst, dst, gtmp[:, q % 2, :], ALU.add).then_inc(g_add, 1)
                    n += 1

                pool.wait_ge(g_mul, NG_GATE * T * (l + 1))
                for g in range(2):
                    pool.dma_start(gate1_b[:, g, :], mod_dram[l, g:g + 1, 2 * D:3 * D].broadcast_to([P, D])).then_inc(gate1_in, 16)
                pool.dma_start(gate2_b[0:CAP_S, :], mod_dram[l, 1:2, 5 * D:6 * D].broadcast_to([CAP_S, D])).then_inc(gate2_in, 16)
                pool.dma_start(gate2_b[CAP_S:CAP, :], mod_dram[l, 0:1, 5 * D:6 * D].broadcast_to([CAP_P, D])).then_inc(gate2_in, 16)

                pool.wait_ge(mt_tr, 2 * T * (l + 1))
                for m in range(T):
                    pool.dma_start(xt[:, m, :], tok_in(l, m)).then_inc(x_in[m], 16)
                for m in range(T):
                    pool.wait_ge(x_new, T * l + m + 1)
                    pool.dma_start(x_dram[m * P:(m + 1) * P, :], xt[:, m, :]).then_inc(x_out, 16)
                    pool.wait_ge(xn_ready, T * q2 + m + 1)
                    pool.dma_start(xn_dram[m * P:(m + 1) * P, :], xn_att[:, m % 2, :]).then_inc(xn_out[m % 2], 16)

                pool.wait_ge(x_out, 16 * T * (l + 1))
                for b in range(2):
                    pool.wait_ge(xn_out[b], xn_store(l, 4 - b))

                def gather(b, ready):
                    pool.wait_ge(idx_ready, ready)
                    pool.sem_inc(pool_held, 1)
                    pool.indirect_dma_start(out=xe[0:CAP, b, :], out_offset=None, in_=xn_dram,
                                            in_offset=bass.IndirectOffsetOnAxis(ap=idx_c[:, b, 0:1], axis=0)).then_inc(xe_in[b], 16)

                def split_low(g, i=None):
                    n = g + 1 if i is None else i * (2 * CH_EXP) + (g + 1)
                    pool.wait_ge(high_done, n)
                    G.tensor_tensor(low[:, g % RING, :, :], ring[:, g % RING, :, :], high[:, g % HIGH, :, :].bitcast(F32),
                                    ALU.subtract).then_inc(low_pool, 1)

                split_low(chunk_no(l, CH_DENSE) + HIGH - 1)
                gather(0, (NE + 1) * l + 1)
                pool.wait_ge(gate2_in, 32 * (l + 1))
                with pool.Fori(0, NE // 2) as i:
                    for e in range(2):
                        n_exp = i * 2 + (NE * l + e)
                        for j in range(HIGH - 1, CH_EXP, 4):
                            g = chunk_no(l, CH_DENSE) + e * CH_EXP + j
                            split_low(g + HIGH, i)
                            if j == HIGH - 1:
                                gather(1 - e, i * 2 + ((NE + 1) * l + e + 2))
                        pool.wait_ge(y_ready, n_exp + 2)
                        pool.sem_inc(pool_held, 1)
                        pool.indirect_dma_start(out=x_dram, out_offset=bass.IndirectOffsetOnAxis(ap=idx_c[:, e, 0:1], axis=0),
                                                in_=ybuf[0:CAP, e, :], in_offset=None, compute_op=ALU.add).then_inc(y_out, 16)
                        pool.wait_ge(y_out, n_exp * 16 + 16)
                        pool.sem_inc(added, 1)

            pool.dma_start(gfin_b, g_final.rearrange("(a n) -> a n", a=1).broadcast_to([P, D])).then_inc(gfin_in, 16)
            pool.wait_ge(y_out, 16 * NE * L)
            pool.wait_ge(xe_tr, 2 * (NE + 1) * L)
            q = 2 * L
            for m in range(T):
                pool.dma_start(xt[:, m, :], tok_in(L, m)).then_inc(x_in[m], 16)
            for m in range(T):
                pool.wait_ge(xn_ready, T * q + m + 1)
                dst = y_sample[0, m * P:(m + 1) * P, :] if m < TS else y_prompt[0]
                pool.dma_start(dst, xn_of(q)[:, m % 2, :]).then_inc(y_done[m % 2], 16)
            pool.wait_ge(kv_out, 16 * N_KV * L)
            for b in range(2):
                pool.wait_ge(y_done[b], 16 * (3 - b))


_INS = ["x_prompt", "x_sample", "cache_diff_k", "cache_diff_v", "cache_na_k", "cache_na_v", "cache_swa_k",
        "cache_swa_v", "cache_mla_ckv", "cache_mla_kpe", "c", "c_ctx", "w_mod", "b_mod", "g_norm1", "g_norm2", "w_in",
        "da_lambda", "da_subln", "na_rpb", "sw_sink", "mla_q_norm", "mla_w_uq", "mla_kv_norm", "mla_w_ukv", "w_gate",
        "w_branch", "w_out", "w_router", "w_e_gate", "w_e_up", "w_e_down", "g_final"]
_OUTS = [(1, NP, D), (1, NS, D), (1, L, NP, 4, 64), (1, L, NP, 4, 64), (1, L, NP, 4, 64), (1, L, NP, 4, 64),
         (1, L, NP, 2, 64), (1, L, NP, 2, 64), (1, L, NP, KVR), (1, L, NP, ROPE_D)]


def position_tables():
    t = np.arange(NS)
    parts = []
    for d4 in (8, 16):
        f = np.float32(10000.0) ** (-np.arange(d4, dtype=np.float32) / np.float32(d4))
        cos, sin = [], []
        for pos in (t // GRID_W, t % GRID_W):
            ang = pos.astype(np.float32)[:, None] * f.astype(np.float32)
            cc, s = np.cos(ang), np.sin(ang)
            cos += [cc, cc]
            sin += [-s, s]
        parts += cos + sin
    rope = np.concatenate(parts, axis=1).astype(np.float32)
    qc, kc = np.arange(GRID_W)[:, None], np.arange(GRID_W)[None, :]
    start = np.clip(qc - 8, 0, GRID_W - 16)
    na = np.where((kc >= start) & (kc < start + 16), 0.0, NEG).astype(np.float32)
    q, k = np.arange(P)[:, None], np.arange(P)[None, :]
    sw = np.stack([np.where(k >= q, 0.0, NEG), np.where(k <= q, 0.0, NEG)], axis=1).astype(np.float32)
    return np.eye(P, dtype=np.float32), rope, np.ascontiguousarray(np.concatenate([na, na], axis=0)[:, ::-1]), sw


def kernel(**inputs):
    import concourse.bacc as _bacc
    from concourse.bass_utils import run_bass_kernel_spmd as _run

    nc = _bacc.Bacc("TRN2", target_bir_lowering=False, num_devices=1)
    arrays, args = {}, []
    given = [(n, np.ascontiguousarray(inputs[n])) for n in _INS]
    given += list(zip(["k_ident", "k_rope", "k_mask_na", "k_mask_sw"], position_tables()))
    for name, a in given:
        arrays[f"in_{name}"] = a
        args.append(nc.dram_tensor(f"in_{name}", a.shape, mybir.dt.from_np(a.dtype), kind="ExternalInput").ap())
    for i, shape in enumerate(_OUTS):
        args.append(nc.dram_tensor(f"out_{i}", shape, F32, kind="ExternalOutput").ap())
    hybrid_step(nc, *args)
    r = _run(nc, [arrays], core_ids=[0])
    return tuple(r.results[0][f"out_{i}"] for i in range(len(_OUTS)))
```

```python
import math
from contextlib import ExitStack

import numpy as np
import concourse.bass as bass
from concourse import mybir

F32 = mybir.dt.float32
F32R = mybir.dt.float32r
U32 = mybir.dt.uint32
ALU = mybir.AluOpType
ACT = mybir.ActivationFunctionType
AX = mybir.AxisListType

D, L, P = 1024, 2, 128
NS, NP = 512, 128
T = (NS + NP) // P
TS = NS // P
KD = D // P
GRID_W, HEADS, HD, DQK = 64, 4, 64, 32
NOPE, ROPE_D = 64, 32
DM_ = NOPE + ROPE_D
QR, KVR = 256, 128
NE, DE, CAP_S, CAP_P = 16, 1024, 64, 16
CAP = CAP_S + CAP_P
EPS = 1e-6
IN_DIM = 2464
AQ, AK, AV, BQ, BK, BV, CQ, CK, CV, DCQ, DCKV, DKPE = (
    0, 256, 512, 768, 1024, 1280, 1536, 1792, 1920, 2048, 2304, 2432)
DRQ = DKPE - NOPE
NEG = -1e30
LAM_INIT = [0.8 - 0.6 * math.exp(-0.3 * l) for l in range(L)]
NW = 512
KC = 2
NQ = KD // KC
RING = 8
HIGH = 4
WIN_N = [512, 512, 512, 512, IN_DIM - 2048]
N_MOD = 6 * D // NW
NG_IN, NG_GATE = 5, 8
CH_MOD = NQ * N_MOD * L
CH_IN, CH_GATE = NQ * NG_IN, (NQ + 1) * NG_GATE
CH_DENSE = CH_IN + CH_GATE + 2 * NQ
CH_EXP = 6 * NQ
CH_GATE0 = 2 * NQ
LOOPED = NE // 2 - 1
CH_LAYER = CH_DENSE + NE * CH_EXP
N_CHUNKS = CH_MOD + L * CH_LAYER
SIG = 6

O_COL = {"A": AQ, "B": BQ, "C": CQ, "D": DCQ}
O_BLOCKS = [AQ, AQ + 128, BQ, BQ + 128, CQ, CQ + 128, DCQ, DCQ + 128]
BLOCKS = [("D", 0), ("D", 1), ("D", 2), ("D", 3), ("A", 0), ("B", 0), ("A", 1), ("B", 1), ("C", 0), ("C", 1)]


def plan_units():
    units, passes = [], 0
    for bi, (br, b) in enumerate(BLOCKS):
        for hh in range(1 if br == "D" else 2):
            for m in range(T):
                head = b if br == "D" else 2 * b + hh
                if m == T - 1:
                    kb = [5]
                elif br == "C":
                    kb = [0] + [1 + j for j in range(max(m - 1, 0), min(m + 2, TS))]
                else:
                    kb = [0, 1, 2, 3, 4]
                n = 2 if br == "A" else 1
                if br == "D":
                    rows = [(0, DM_)]
                elif br == "A":
                    rows = [(64 * hh, 32), (64 * hh + 32, 32)]
                else:
                    rows = [(64 * hh, 64)]
                units.append(dict(bi=bi, br=br, b=b, hh=hh, m=m, head=head, kb=kb, rows=rows,
                                  passes=list(range(passes, passes + n))))
                passes += n
    return units, passes


UNITS, N_PASS = plan_units()
N_UNIT = len(UNITS)
UNIT_OF = {p: i for i, u in enumerate(UNITS) for p in u["passes"]}
FIRST_UNIT = {bi: min(i for i, u in enumerate(UNITS) if u["bi"] == bi) for bi in range(len(BLOCKS))}
LAST_UNIT = {bi: max(i for i, u in enumerate(UNITS) if u["bi"] == bi) for bi in range(len(BLOCKS))}
SCALE = {"A": DQK ** -0.5, "B": HD ** -0.5, "C": HD ** -0.5, "D": DM_ ** -0.5}
PREP_AT = {}
for _bi in range(1, len(BLOCKS)):
    for _g in range(4):
        PREP_AT.setdefault(FIRST_UNIT[_bi - 1] + 1 + _g, []).append((_bi, _g))
A_UNITS = [i for i, u in enumerate(UNITS) if u["br"] == "A"]
B_UNITS = [i for i, u in enumerate(UNITS) if u["br"] == "B"]
N_C = sum(1 for u in UNITS if u["br"] == "C")
C_BEFORE = [sum(1 for u in UNITS[:i] if u["br"] == "C") for i in range(N_UNIT + 1)]
ADDS = [sum(1 for r in range(q) if r // T % 4) for q in range(8 * T + 1)]
A_BEFORE = [sum(1 for a in A_UNITS if a < i) for i in range(N_UNIT + 1)]
TAIL_BEFORE = [sum(1 for u in UNITS[:i] if len(u["kb"]) > 4) for i in range(N_UNIT + 1)]


def segments(u):
    out, col = [], 0
    runs = [(0, 1)] if u["kb"][0] == 0 else []
    rest = [k for k in u["kb"] if k]
    runs.append((rest[0], len(rest)))
    for k0, n in runs:
        a, w = k0 * P, n * P
        while w:
            s = min(w, NW - col % NW)
            out.append((col, a, s))
            col, a, w = col + s, a + s, w - s
    return out


def chunk_no(l, c):
    return CH_MOD + l * CH_LAYER + c


def width_of(g):
    c = (g - CH_MOD) % CH_LAYER
    return WIN_N[-1] if CH_MOD <= g < N_CHUNKS and CH_IN - NQ <= c < CH_IN else NW


def by_pool(g):
    l, c = divmod(g - CH_MOD, CH_LAYER)
    return g >= CH_MOD and g % 4 == 3 and (c >= CH_DENSE or (c < HIGH and l > 0))


LOW_POOL = [sum(map(by_pool, range(g + 1))) for g in range(N_CHUNKS + HIGH)]
LOW_DVE = [g + 1 - LOW_POOL[g] for g in range(N_CHUNKS + HIGH)]


def hybrid_step(nc, x_prompt, x_sample, cache_diff_k, cache_diff_v, cache_na_k, cache_na_v, cache_swa_k,
                cache_swa_v, cache_mla_ckv, cache_mla_kpe, c, c_ctx, w_mod, b_mod, g_norm1, g_norm2, w_in,
                da_lambda, da_subln, na_rpb, sw_sink, mla_q_norm, mla_w_uq, mla_kv_norm, mla_w_ukv, w_gate,
                w_branch, w_out, w_router, w_e_gate, w_e_up, w_e_down, g_final,
                k_ident, k_rope, k_mask_na, k_mask_sw,
                y_prompt, y_sample, new_diff_k, new_diff_v, new_na_k, new_na_v, new_swa_k, new_swa_v,
                new_mla_ckv, new_mla_kpe):
    ctx = ExitStack()
    with ctx:
        def sb(name, shape, dt=F32):
            return ctx.enter_context(nc.sbuf_tensor(name, shape, dt))

        def sem(name):
            return ctx.enter_context(nc.semaphore(name))

        x_dram = nc.dram_tensor("x_resid", (T * P, D), F32, kind="Internal").ap()
        xn_dram = nc.dram_tensor("x_normed", (T * P, D), F32, kind="Internal").ap()
        mod_dram = nc.dram_tensor("mod_rows", (L, 2, 6 * D), F32, kind="Internal").ap()
        rpb_dram = nc.dram_tensor("rpb_padded", (L, HEADS * 15, 127), F32, kind="Internal").ap()

        def over(name, shape, base, first):
            return nc.alloc_sbuf_tensor_at(name, shape, F32R, offset=(base + 31) // 32 * 32 + 4 * first)

        ring_at = nc.sbuf_base
        ring = sb("ring", [P, RING, KC, NW])
        low = over("low", [P, RING, KC, NW], ring_at, 0)
        high = sb("high", [P, HIGH, KC, NW], F32R)
        hT = [sb("hT_high", [P, KD, T * P], F32R), sb("hT_low", [P, KD, T * P], F32R)]
        WORK_N = T * IN_DIM
        work_at = nc.sbuf_base
        work = sb("work", [P, WORK_N])
        ATT_N = 2 * KD * T * P
        att_at = nc.sbuf_base
        att = sb("att", [P, ATT_N])
        u = work[:, :].rearrange("p (m n) -> p m n", m=T)
        merged = work[:, 0:T * D].rearrange("p (m n) -> p m n", m=T)
        mergedT = [over("mergedT_high", [P, KD, T * P], work_at, 5120), over("mergedT_low", [P, KD, T * P], att_at, 0)]
        sig = work[:, 5120:5120 + SIG * NW].rearrange("p (b n) -> p b n", b=SIG)
        gtmp = work[:, 11264:12288].rearrange("p (b n) -> p b n", b=2)
        xt = work[:, 0:T * D].rearrange("p (b n) -> p b n", b=T)
        xn_work = work[:, 5120:7168].rearrange("p (b n) -> p b n", b=2)
        xn_att = att[:, 8192:10240].rearrange("p (b n) -> p b n", b=2)
        sq = work[:, 10240:11264]
        xe = work[:, 0:2048].rearrange("p (b n) -> p b n", b=2)
        xeT = [over("xeT_high", [P, 2, KD, CAP], work_at, 2048), over("xeT_low", [P, 2, KD, CAP], work_at, 3328)]
        hid = work[:, 4608:5632]
        sil = work[:, 5632:6656].rearrange("p (b n) -> p b n", b=2)
        hidT = [over("hidT_high", [P, KD, CAP], work_at, 6656), over("hidT_low", [P, KD, CAP], work_at, 7296)]
        ybuf = work[:, 7936:9984].rearrange("p (b n) -> p b n", b=2)
        affT = work[0:NE, 10240:10240 + T * P]
        qT = att[:, 0:1280].rearrange("p (b n) -> p b n", b=2)
        kT = att[:, 1280:2816].rearrange("p (b n) -> p b n", b=2)
        prob = att[:, 2816:5376].rearrange("p (b n) -> p b n", b=4)
        cqT = att[:, 2816:4096].rearrange("p (b n) -> p b n", b=2)
        probT = att[:, 5376:6656].rearrange("p (b n) -> p b n", b=2)
        sqs = att[:, 5376:5632]
        na_tab = att[:, 6656:8448].rearrange("p (h n) -> p h n", h=2)
        c_ka, c_va, c_kb, c_vb = (att[:, 8448 + 256 * i:8704 + 256 * i] for i in range(4))
        c_kc, c_vc, c_ckv = (att[:, 9472 + 128 * i:9600 + 128 * i] for i in range(3))
        c_kpe = att[:, 9856:9952]
        oT = [over("oT_high", [P, KD, T * P], att_at, 0), over("oT_low", [P, KD, T * P], att_at, 5120)]
        gate1_b = att[:, 5120:7168].rearrange("p (g n) -> p g n", g=2)
        gate2_b = att[:, 7168:8192]
        gfin_b = att[:, 8192:9216]

        ckvT = sb("ckvT", [P, 6 * P])
        vmla = sb("vmla", [P, 6, 256])
        mask_sw = sb("mask_sw", [P, 2, P])
        mask_na = sb("mask_na", [P, GRID_W])
        rope = sb("rope", [P, TS, 192])
        ident = sb("ident", [P, P])
        w_uq = sb("w_uq", [P, 2, HEADS * DM_])
        w_ukv = sb("w_ukv", [P, 512])
        w_r = sb("w_r", [P, KD, NE])
        w_r2 = [sb("w_r_high", [P, KD, NE], F32R), sb("w_r_low", [P, KD, NE], F32R)]
        qn_b = sb("qn_b", [P, QR])
        kvn_b = sb("kvn_b", [P, KVR])
        lam_b = sb("lam_b", [P, 128])
        sub_b = sb("sub_b", [P, HD])
        sink_b = sb("sink_b", [P, HEADS])
        rtmp = sb("rtmp", [P, 512])
        rtmp2 = sb("rtmp2", [P, 128])
        rpad = sb("rpad", [HEADS * 15, 127])
        rraw = sb("rraw", [HEADS * 15, 31])
        modcol_all = sb("modcol", [P, 8 + L * 6 * KD * 2])
        modcol = modcol_all[:, 8:]
        amod = sb("amod", [P, L * 2 * KD * 2])
        gn_col = sb("gn_col", [P, L * 2, KD])
        cT = sb("cT", [P, 2, KD])
        csf = sb("csf", [P, KD, 2])
        csT = [sb("csT_high", [P, KD, 2], F32R), sb("csT_low", [P, KD, 2], F32R)]
        bm = work[0:2, 10240:11264].rearrange("p (b n) -> p b n", b=2)
        modrow = work[0:2, 11264:12288].rearrange("p (b n) -> p b n", b=2)
        st = sb("st", [P, 160])
        ss, var, sd, rstd = st[:, 0:5], st[:, 5:10], st[:, 10:15], st[:, 15:20]
        s10, v10, r10 = st[:, 20:30], st[:, 30:40], st[:, 40:50]
        s20, v20, r20 = st[:, 50:70], st[:, 70:90], st[:, 90:110]
        mx, negm, sm = st[:, 110:118], st[:, 118:126], st[:, 126:134]
        rinv, cmap, es = st[:, 134:142], st[:, 142:146], st[:, 154:158]
        lam, neglam = st[:, 148:150], st[:, 150:151]
        lg = sb("lg", [P, T, NE])
        lgs = sb("lgs", [P, 2, T])
        top_v = sb("top_v", [NE, CAP])
        top_i = sb("top_i", [NE, CAP], U32)
        top_f = sb("top_f", [NE, CAP])
        gateT = sb("gateT", [CAP, NE])
        idxT = sb("idxT", [CAP, NE], U32)
        gate_c = sb("gate_c", [CAP, 2])
        idx_s = sb("idx_s", [CAP, 2, 2], U32)
        idx_g = sb("idx_g", [CAP, 2, 2], U32)
        ps = [ctx.enter_context(nc.psum_tensor(f"bank{i}", [P, 1024], F32)) for i in range(4)]

        def bank(i, a=0, b=NW):
            return ps[i // 2][:, NW * (i % 2) + a:NW * (i % 2) + b]

        const_in = sem("const_in")
        ring_full = [sem(f"ring_full{i}") for i in range(RING)]
        ring_used = sem("ring_used")
        high_done, low_dve, low_pool = sem("high_done"), sem("low_dve"), sem("low_pool")
        small_in = sem("small_in")
        bm_full = [sem(f"bm_full{i}") for i in range(2)]
        cs_ready = sem("cs_ready")
        mod_row, mod_tr, mod_col = sem("mod_row"), sem("mod_tr"), sem("mod_col")
        mod_out = [sem(f"mod_out{i}") for i in range(2)]
        amod_ready = sem("amod_ready")
        x_in = [sem(f"x_in{i}") for i in range(T)]
        mod_done = sem("mod_done")
        var_ready, sd_ready, xn_ready = sem("var_ready"), sem("sd_ready"), sem("xn_ready")
        norm_tr, norm_high, norm_low = sem("norm_tr"), sem("norm_high"), sem("norm_low")
        u_full, u_act, u_dve = sem("u_full"), sem("u_act"), sem("u_dve")
        c_var, c_sd, cn_ready = sem("c_var"), sem("c_sd"), sem("cn_ready")
        kpe_ready = sem("kpe_ready")
        rope_a = sem("rope_a")
        kv_out = sem("kv_out")
        x_out = sem("x_out")
        xn_out, y_done = ([sem(f"{n}{i}") for i in range(2)] for n in ("xn_out", "y_done"))
        ct_tr, ct_ev = sem("ct_tr"), sem("ct_ev")
        qm_full, qm_ready = sem("qm_full"), sem("qm_ready")
        vm_full, vm_ev = sem("vm_full"), sem("vm_ev")
        lam_z, lam_e, lam_ready = sem("lam_z"), sem("lam_e"), sem("lam_ready")
        prep_tr, prep_ev = sem("prep_tr"), sem("prep_ev")
        s_full, s_max, p_ready, w_ready = sem("s_full"), sem("s_max"), sem("p_ready"), sem("w_ready")
        es_ready = sem("es_ready")
        t_full, t_act, t_dve = sem("t_full"), sem("t_act"), sem("t_dve")
        o_full, o_ev = sem("o_full"), sem("o_ev")
        pad_ready, pad_out, rpb_in = sem("pad_ready"), sem("pad_out"), sem("rpb_in")
        natab_in, natab_ready = sem("natab_in"), sem("natab_ready")
        on_var, on_sd, on_ready = sem("on_var"), sem("on_sd"), sem("on_ready")
        ot_tr, ot_high, ot_low = sem("ot_tr"), sem("ot_high"), sem("ot_low")
        gate_full, b_full = sem("gate_full"), sem("b_full")
        g_sig, g_mul, g_add = sem("g_sig"), sem("g_mul"), sem("g_add")
        mt_tr, mt_high, mt_low = sem("mt_tr"), sem("mt_high"), sem("mt_low")
        wo_full, wo_half, x_new = sem("wo_full"), sem("wo_half"), sem("x_new")
        gate1_in, gate2_in, gfin_in = sem("gate1_in"), sem("gate2_in"), sem("gfin_in")
        lg_full, lg_sub, lg_exp, aff_ready = sem("lg_full"), sem("lg_sub"), sem("lg_exp"), sem("aff_ready")
        affT_tr, top_ready, topT_tr, topT_ready = sem("affT_tr"), sem("top_ready"), sem("topT_tr"), sem("topT_ready")
        idx_ready, gate_set = sem("idx_ready"), sem("gate_set")
        xe_in = [sem(f"xe_in{i}") for i in range(2)]
        xe_tr, xe_mod, xe_high, xe_ready = sem("xe_tr"), sem("xe_mod"), sem("xe_high"), sem("xe_ready")
        wr_high, wr_ready = sem("wr_high"), sem("wr_ready")
        silu_ready, hid_ready = sem("silu_ready"), sem("hid_ready")
        hid_tr, hidT_high, hidT_low = sem("hid_tr"), sem("hidT_high"), sem("hidT_low")
        y_ready, y_out, added = sem("y_ready"), sem("y_out"), sem("added")
        pe_held, pool_held = sem("pe_held"), sem("pool_held")
        dve_step, pool_step, exp_step = sem("dve_step"), sem("pool_step"), sem("exp_step")

        N_CONST = 6 + 2 * L
        N_SMALL = 18
        N_KV = 8
        BUF = 2

        def tok_in(l, m):
            if l == 0:
                return x_sample[0, m * P:(m + 1) * P, :] if m < TS else x_prompt[0]
            return x_dram[m * P:(m + 1) * P, :]

        def xn_of(q):
            return xn_att if q % 2 and q < 2 * L else xn_work

        def xn_store(l, m):
            return 16 * ((3 if m % 2 == 0 else 2) * l + m // 2 + 1)

        def w_chunk(w, n0, width, kq):
            return w.rearrange("(k p) n -> p k n", p=P)[:, kq * KC:(kq + 1) * KC, n0:n0 + width]

        def three(out, lhs, rhs_high, rhs_low, start, stop):
            nc.tensor.matmul(out, lhs[0], rhs_high, start=start, stop=False)
            nc.tensor.matmul(out, lhs[0], rhs_low, start=False, stop=False)
            return nc.tensor.matmul(out, lhs[1], rhs_high, start=False, stop=stop)

        def u_counts(l, g):
            return 13 * l + g // 2 + 1, 12 * l + (g + 1) // 2

        def k_src(br, b, kb):
            if br == "A":
                return c_ka[:, 128 * b:128 * b + 128] if kb == 0 else u[:, kb - 1, AK + 128 * b:AK + 128 * b + 128]
            if br == "B":
                return c_kb[:, 128 * b:128 * b + 128] if kb == 0 else u[:, kb - 1, BK + 128 * b:BK + 128 * b + 128]
            return c_kc[:, :] if kb == 0 else u[:, kb - 1, CK:CK + 128]

        def v_src(un, kb):
            h = un["head"]
            if un["br"] == "D":
                return vmla[:, kb, 64 * h:64 * h + 64]
            if un["br"] == "C":
                h = h // 2
            cv, off = {"A": (c_va, AV), "B": (c_vb, BV), "C": (c_vc, CV)}[un["br"]]
            return cv[:, 64 * h:64 * h + 64] if kb == 0 else u[:, kb - 1, off + 64 * h:off + 64 * h + 64]

        def gain_col(l, w, k, m):
            a = ((l * 2 + w) * KD + k) * 2 + (1 if m < TS else 0)
            return amod[:, a:a + 1]

        def shift_col(l, w, k, m):
            a = ((l * 6 + 3 * w) * KD + k) * 2 + (1 if m < TS else 0)
            return modcol[:, a:a + 1]

        block = ctx.enter_context(nc.Block())

        @block.sync
        def _(sp):
            sp.dma_start(ident[:, :], k_ident).then_inc(const_in, 16)
            with nc.allow_non_contiguous_dma("columns of small vectors"):
                sp.dma_start(cT[:, 0, :], c_ctx.rearrange("(k p) -> p k", p=P)).then_inc(const_in, 16)
                sp.dma_start(cT[:, 1, :], c[0].rearrange("(k p) -> p k", p=P)).then_inc(const_in, 16)
                for w, g in ((0, g_norm1), (1, g_norm2)):
                    for l in range(L):
                        sp.dma_start(gn_col[:, 2 * l + w, :], g[l].rearrange("(k p) -> p k", p=P)).then_inc(const_in, 16)
            sp.dma_start(rope[:, :, :], k_rope.rearrange("(m p) n -> p m n", p=P)).then_inc(const_in, 16)
            sp.dma_start(mask_na[:, :], k_mask_na).then_inc(const_in, 16)
            sp.dma_start(mask_sw[:, :, :], k_mask_sw).then_inc(const_in, 16)

            def fill(slot, src, used, width=NW):
                if used is not None:
                    sp.wait_ge(ring_used, used)
                sp.dma_start(ring[:, slot, :, 0:width], src).then_inc(ring_full[slot], 16)

            for l in range(L):
                w3 = w_mod[l].rearrange("(k p) n -> p k n", p=P)
                if l == 0:
                    for j in range(RING):
                        fill(j, w_chunk(w_mod[0], j // NQ * NW, NW, j % NQ), None)
                with sp.Fori(1 if l == 0 else 0, N_MOD // 2) as i:
                    for j in range(2 * NQ):
                        fill(j, w3[:, (j % NQ) * KC:(j % NQ + 1) * KC, bass.ds((i * 2 + j // NQ) * NW, NW)],
                             i * (2 * NQ) + (l * NQ * N_MOD + j - RING + 1))
            for l in range(L):
                if l:
                    sp.wait_ge(ot_tr, 2 * T * l)
                    sp.wait_ge(lg_full, l)
                    sp.wait_ge(on_ready, T * l)
                row = lambda a: a.rearrange("(a n) -> a n", a=1)
                small = [
                    (qn_b[:, :], row(mla_q_norm[l]).broadcast_to([P, QR])),
                    (kvn_b[:, :], row(mla_kv_norm[l]).broadcast_to([P, KVR])),
                    (lam_b[:, :], da_lambda[l].rearrange("a n -> (a n)").rearrange("(a n) -> a n", a=1).broadcast_to([P, 128])),
                    (sub_b[:, :], row(da_subln[l]).broadcast_to([P, HD])),
                    (sink_b[:, :], row(sw_sink[l]).broadcast_to([P, HEADS])),
                    (w_uq[:, :, :], mla_w_uq[l].rearrange("(k p) n -> p k n", p=P)),
                    (w_ukv[:, :], mla_w_ukv[l]),
                    (w_r[:, :, :], w_router[l].rearrange("(k p) n -> p k n", p=P)),
                    (rraw[:, :], na_rpb[l].rearrange("h a b -> (h a) b")),
                ]
                for dst, src in small:
                    sp.dma_start(dst, src).then_inc(small_in, 16)
                if l:
                    sp.wait_ge(xe_tr, 2 * NE * (l - 1) + 2)
                for dst, src in [
                    (c_ka, cache_diff_k[0, l].rearrange("t h n -> t (h n)")),
                    (c_va, cache_diff_v[0, l].rearrange("t h n -> t (h n)")),
                    (c_kb, cache_na_k[0, l].rearrange("t h n -> t (h n)")),
                    (c_vb, cache_na_v[0, l].rearrange("t h n -> t (h n)")),
                    (c_kc, cache_swa_k[0, l].rearrange("t h n -> t (h n)")),
                    (c_vc, cache_swa_v[0, l].rearrange("t h n -> t (h n)")),
                    (c_ckv, cache_mla_ckv[0, l]),
                    (c_kpe[:, 0:64], cache_mla_ckv[0, l][:, 0:64]),
                    (c_kpe[:, 64:96], cache_mla_kpe[0, l]),
                ]:
                    sp.dma_start(dst, src).then_inc(small_in, 16)
                n = 0

                def cache_out():
                    sp.wait_ge(u_act, 13 * (l + 1))
                    sp.wait_ge(u_dve, 12 * (l + 1))
                    sp.wait_ge(cn_ready, T * (l + 1))
                    for dst, src in [(new_mla_ckv[0, l], u[:, T - 1, DCKV:DCKV + KVR]), (new_mla_kpe[0, l], u[:, T - 1, DKPE:DKPE + ROPE_D])] + [
                            (dst[0, l].rearrange("t h n -> t (h n)"), u[:, T - 1, c0:c0 + h * 64])
                            for dst, c0, h in ((new_diff_k, AK, HEADS), (new_diff_v, AV, HEADS), (new_na_k, BK, HEADS),
                                               (new_na_v, BV, HEADS), (new_swa_k, CK, 2), (new_swa_v, CV, 2))]:
                        sp.dma_start(dst, src).then_inc(kv_out, 16)

                def dense(w, n0, width=NW, chunks=NQ):
                    nonlocal n
                    for kq in range(chunks):
                        if n == CH_IN + RING:
                            cache_out()
                        g = chunk_no(l, n)
                        fill(g % RING, w_chunk(w, n0, width, kq), g - RING + 1, width)
                        n += 1

                for j in range(NG_IN):
                    dense(w_in[l], j * NW, WIN_N[j])
                for j in range(NG_GATE):
                    half, br = j // 4, j % 4
                    dense(w_gate[l], br * D + half * NW)
                    dense(w_branch[l, br], half * NW, chunks=1)
                for j in range(2):
                    dense(w_out[l], j * NW)
                g0 = chunk_no(l, CH_DENSE)

                def matrix(w, n, g, i):
                    for c in range(2 * NQ):
                        half, kq = divmod(c, NQ)
                        src = w[l].rearrange("e (k p) n -> p e k n", p=P)[
                            :, bass.ds(n, 1), kq * KC:(kq + 1) * KC, half * NW:(half + 1) * NW]
                        fill((g + c) % RING, src.rearrange("p e k n -> p (e k) n"), i * (2 * CH_EXP) + (g + c - RING + 1))

                def expert(e, i, last=False):
                    g = g0 + CH_GATE0 + e * CH_EXP
                    matrix(w_e_up, i * 2 + e, g, i)
                    if not last:
                        matrix(w_e_gate, i * 2 + (e + 1), g + 2 * NQ, i)
                    matrix(w_e_down, i * 2 + e, g + (2 if last else 4) * NQ, i)

                matrix(w_e_gate, 0, g0, 0)
                with sp.Fori(0, LOOPED) as i:
                    expert(0, i)
                    expert(1, i)
                expert(0, LOOPED)
                expert(1, LOOPED, last=True)
            for j in range(HIGH):
                g = N_CHUNKS + j
                fill(g % RING, w_chunk(w_e_down[L - 1, NE - 1], 0, NW, j), g - RING + 1)

        @block.tensor
        def _(pe):
            mm, tr = nc.tensor.matmul, nc.tensor.transpose

            def split_done(g, i=None):
                s, n = (low_pool, LOW_POOL[g]) if by_pool(g) else (low_dve, LOW_DVE[g])
                if i is None:
                    pe.wait_ge(s, n)
                else:
                    pe.wait_ge(s, i * (2 * CH_EXP // 4 * (1 if by_pool(g) else 3)) + n)

            def turn4(dst, src, done):
                for k in range(4):
                    ins = tr(dst(k), src(k), ident[:, :])
                ins.then_inc(done, 1)

            pe.wait_ge(const_in, 16 * N_CONST)
            pe.wait_ge(cs_ready, 4)
            pe.sem_inc(mod_tr, BUF - 1)

            def cols(j, row):
                pe.wait_ge(mod_row, row + BUF)
                pe.wait_ge(mod_col, row + (BUF - 1))
                pe.sem_inc(pe_held, 1)
                for b in range(4):
                    ins = tr(bank(2 + j, 2 * b, 2 * b + 2), modrow[:, j, b * P:(b + 1) * P], ident[0:2, 0:2])
                ins.then_inc(mod_tr, 1)

            for l in range(L):
                with pe.Fori(0, N_MOD // 2) as i:
                    def rows(j):
                        for kq in range(NQ):
                            c = NQ * j + kq
                            pe.wait_ge(low_dve, i * (2 * NQ) + (l * NQ * N_MOD + c + 1))
                            for k in range(KC):
                                kk = kq * KC + k
                                ins = three(bank(j)[0:2, :], [t[:, kk, :] for t in csT], high[:, c % HIGH, k, :], low[:, c % RING, k, :],
                                            kk == 0, kk == KD - 1)
                            ins.then_inc(ring_used, 1)

                    for j in range(2):
                        rows(j)
                        cols(1 - j, i * 2 + (l * N_MOD + j))
            cols(1, L * N_MOD)
            pe.wait_ge(mod_col, L * N_MOD + 1 + BUF)

            for l in range(L):
                q1, q2 = 2 * l, 2 * l + 1

                def norm_turn(q, m, banks):
                    t = T * q + m
                    pe.wait_ge(xn_ready, t + 1)
                    if m >= 2:
                        pe.wait_ge(norm_low, 2 * (t - 1))
                    for half in range(2):
                        b = banks + 2 * (m % 2) + half
                        turn4(lambda k: bank(b, k * P, (k + 1) * P),
                              lambda k: xn_of(q)[:, m % 2, (4 * half + k) * P:(4 * half + k + 1) * P], norm_tr)

                if l:
                    pe.wait_ge(y_ready, NE * l + 1)
                    pe.wait_ge(xe_ready, 2 * NE * l)
                def w_in_part(n, m, kq):
                    q, g = T * n + m, chunk_no(l, NQ * n + kq)
                    for k in range(KC):
                        kk = kq * KC + k
                        ins = three(bank(q % 8, 0, WIN_N[n]), [t[:, kk, m * P:(m + 1) * P] for t in hT],
                                    high[:, g % HIGH, k, 0:WIN_N[n]], low[:, g % RING, k, 0:WIN_N[n]], kk == 0, kk == KD - 1)
                    if kq == NQ - 1 and m < T - 1:
                        ins.then_inc(u_full, 1)
                    if m == T - 1:
                        ins.then_inc(ring_used, 1)

                norm_turn(q1, 0, 4)
                for m in range(T):
                    if m < T - 1:
                        norm_turn(q1, m + 1, 4)
                    pe.wait_ge(norm_low, 2 * (T * q1 + m + 1))
                    for kq in range(NQ):
                        if m == 0:
                            split_done(chunk_no(l, kq))
                        w_in_part(0, m, kq)
                for n in range(1, NG_IN):
                    for kq in range(NQ):
                        split_done(chunk_no(l, NQ * n + kq))
                        for m in range(T):
                            q = T * n + m
                            if kq == 0 and q >= 8:
                                a, d = u_counts(l, q - 8)
                                pe.wait_ge(u_act, a)
                                pe.wait_ge(u_dve, d)
                            w_in_part(n, m, kq)

                pe.wait_ge(u_act, 13 * (l + 1))
                pe.wait_ge(u_dve, 12 * (l + 1))
                for m in range(T + 1):
                    if m < T:
                        pe.wait_ge(cn_ready, T * l + m + 1)
                        pe.wait_ge(kpe_ready, TS * l + min(m + 1, TS))
                    else:
                        pe.wait_ge(small_in, 16 * N_SMALL * (l + 1))
                    if m >= 4:
                        pe.wait_ge(ct_ev, 6 * l + m - 3)
                    b = m % 4
                    tr(bank(b, 2 * P, 3 * P), u[:, m, DCKV:DCKV + P] if m < T else c_ckv, ident[:, :])
                    if m < T:
                        for k in range(2):
                            tr(bank(b, k * P, (k + 1) * P), u[:, m, DCQ + k * P:DCQ + (k + 1) * P], ident[:, :])
                    tr(bank(b, 3 * P, 4 * P)[0:DM_, :], u[:, m, DRQ:DRQ + DM_] if m < T else c_kpe, ident[:, :]).then_inc(ct_tr, 1)
                for m in range(T):
                    pe.wait_ge(ct_ev, 6 * l + m + 1)
                    if m >= 4:
                        pe.wait_ge(qm_ready, T * l + m - 3)
                    for k in range(2):
                        ins = mm(bank(4 + m % 4, 0, HEADS * DM_), cqT[:, k, m * P:(m + 1) * P], w_uq[:, k, :], start=(k == 0), stop=(k == 1))
                    ins.then_inc(qm_full, 1)
                pe.wait_ge(ct_ev, 6 * l + 6)
                for kb in range(6):
                    ins = mm(bank(kb // 2, 256 * (kb % 2), 256 * (kb % 2) + 256), ckvT[:, kb * P:(kb + 1) * P],
                             w_ukv[:, :].rearrange("p (h n) -> p h n", h=HEADS)[:, :, NOPE:NOPE + HD], start=True, stop=True)
                    if kb % 2:
                        ins.then_inc(vm_full, 1)

                def prep(bi, g):
                    br, b = BLOCKS[bi]
                    if 4 * bi + g:
                        pe.wait_ge(prep_ev, 4 * len(BLOCKS) * l + 4 * bi + g)
                    if bi == 0 and g == 0:
                        pe.wait_ge(qm_ready, T * (l + 1))
                        pe.wait_ge(vm_ev, 3 * (l + 1))
                    if br in "AC" and g == 0:
                        pe.wait_ge(rope_a, TS * (l + 1))
                    if g < 2:
                        for i, m in enumerate(range(4) if g == 0 else [4]):
                            if br == "D":
                                src, n = u[:, m, DCQ + DM_ * b:DCQ + DM_ * (b + 1)], DM_
                            else:
                                src, n = u[:, m, O_COL[br] + P * b:O_COL[br] + P * (b + 1)], P
                            ins = tr(bank(7, i * P, (i + 1) * P)[0:n, :], src, ident[:, :])
                    elif br == "D":
                        a, e = (0, 512) if g == 2 else (512, 768)
                        ins = mm(bank(7, 0, e - a)[0:NOPE, :], w_ukv[:, 128 * b:128 * b + NOPE], ckvT[:, a:e], start=True, stop=True)
                    else:
                        for i, kb in enumerate(range(4) if g == 2 else [4, 5]):
                            ins = tr(bank(7, i * P, (i + 1) * P), k_src(br, b, kb), ident[:, :])
                    ins.then_inc(prep_tr, 1)

                def scores(ui):
                    un = UNITS[ui]
                    if ui == FIRST_UNIT[un["bi"]]:
                        pe.wait_ge(prep_ev, 4 * len(BLOCKS) * l + 4 * (un["bi"] + 1))
                    for (r0, rn), p in zip(un["rows"], un["passes"]):
                        if p >= 2:
                            pe.wait_ge(p_ready, N_PASS * l + p - 1)
                        b = un["bi"] % 2
                        for col, a, w in segments(un):
                            ins = mm(ps[p % 2][:, col:col + w], qT[r0:r0 + rn, b, un["m"] * P:(un["m"] + 1) * P],
                                     kT[r0:r0 + rn, b, a:a + w], start=True, stop=True)
                        ins.then_inc(s_full, 1)

                def turn(ui):
                    un = UNITS[ui]
                    if un["br"] == "A":
                        pe.wait_ge(w_ready, len(A_UNITS) * l + A_BEFORE[ui] + 1)
                    else:
                        pe.wait_ge(p_ready, N_PASS * l + un["passes"][0] + 1)
                    if ui:
                        pe.wait_ge(t_act, N_UNIT * l + ui)
                        pe.wait_ge(t_dve, TAIL_BEFORE[N_UNIT] * l + TAIL_BEFORE[ui])
                    for i in range(len(un["kb"])):
                        ins = tr(ps[2][:, i * P:(i + 1) * P], prob[:, un["passes"][0] % 4, i * P:(i + 1) * P], ident[:, :])
                    ins.then_inc(t_full, 1)

                def values(ui):
                    un = UNITS[ui]
                    pe.wait_ge(t_act, N_UNIT * l + ui + 1)
                    pe.wait_ge(t_dve, TAIL_BEFORE[N_UNIT] * l + TAIL_BEFORE[ui + 1])
                    if ui:
                        pe.wait_ge(o_ev, N_UNIT * l + ui)
                    for i, kb in enumerate(un["kb"]):
                        ins = mm(bank(6, 0, HD), probT[:, ui % 2, i * P:(i + 1) * P], v_src(un, kb),
                                 start=(i == 0), stop=(i == len(un["kb"]) - 1))
                    ins.then_inc(o_full, 1)

                for g in range(4):
                    prep(0, g)
                for ui in range(N_UNIT + 2):
                    if ui < N_UNIT:
                        scores(ui)
                    if 1 <= ui <= N_UNIT:
                        turn(ui - 1)
                    if ui >= 2:
                        values(ui - 2)
                    for bi, g in PREP_AT.get(ui, []):
                        prep(bi, g)

                pe.wait_ge(o_ev, N_UNIT * (l + 1))
                for m in range(T):
                    pe.wait_ge(on_ready, T * l + m + 1)
                    if m >= 2:
                        pe.wait_ge(ot_low, 2 * (T * l + m - 1))
                    for half in range(2):
                        turn4(lambda k: bank(2 * (m % 2) + half, k * P, (k + 1) * P),
                              lambda k: u[:, m, O_BLOCKS[4 * half + k]:O_BLOCKS[4 * half + k] + P], ot_tr)
                pe.wait_ge(ot_low, 2 * T * (l + 1))

                for j in range(NG_GATE):
                    for kq in range(NQ + 1):
                        g = chunk_no(l, CH_IN + (NQ + 1) * j + kq)
                        split_done(g)
                        for m in range(T):
                            q = T * j + m
                            if kq == 0 and q >= SIG:
                                pe.wait_ge(g_sig, NG_GATE * T * l + q - SIG + 1)
                            if kq == NQ and q >= 2:
                                pe.wait_ge(g_mul, NG_GATE * T * l + q - 1)
                            for k in range(KC):
                                kk = kq * KC + k
                                if kq < NQ:
                                    ins = three(bank(q % SIG), [t[:, kk, m * P:(m + 1) * P] for t in hT],
                                                high[:, g % HIGH, k, :], low[:, g % RING, k, :], kk == 0, kk == KD - 1)
                                else:
                                    ins = three(bank(6 + q % 2), [t[:, KC * (j % 4) + k, m * P:(m + 1) * P] for t in oT],
                                                high[:, g % HIGH, k, :], low[:, g % RING, k, :], k == 0, k == KC - 1)
                            if m < T - 1 and kq == NQ - 1:
                                ins.then_inc(gate_full, 1)
                            if m < T - 1 and kq == NQ:
                                ins.then_inc(b_full, 1)
                        ins.then_inc(ring_used, 1)

                pe.wait_ge(g_mul, NG_GATE * T * (l + 1))
                for m in range(T):
                    pe.wait_ge(g_add, 6 * T * l + 5 * T + m + 1)
                    if m >= 2:
                        pe.wait_ge(mt_low, 2 * (T * l + m - 1))
                    for half in range(2):
                        turn4(lambda k: bank(4 + 2 * (m % 2) + half, k * P, (k + 1) * P),
                              lambda k: merged[:, m, (4 * half + k) * P:(4 * half + k + 1) * P], mt_tr)

                def w_out_part(half, m, kq):
                    g = chunk_no(l, CH_DENSE - 2 * NQ + NQ * half + kq)
                    for k in range(KC):
                        kk = kq * KC + k
                        ins = three(bank((T * half + m) % 8), [t[:, kk, m * P:(m + 1) * P] for t in mergedT],
                                    high[:, g % HIGH, k, :], low[:, g % RING, k, :], kk == 0, kk == KD - 1)
                    if kq == NQ - 1 and m < T - 1:
                        ins.then_inc(wo_full, 1)
                    if m == T - 1:
                        ins.then_inc(ring_used, 1)

                for kq in range(NQ):
                    split_done(chunk_no(l, CH_DENSE - 2 * NQ + kq))
                    for m in range(T):
                        if kq == 0:
                            pe.wait_ge(mt_low, 2 * (T * l + m + 1))
                            if m == 4:
                                pe.wait_ge(mt_low, 2 * T * (l + 1))
                        w_out_part(0, m, kq)
                for m in range(T):
                    if T + m >= 8:
                        pe.wait_ge(wo_half, T * l + T + m - 7)
                    for kq in range(NQ):
                        if m == 0:
                            split_done(chunk_no(l, CH_DENSE - NQ + kq))
                        w_out_part(1, m, kq)
                pe.wait_ge(wo_half, T * (l + 1))
                pe.wait_ge(wr_ready, l + 1)
                for m in range(T + 1):
                    if m < T:
                        norm_turn(q2, m, 2)
                    if m >= 1:
                        pe.wait_ge(norm_low, 2 * (T * q2 + m))
                        for k in range(KD):
                            ins = three(bank(6, NE * (m - 1), NE * m), [t[:, k, (m - 1) * P:m * P] for t in hT],
                                        w_r2[0][:, k, :], w_r2[1][:, k, :], k == 0, k == KD - 1)
                ins.then_inc(lg_full, 1)

                pe.wait_ge(aff_ready, l + 1)
                for m in range(T):
                    ins = tr(bank(1 + m // 4, (m % 4) * P, (m % 4 + 1) * P)[0:NE, :], lg[:, m, :], ident[:, :])
                ins.then_inc(affT_tr, 1)
                pe.wait_ge(top_ready, l + 1)
                tr(bank(3, 0, NE)[0:CAP, :], top_v[:, :], ident[0:NE, 0:NE])
                tr(bank(3, NE, 2 * NE)[0:CAP, :], top_f[:, :], ident[0:NE, 0:NE]).then_inc(topT_tr, 1)

                def rows_turn(b, fills):
                    pe.wait_ge(xe_in[b], fills)
                    for half in range(2):
                        for k in range(4):
                            kk = 4 * half + k
                            ins = tr(bank(6 + half, k * CAP, (k + 1) * CAP), xe[0:CAP, b, kk * P:(kk + 1) * P], ident[0:CAP, 0:CAP])
                        ins.then_inc(xe_tr, 1)

                pe.wait_ge(topT_ready, l + 1)
                rows_turn(0, 16 * (NE // 2 * l + 1))
                g0 = chunk_no(l, CH_DENSE)

                def matrix(g, i, first, stat, before=()):
                    for c in range(2 * NQ):
                        for at, step in before:
                            if at == c:
                                step()
                        split_done(g + c, i)
                        for k in range(KC):
                            kk = (c % NQ) * KC + k
                            ins = three(bank(first + c // NQ)[0:CAP, :], stat(kk), high[:, (g + c) % HIGH, k, :],
                                        low[:, (g + c) % RING, k, :], kk == 0, kk == KD - 1)
                        ins.then_inc(ring_used, 1)

                def expert(e, i, last=False):
                    g = g0 + CH_GATE0 + e * CH_EXP
                    n_exp = i * 2 + (NE * l + e)

                    def turn_next():
                        rows_turn(1 - e, i * 16 + 16 * (NE // 2 * l + (1 if e == 0 else 2)))

                    def turn_hid():
                        for half in range(2):
                            pe.wait_ge(hid_ready, n_exp * 2 + (half + 1 + BUF))
                            for k in range(4):
                                kk = 4 * half + k
                                ins = tr(bank(6 + half, k * CAP, (k + 1) * CAP), hid[0:CAP, kk * P:(kk + 1) * P], ident[0:CAP, 0:CAP])
                            ins.then_inc(hid_tr, 1)

                    def silu_read(half):
                        return lambda: pe.wait_ge(silu_ready, n_exp * 2 + (half + 1))

                    def hid_in(half):
                        return lambda: pe.wait_ge(hidT_low, n_exp * 2 + (half + 1))

                    rows_of = lambda b: lambda kk: [t[:, b, kk, :] for t in xeT]
                    matrix(g, i, 2, rows_of(e), [] if last else [(2, turn_next)])
                    if not last:
                        pe.wait_ge(xe_ready, n_exp * 2 + 4)
                        matrix(g + 2 * NQ, i, 0, rows_of(1 - e), [(0, silu_read(0)), (NQ, silu_read(1)), (NQ, turn_hid)])
                    else:
                        turn_hid()
                    pe.wait_ge(y_ready, n_exp + 1)
                    matrix(g + (2 if last else 4) * NQ, i, 4, lambda kk: [t[:, kk, :] for t in hidT], [(0, hid_in(0)), (2, hid_in(1))])

                pe.wait_ge(xe_ready, 2 * NE * l + 2)
                matrix(g0, 0, 0, lambda kk: [t[:, 0, kk, :] for t in xeT])
                with pe.Fori(0, LOOPED) as i:
                    expert(0, i)
                    expert(1, i)
                expert(0, LOOPED)
                expert(1, LOOPED, last=True)

        @block.scalar
        def _(act):
            A = nc.scalar.activation

            def split_high(g, i=None):
                if i is None:
                    act.wait_ge(ring_full[g % RING], 16 * (g // RING + 1))
                    if g >= HIGH:
                        act.wait_ge(ring_used, g - HIGH + 1)
                else:
                    act.wait_ge(ring_full[g % RING], i * (16 * 2 * CH_EXP // RING) + 16 * (g // RING + 1))
                    act.wait_ge(ring_used, i * (2 * CH_EXP) + (g - HIGH + 1))
                w = width_of(g)
                A(high[:, g % HIGH, :, 0:w], ring[:, g % RING, :, 0:w], ACT.Copy).then_inc(high_done, 1)

            def high_part(dst, src, done):
                return A(dst, src.rearrange("p (k n) -> p k n", k=4), ACT.Copy).then_inc(done, 1)

            act.wait_ge(const_in, 16 * N_CONST)
            for b in range(2):
                act.sem_inc(mod_out[b], 16)
            for g in range(2):
                A(csf[:, :, g], cT[:, g, :], ACT.Silu).then_inc(cs_ready, 1)
            act.wait_ge(cs_ready, 2)
            A(csT[0][:, :, :], csf[:, :, :], ACT.Copy).then_inc(cs_ready, 1)
            for g in range(HIGH):
                split_high(g)
            for l in range(L):
                with act.Fori(0, N_MOD // 2) as i:
                    for j in range(2):
                        act.wait_ge(mod_row, i * 2 + (l * N_MOD + j - 1 + BUF))
                        act.dma_start(bm[:, j, :], b_mod[l:l + 1, bass.ds((i * 2 + j) * NW, NW)].broadcast_to([2, NW])).then_inc(bm_full[j], 16)
                        for kq in range(NQ):
                            g = l * NQ * N_MOD + NQ * j + kq + HIGH
                            act.wait_ge(ring_full[g % RING], i * 16 + 16 * (g // RING + 1))
                            act.wait_ge(ring_used, i * (2 * NQ) + (g - HIGH + 1))
                            A(high[:, g % HIGH, :, :], ring[:, g % RING, :, :], ACT.Copy).then_inc(high_done, 1)
                        act.wait_ge(mod_row, i * 2 + (l * N_MOD + j + 1 + BUF))
                        act.dma_start(mod_dram[l][:, bass.ds((i * 2 + j) * NW, NW)], modrow[:, j, :]).then_inc(mod_out[j], 16)
            act.wait_ge(amod_ready, 2 * L)

            for l in range(L):
                q1, q2 = 2 * l, 2 * l + 1

                def std(q, m):
                    t = T * q + m
                    act.wait_ge(var_ready, t + 1)
                    A(sd[:, m:m + 1], var[:, m:m + 1], ACT.Sqrt).then_inc(sd_ready, 1)

                def modulate(q, m, banks):
                    t = T * q + m
                    for half in range(2):
                        act.wait_ge(norm_tr, 2 * t + half + 1)
                        b = banks + 2 * (m % 2) + half
                        for k in range(4):
                            kk = 4 * half + k
                            ins = A(bank(b, k * P, (k + 1) * P), bank(b, k * P, (k + 1) * P), ACT.Identity,
                                    bias=shift_col(l, q % 2, kk, m), scale=gain_col(l, q % 2, kk, m))
                        ins.then_inc(mod_done, 1)
                        act.wait_ge(mod_done, 2 * t + half + 1)
                        high_part(hT[0][:, 4 * half:4 * half + 4, m * P:(m + 1) * P], bank(b), norm_high)

                std(q1, 0)
                for m in range(T):
                    if m + 1 < T:
                        std(q1, m + 1)
                    modulate(q1, m, 4)

                for n in range(NG_IN):
                    for kq in range(NQ):
                        g = chunk_no(l, NQ * n + kq)
                        if kq == NQ - 1:
                            for m in range(T):
                                q = T * n + m
                                if q % 2 == 0:
                                    if m < T - 1:
                                        act.wait_ge(u_full, (T - 1) * (NG_IN * l + n) + m + 1)
                                    else:
                                        act.wait_ge(ring_used, g + 1)
                                    A(u[:, m, n * NW:n * NW + WIN_N[n]], bank(q % 8, 0, WIN_N[n]), ACT.Copy).then_inc(u_act, 1)
                        split_high(g + HIGH)

                act.wait_ge(c_var, l + 1)
                A(r10, v10, ACT.Sqrt).then_inc(c_sd, 1)
                for m in range(T + 1):
                    act.wait_ge(ct_tr, 6 * l + m + 1)
                    b = m % 4
                    at = (m + 1) * P if m < T else 0
                    if m < T:
                        A(cqT[:, :, m * P:(m + 1) * P], bank(b, 0, 2 * P).rearrange("p (k n) -> p k n", k=2), ACT.Copy)
                    A(ckvT[:, at:at + P], bank(b, 2 * P, 3 * P), ACT.Copy)
                    for z in range(2):
                        ins = A(kT[NOPE:DM_, z, at:at + P], bank(b, 3 * P, 4 * P)[NOPE:DM_, :], ACT.Copy)
                    ins.then_inc(ct_ev, 1)
                for z in range(3):
                    act.wait_ge(vm_full, 3 * l + z + 1)
                    A(vmla[:, 2 * z:2 * z + 2, :], bank(z).rearrange("p (k n) -> p k n", k=2), ACT.Copy).then_inc(vm_ev, 1)
                act.wait_ge(lam_z, l + 1)
                A(lam, lam, ACT.Exp).then_inc(lam_e, 1)

                def prep_out(bi, g):
                    br, b = BLOCKS[bi]
                    z = bi % 2
                    act.wait_ge(prep_tr, 4 * len(BLOCKS) * l + 4 * bi + g + 1)
                    a, e = ((0, 512), (512, 640), (0, 512), (512, 768))[g]
                    n = e - a
                    if g < 2:
                        r = DM_ if br == "D" else P
                        ins = A(qT[0:r, z, a:e], bank(7, 0, n)[0:r, :], ACT.Copy)
                    elif br == "C":
                        A(kT[0:64, z, a:e], bank(7, 0, n)[64 * b:64 * b + 64, :], ACT.Copy)
                        ins = A(kT[64:128, z, a:e], bank(7, 0, n)[64 * b:64 * b + 64, :], ACT.Copy)
                    else:
                        r = NOPE if br == "D" else P
                        ins = A(kT[0:r, z, a:e], bank(7, 0, n)[0:r, :], ACT.Copy)
                    ins.then_inc(prep_ev, 1)

                for g in range(4):
                    prep_out(0, g)
                for ui in range(N_UNIT + 2):
                    if ui < N_UNIT:
                        un = UNITS[ui]
                        w = len(un["kb"]) * P
                        for p in un["passes"]:
                            act.wait_ge(s_max, N_PASS * l + p + 1)
                            if p >= 4:
                                act.wait_ge(t_full, N_UNIT * l + UNIT_OF[p - 4] + 1)
                            A(prob[:, p % 4, 0:w], ps[p % 2][:, 0:w], ACT.Exp, bias=negm[:, p % 8:p % 8 + 1],
                              scale=SCALE[un["br"]], accum_out=sm[:, p % 8:p % 8 + 1]).then_inc(p_ready, 1)
                        if un["br"] == "C":
                            p, h = un["passes"][0], un["head"]
                            A(es[:, ui % 4:ui % 4 + 1], sink_b[:, h:h + 1], ACT.Exp, bias=negm[:, p % 8:p % 8 + 1],
                              scale=SCALE["C"]).then_inc(es_ready, 1)
                    if 1 <= ui <= N_UNIT:
                        v = ui - 1
                        w = min(len(UNITS[v]["kb"]), 4) * P
                        act.wait_ge(t_full, N_UNIT * l + v + 1)
                        if v >= 2:
                            act.wait_ge(o_full, N_UNIT * l + v - 1)
                        A(probT[:, v % 2, 0:w], ps[2][:, 0:w], ACT.Copy).then_inc(t_act, 1)
                    for bi, g in PREP_AT.get(ui, []):
                        prep_out(bi, g)

                act.wait_ge(on_var, l + 1)
                A(r20, v20, ACT.Sqrt).then_inc(on_sd, 1)
                for m in range(T):
                    for half in range(2):
                        act.wait_ge(ot_tr, 2 * (T * l + m) + half + 1)
                        high_part(oT[0][:, 4 * half:4 * half + 4, m * P:(m + 1) * P], bank(2 * (m % 2) + half), ot_high)

                for j in range(NG_GATE):
                    for kq in range(NQ + 1):
                        g = chunk_no(l, CH_IN + (NQ + 1) * j + kq)
                        if kq == NQ - 1:
                            for m in range(T):
                                q = T * j + m
                                if m < T - 1:
                                    act.wait_ge(gate_full, (T - 1) * (NG_GATE * l + j) + m + 1)
                                else:
                                    act.wait_ge(ring_used, g + 1)
                                if q >= SIG:
                                    act.wait_ge(g_mul, NG_GATE * T * l + q - SIG + 1)
                                A(sig[:, q % SIG, :], bank(q % SIG), ACT.Sigmoid).then_inc(g_sig, 1)
                        split_high(g + HIGH)
                for m in range(T):
                    for half in range(2):
                        act.wait_ge(mt_tr, 2 * (T * l + m) + half + 1)
                        high_part(mergedT[0][:, 4 * half:4 * half + 4, m * P:(m + 1) * P], bank(4 + 2 * (m % 2) + half), mt_high)
                A(w_r2[0][:, :, :], w_r[:, :, :], ACT.Copy).then_inc(wr_high, 1)

                for c in range(CH_DENSE - 2 * NQ, CH_DENSE - NQ):
                    split_high(chunk_no(l, c) + HIGH)

                std(q2, 0)
                for m in range(T):
                    if m + 1 < T:
                        std(q2, m + 1)
                    modulate(q2, m, 2)
                for c in range(CH_DENSE - NQ, CH_DENSE):
                    split_high(chunk_no(l, c) + HIGH)

                act.wait_ge(lg_sub, l + 1)
                A(lg[:, :, :], lg[:, :, :], ACT.Exp).then_inc(lg_exp, 1)

                g0 = chunk_no(l, CH_DENSE)

                def rows_high(b, mods):
                    for half in range(2):
                        act.wait_ge(xe_mod, mods + (half + 1))
                        high_part(xeT[0][:, b, 4 * half:4 * half + 4, :], bank(6 + half, 0, 4 * CAP), xe_high)

                def silu(half, n, used):
                    act.wait_ge(ring_used, used)
                    act.wait_ge(hid_ready, n * 2 + BUF)
                    A(sil[0:CAP, half, :], bank(half)[0:CAP, :], ACT.Silu).then_inc(silu_ready, 1)

                def expert(e, i, last=False):
                    n_exp = i * 2 + (NE * l + e)
                    for j in range((4 if last else 6) * NQ):
                        g = g0 + CH_GATE0 + e * CH_EXP + j
                        if j == 4 and not last:
                            rows_high(1 - e, n_exp * 2 + 2)
                        if j in (3 * NQ, 4 * NQ) and not last:
                            silu(j // NQ - 3, n_exp + 1, i * (2 * CH_EXP) + g)
                        if j == (2 * NQ if last else 3 * NQ + 1):
                            for half in range(2):
                                act.wait_ge(hid_tr, n_exp * 2 + (half + 1))
                                high_part(hidT[0][:, 4 * half:4 * half + 4, :], bank(6 + half, 0, 4 * CAP), hidT_high)
                        split_high(g + HIGH, i)

                rows_high(0, 2 * NE * l)
                for j in range(CH_GATE0):
                    if j == NQ:
                        silu(0, NE * l, g0 + NQ)
                    split_high(g0 + j + HIGH)
                silu(1, NE * l, g0 + CH_GATE0)
                with act.Fori(0, LOOPED) as i:
                    expert(0, i)
                    expert(1, i)
                expert(0, LOOPED)
                expert(1, LOOPED, last=True)

            for m in range(T):
                act.wait_ge(var_ready, T * 2 * L + m + 1)
                A(sd[:, m:m + 1], var[:, m:m + 1], ACT.Sqrt).then_inc(sd_ready, 1)

        @block.vector
        def _(dve):
            V = nc.vector
            steps = [0]

            def then(ins):
                steps[0] += 1
                ins.then_inc(dve_step, 1)
                dve.wait_ge(dve_step, steps[0])

            def split_low(g):
                if by_pool(g):
                    return
                dve.wait_ge(high_done, g + 1)
                w = width_of(g)
                V.tensor_tensor(low[:, g % RING, :, 0:w], ring[:, g % RING, :, 0:w], high[:, g % HIGH, :, 0:w].bitcast(F32),
                                ALU.subtract).then_inc(low_dve, 1)

            def low_part(dst, src, top, done):
                V.tensor_tensor(dst, src.rearrange("p (k n) -> p k n", k=4), top.bitcast(F32), ALU.subtract).then_inc(done, 1)

            def backwards(ap):
                dims = [list(d) for d in ap.ap]
                step, n = dims[-1]
                return bass.AP(ap.tensor, ap.offset + step * (n - 1), dims[:-1] + [[-step, n]])

            def rope_tile(X, cos, sin, tmp, heads, q):
                t = tmp.rearrange("p (h a j q) -> p h a j q", h=heads, a=2, j=2)
                for j in range(2):
                    s = sin.rearrange("p (o a j q) -> p o a j q", o=1, a=2, j=2)[:, :, :, j, :].broadcast_to([P, heads, 2, q])
                    then(V.tensor_tensor(t[:, :, :, j, :], X[:, :, :, 1 - j, :], s, ALU.mult))
                flat = X.rearrange("p h a j q -> p h (a j q)")
                cc = cos.rearrange("p (o n) -> p o n", o=1).broadcast_to([P, heads, 4 * q])
                then(V.tensor_tensor(flat, flat, cc, ALU.mult))
                return V.tensor_tensor(flat, flat, tmp.rearrange("p (h n) -> p h n", h=heads), ALU.add)

            then(V.memset(rpad[:, :], 0.0))
            dve.wait_ge(const_in, 16 * N_CONST)
            then(V.memset(modrow[:, 1, :], 0.0))
            dve.sem_inc(mod_row, BUF)
            dve.sem_inc(mod_col, BUF)
            dve.sem_inc(hid_ready, BUF)
            dve.sem_inc(y_ready, 1)
            dve.wait_ge(cs_ready, 3)
            V.tensor_tensor(csT[1][:, :, :], csf[:, :, :], csT[0][:, :, :].bitcast(F32), ALU.subtract).then_inc(cs_ready, 1)
            for g in range(HIGH):
                split_low(g)
            for l in range(L):
                with dve.Fori(0, N_MOD // 2) as i:
                    for j in range(2):
                        q0 = l * N_MOD + j
                        for kq in range(NQ):
                            g = l * NQ * N_MOD + NQ * j + kq + HIGH
                            dve.wait_ge(high_done, i * (2 * NQ) + (g + 1))
                            V.tensor_tensor(low[:, g % RING, :, :], ring[:, g % RING, :, :], high[:, g % HIGH, :, :].bitcast(F32),
                                            ALU.subtract).then_inc(low_dve, 1)
                        dve.wait_ge(ring_used, i * (2 * NQ) + (NQ * q0 + NQ))
                        dve.wait_ge(bm_full[j], i * 16 + 16 * (l * (N_MOD // 2) + 1))
                        dve.wait_ge(mod_tr, i * 2 + (q0 - 1 + BUF))
                        dve.wait_ge(mod_out[j], i * 16 + 16 * (l * (N_MOD // 2) + 1))
                        V.tensor_tensor(modrow[:, j, :], bank(j)[0:2, :], bm[:, j, :], ALU.add).then_inc(mod_row, 1)
                        dve.wait_ge(mod_tr, i * 2 + (q0 + BUF))
                        V.tensor_copy(modcol_all[:, bass.ds(i * 16 + q0 * 8, 8)], bank(3 - j, 0, 8)).then_inc(mod_col, 1)
            dve.wait_ge(mod_tr, L * N_MOD + BUF)
            V.tensor_copy(modcol[:, (L * N_MOD - 1) * 8:L * N_MOD * 8], bank(3, 0, 8)).then_inc(mod_col, 1)
            dve.wait_ge(mod_col, L * N_MOD + 1 + BUF)
            for l in range(L):
                for w in range(2):
                    a = (l * 6 + 1 + 3 * w) * KD * 2
                    V.scalar_tensor_tensor(
                        out=amod[:, (l * 2 + w) * KD * 2:(l * 2 + w + 1) * KD * 2].rearrange("p (k g) -> p k g", g=2),
                        in0=modcol[:, a:a + KD * 2].rearrange("p (k g) -> p k g", g=2), scalar=1.0,
                        in1=gn_col[:, l * 2 + w, :].rearrange("p (k o) -> p k o", o=1).broadcast_to([P, KD, 2]),
                        op0=ALU.add, op1=ALU.mult).then_inc(amod_ready, 1)
            dve.wait_ge(amod_ready, 2 * L)

            def stats(q, m, last=False):
                t = T * q + m
                then(V.tensor_tensor_reduce(sq, xt[:, m, :], xt[:, m, :], 1.0, 0.0, ALU.mult, ALU.add, ss[:, m:m + 1]))
                V.tensor_scalar(var[:, m:m + 1], ss[:, m:m + 1], 1.0 / D, EPS, ALU.mult, ALU.add).then_inc(var_ready, 1)
                dve.wait_ge(sd_ready, t + 1)
                then(V.reciprocal(rstd[:, m:m + 1], sd[:, m:m + 1]))
                if m >= 2 and not last:
                    dve.wait_ge(norm_tr, 2 * (t - 1))
                    if q % 2:
                        dve.wait_ge(xn_out[m % 2], xn_store(q // 2, m) - 16)
                if last:
                    if m >= 2:
                        dve.wait_ge(y_done[m % 2], 16 * (m // 2))
                    V.scalar_tensor_tensor(out=xn_of(q)[:, m % 2, :], in0=xt[:, m, :], scalar=rstd[:, m:m + 1], in1=gfin_b,
                                           op0=ALU.mult, op1=ALU.mult).then_inc(xn_ready, 1)
                else:
                    V.tensor_scalar(xn_of(q)[:, m % 2, :], xt[:, m, :], rstd[:, m:m + 1], None, ALU.mult).then_inc(xn_ready, 1)

            def norm_lows(q, m, banks):
                t = T * q + m
                for half in range(2):
                    ks = slice(4 * half, 4 * half + 4)
                    dve.wait_ge(norm_high, 2 * t + half + 1)
                    low_part(hT[1][:, ks, m * P:(m + 1) * P], bank(banks + 2 * (m % 2) + half), hT[0][:, ks, m * P:(m + 1) * P], norm_low)

            for l in range(L):
                q1, q2 = 2 * l, 2 * l + 1
                for m in range(T + 1):
                    if m < T:
                        dve.wait_ge(x_in[m], 16 * (q1 + 1))
                        stats(q1, m)
                    if m >= 1:
                        norm_lows(q1, m - 1, 4)

                for n in range(NG_IN):
                    for kq in range(NQ):
                        g = chunk_no(l, NQ * n + kq)
                        if kq == NQ - 1:
                            for m in range(T):
                                q = T * n + m
                                if q % 2:
                                    if m < T - 1:
                                        dve.wait_ge(u_full, (T - 1) * (NG_IN * l + n) + m + 1)
                                    else:
                                        dve.wait_ge(ring_used, g + 1)
                                    V.tensor_copy(u[:, m, n * NW:n * NW + WIN_N[n]], bank(q % 8, 0, WIN_N[n])).then_inc(u_dve, 1)
                        split_low(g + HIGH)

                dve.wait_ge(small_in, 16 * N_SMALL * (l + 1))
                for m in range(T):
                    a, d = u_counts(l, 4 * T + m)
                    dve.wait_ge(u_act, a)
                    dve.wait_ge(u_dve, d)
                    then(V.tensor_tensor_reduce(sqs, u[:, m, DCQ:DCQ + QR], u[:, m, DCQ:DCQ + QR], 1.0, 0.0, ALU.mult, ALU.add, s10[:, 2 * m:2 * m + 1]))
                    then(V.tensor_tensor_reduce(sqs[:, 0:KVR], u[:, m, DCKV:DCKV + KVR], u[:, m, DCKV:DCKV + KVR], 1.0, 0.0, ALU.mult, ALU.add, s10[:, 2 * m + 1:2 * m + 2]))
                then(V.tensor_scalar(v10[:, 0:10:2], s10[:, 0:10:2], 1.0 / QR, EPS, ALU.mult, ALU.add))
                V.tensor_scalar(v10[:, 1:10:2], s10[:, 1:10:2], 1.0 / KVR, EPS, ALU.mult, ALU.add).then_inc(c_var, 1)
                for m in range(TS):
                    X = u[:, m, DKPE:DKPE + 32].rearrange("p (h a j q) -> p h a j q", h=1, a=2, j=2)
                    rope_tile(X, rope[:, m, 0:32], rope[:, m, 32:64], rtmp2[:, 0:32], 1, 8).then_inc(kpe_ready, 1)
                    dve.wait_ge(kpe_ready, TS * l + m + 1)
                dve.wait_ge(c_sd, l + 1)
                then(V.reciprocal(r10, r10))
                for m in range(T):
                    V.scalar_tensor_tensor(out=u[:, m, DCQ:DCQ + QR], in0=u[:, m, DCQ:DCQ + QR], scalar=r10[:, 2 * m:2 * m + 1],
                                           in1=qn_b[:, :], op0=ALU.mult, op1=ALU.mult)
                    V.scalar_tensor_tensor(out=u[:, m, DCKV:DCKV + KVR], in0=u[:, m, DCKV:DCKV + KVR], scalar=r10[:, 2 * m + 1:2 * m + 2],
                                           in1=kvn_b[:, :], op0=ALU.mult, op1=ALU.mult).then_inc(cn_ready, 1)

                then(V.tensor_tensor_reduce(rtmp2[:, 0:32], lam_b[:, 0:32], lam_b[:, 32:64], 1.0, 0.0, ALU.mult, ALU.add, lam[:, 0:1]))
                V.tensor_tensor_reduce(rtmp2[:, 32:64], lam_b[:, 64:96], lam_b[:, 96:128], 1.0, 0.0, ALU.mult, ALU.add, lam[:, 1:2]).then_inc(lam_z, 1)
                then(V.tensor_scalar(sub_b[:, :], sub_b[:, :], 1.0 - LAM_INIT[l], None, ALU.mult))
                then(V.tensor_scalar(sink_b[:, :], sink_b[:, :], 1.0 / SCALE["C"], None, ALU.mult))
                if l:
                    dve.wait_ge(pad_out, 16 * l)
                V.tensor_scalar(rpad[:, 48:79], backwards(rraw[:, :]), 1.0 / SCALE["B"], None, ALU.mult).then_inc(pad_ready, 1)

                for m in range(T):
                    dve.wait_ge(qm_full, T * l + m + 1)
                    if m == T - 1:
                        dve.wait_ge(kv_out, 16 * N_KV * (l + 1))
                    src = bank(4 + m % 4, 0, HEADS * DM_)
                    dst = u[:, m, DCQ:DCQ + HEADS * DM_]
                    if m == T - 1:
                        V.tensor_copy(dst, src).then_inc(qm_ready, 1)
                        continue
                    then(V.tensor_copy(dst, src))
                    X = dst.rearrange("p (h n) -> p h n", h=HEADS)[:, :, NOPE:DM_].rearrange("p h (a j q) -> p h a j q", a=2, j=2)
                    rope_tile(X, rope[:, m, 0:32], rope[:, m, 32:64], rtmp2[:, 0:128], HEADS, 8).then_inc(qm_ready, 1)
                    dve.wait_ge(qm_ready, T * l + m + 1)
                dve.wait_ge(lam_e, l + 1)
                then(V.tensor_tensor(neglam, lam[:, 1:2], lam[:, 0:1], ALU.subtract))
                then(V.tensor_scalar(neglam, neglam, LAM_INIT[l], None, ALU.subtract))

                def combine(v):
                    w = len(UNITS[v]["kb"]) * P
                    p1, p2 = UNITS[v]["passes"]
                    dve.wait_ge(p_ready, N_PASS * l + p2 + 1)
                    then(V.reciprocal(cmap[:, v % 4:v % 4 + 1], sm[:, p2 % 8:p2 % 8 + 1]))
                    then(V.scalar_tensor_tensor(out=cmap[:, v % 4:v % 4 + 1], in0=cmap[:, v % 4:v % 4 + 1], scalar=neglam,
                                                in1=sm[:, p1 % 8:p1 % 8 + 1], op0=ALU.mult, op1=ALU.mult))
                    V.scalar_tensor_tensor(out=prob[:, p1 % 4, 0:w], in0=prob[:, p2 % 4, 0:w], scalar=cmap[:, v % 4:v % 4 + 1],
                                           in1=prob[:, p1 % 4, 0:w], op0=ALU.mult, op1=ALU.add).then_inc(w_ready, 1)

                for ui in range(N_UNIT + 2):
                    if ui < N_UNIT:
                        un = UNITS[ui]
                        br, m, w = un["br"], un["m"], len(un["kb"]) * P
                        if br == "B" and ui == FIRST_UNIT[un["bi"]]:
                            dve.wait_ge(natab_in, 64 * (2 * l + un["b"] + 1))
                            for h in range(2):
                                tab = na_tab[:, h, :].rearrange("p (j n) -> p j n", n=GRID_W)
                                msk = mask_na[:, :].rearrange("p (o n) -> p o n", o=1).broadcast_to([P, 14, GRID_W])
                                then(V.tensor_tensor(tab, tab, msk, ALU.add))
                        for p in un["passes"]:
                            if br == "A" and p == un["passes"][1] and ui and UNITS[ui - 1]["br"] == "A":
                                combine(ui - 1)
                            dve.wait_ge(s_full, N_PASS * l + p + 1)
                            S = ps[p % 2]
                            if br == "B" and m < TS:
                                j0 = (6 - 2 * m) * GRID_W
                                loc = S[:, P:5 * P].rearrange("p (r n) -> p r n", n=GRID_W)
                                then(V.tensor_tensor(loc, loc, backwards(na_tab[:, un["hh"], j0:j0 + 4 * P].rearrange("p (r n) -> p r n", n=GRID_W)), ALU.add))
                            if br == "C" and m < TS:
                                if m > 0:
                                    then(V.tensor_tensor(S[:, P:2 * P], S[:, P:2 * P], mask_sw[:, 0, :], ALU.add))
                                if m < TS - 1:
                                    then(V.tensor_tensor(S[:, w - P:w], S[:, w - P:w], mask_sw[:, 1, :], ALU.add))
                            c8 = p % 8
                            then(V.tensor_reduce(mx[:, c8:c8 + 1], S[:, 0:w], AX.X, ALU.max))
                            if br == "C":
                                h = un["head"]
                                V.tensor_scalar(negm[:, c8:c8 + 1], mx[:, c8:c8 + 1], sink_b[:, h:h + 1], -SCALE[br], ALU.max, ALU.mult).then_inc(s_max, 1)
                            else:
                                V.tensor_scalar(negm[:, c8:c8 + 1], mx[:, c8:c8 + 1], -SCALE[br], None, ALU.mult).then_inc(s_max, 1)
                    if 1 <= ui <= N_UNIT:
                        v = ui - 1
                        un = UNITS[v]
                        w = len(un["kb"]) * P
                        if un["br"] == "A" and not (ui < N_UNIT and UNITS[ui]["br"] == "A"):
                            combine(v)
                        if len(un["kb"]) > 4:
                            dve.wait_ge(t_full, N_UNIT * l + v + 1)
                            if v >= 2:
                                dve.wait_ge(o_full, N_UNIT * l + v - 1)
                            V.tensor_copy(probT[:, v % 2, 4 * P:5 * P], ps[2][:, 4 * P:5 * P]).then_inc(t_dve, 1)
                    if ui >= 2:
                        v = ui - 2
                        un = UNITS[v]
                        p, r = un["passes"][0] % 8, v % 8
                        dve.wait_ge(p_ready, N_PASS * l + un["passes"][-1] + 1)
                        if un["br"] == "C":
                            dve.wait_ge(es_ready, N_C * l + C_BEFORE[v] + 1)
                            then(V.tensor_tensor(sm[:, p:p + 1], sm[:, p:p + 1], es[:, v % 4:v % 4 + 1], ALU.add))
                        then(V.reciprocal(rinv[:, r:r + 1], sm[:, p:p + 1]))
                        dve.wait_ge(o_full, N_UNIT * l + v + 1)
                        col = O_COL[un["br"]] + HD * un["head"]
                        V.tensor_scalar(u[:, un["m"], col:col + HD], bank(6, 0, HD), rinv[:, r:r + 1], None, ALU.mult).then_inc(o_ev, 1)

                dve.wait_ge(o_ev, N_UNIT * (l + 1))
                for m in range(T):
                    then(V.tensor_tensor(sqs, u[:, m, AQ:AQ + 256], u[:, m, AQ:AQ + 256], ALU.mult))
                    then(V.tensor_reduce(s20[:, 4 * m:4 * m + 4], sqs.rearrange("p (h n) -> p h n", h=HEADS), AX.X, ALU.add))
                V.tensor_scalar(v20, s20, 1.0 / HD, EPS, ALU.mult, ALU.add).then_inc(on_var, 1)
                dve.wait_ge(on_sd, l + 1)
                then(V.reciprocal(r20, r20))
                for m in range(T):
                    o = u[:, m, AQ:AQ + 256].rearrange("p (h n) -> p h n", h=HEADS)
                    rs = r20[:, 4 * m:4 * m + 4].rearrange("p (h o) -> p h o", o=1).broadcast_to([P, HEADS, HD])
                    gs = sub_b[:, :].rearrange("p (o n) -> p o n", o=1).broadcast_to([P, HEADS, HD])
                    then(V.tensor_tensor(o, o, rs, ALU.mult))
                    V.tensor_tensor(o, o, gs, ALU.mult).then_inc(on_ready, 1)
                for m in range(T):
                    for half in range(2):
                        ks = slice(4 * half, 4 * half + 4)
                        dve.wait_ge(ot_high, 2 * (T * l + m) + half + 1)
                        low_part(oT[1][:, ks, m * P:(m + 1) * P], bank(2 * (m % 2) + half), oT[0][:, ks, m * P:(m + 1) * P], ot_low)

                for j in range(NG_GATE):
                    half, br = divmod(j, 4)
                    for kq in range(NQ + 1):
                        g = chunk_no(l, CH_IN + (NQ + 1) * j + kq)
                        if kq == NQ:
                            for m in range(T):
                                q = T * j + m
                                dve.wait_ge(g_sig, NG_GATE * T * l + q + 1)
                                if m < T - 1:
                                    dve.wait_ge(b_full, (T - 1) * (NG_GATE * l + j) + m + 1)
                                else:
                                    dve.wait_ge(ring_used, g + 1)
                                if br == 0:
                                    dst = merged[:, m, half * NW:(half + 1) * NW]
                                else:
                                    dst = gtmp[:, q % 2, :]
                                    if ADDS[q - 1]:
                                        dve.wait_ge(g_add, 6 * T * l + ADDS[q - 1])
                                V.tensor_tensor(dst, sig[:, q % SIG, :], bank(6 + q % 2), ALU.mult).then_inc(g_mul, 1)
                        split_low(g + HIGH)
                for m in range(T):
                    for half in range(2):
                        ks = slice(4 * half, 4 * half + 4)
                        dve.wait_ge(mt_high, 2 * (T * l + m) + half + 1)
                        low_part(mergedT[1][:, ks, m * P:(m + 1) * P], bank(4 + 2 * (m % 2) + half), mergedT[0][:, ks, m * P:(m + 1) * P], mt_low)
                dve.wait_ge(wr_high, l + 1)
                V.tensor_tensor(w_r2[1][:, :, :], w_r[:, :, :], w_r2[0][:, :, :].bitcast(F32), ALU.subtract).then_inc(wr_ready, 1)

                def residual(half, m, g):
                    cols = slice(half * NW, (half + 1) * NW)
                    if m < T - 1:
                        dve.wait_ge(wo_full, (T - 1) * (2 * l + half) + m + 1)
                    else:
                        dve.wait_ge(ring_used, g + 1)
                    dve.wait_ge(x_in[m], 16 * (q2 + 1))
                    then(V.tensor_tensor(sq[:, 0:NW], bank((T * half + m) % 8), gate1_b[:, 1 if m < TS else 0, cols], ALU.mult))
                    return V.tensor_tensor(xt[:, m, cols], xt[:, m, cols], sq[:, 0:NW], ALU.add)

                for half in range(2):
                    for kq in range(NQ):
                        g = chunk_no(l, CH_DENSE - 2 * NQ + NQ * half + kq)
                        if kq == NQ - 1 and half == 0:
                            dve.wait_ge(gate1_in, 32 * (l + 1))
                            for m in range(T):
                                residual(0, m, g).then_inc(wo_half, 1)
                                dve.wait_ge(wo_half, T * l + m + 1)
                        if half == 0:
                            split_low(g + HIGH)
                for m in range(T + 1):
                    if m < T:
                        residual(1, m, g).then_inc(x_new, 1)
                        dve.wait_ge(x_new, T * l + m + 1)
                        stats(q2, m)
                    if m >= 1:
                        norm_lows(q2, m - 1, 2)
                for c in range(CH_DENSE - NQ, CH_DENSE):
                    split_low(chunk_no(l, c) + HIGH)

                dve.wait_ge(lg_full, l + 1)
                z = bank(6, 0, T * NE).rearrange("p (m e) -> p m e", m=T)
                col = lambda i: lgs[:, i, :].rearrange("p (m o) -> p m o", o=1).broadcast_to([P, T, NE])
                then(V.tensor_reduce(lgs[:, 0, :], z, AX.X, ALU.max))
                V.tensor_tensor(lg[:, :, :], z, col(0), ALU.subtract).then_inc(lg_sub, 1)
                dve.wait_ge(lg_exp, l + 1)
                then(V.tensor_reduce(lgs[:, 1, :], lg[:, :, :], AX.X, ALU.add))
                then(V.reciprocal(lgs[:, 1, :], lgs[:, 1, :]))
                V.tensor_tensor(lg[:, :, :], lg[:, :, :], col(1), ALU.mult).then_inc(aff_ready, 1)
                dve.wait_ge(affT_tr, l + 1)
                then(V.tensor_copy(affT[:, 0:NS], bank(1)[0:NE, :]))
                then(V.tensor_copy(affT[:, NS:NS + NP], bank(2, 0, NP)[0:NE, :]))
                for a, n, r0, rounds in ((0, NS, 0, CAP_S // 8), (NS, NP, CAP_S, CAP_P // 8)):
                    for r in range(rounds):
                        v8 = slice(r0 + 8 * r, r0 + 8 * r + 8)
                        src = affT[:, a:a + n]
                        then(V.max(top_v[:, v8], src))
                        then(V.max_index(top_i[:, v8], top_v[:, v8], src))
                        if r < rounds - 1:
                            then(V.match_replace(src, top_v[:, v8], src, -1.0))
                then(V.tensor_copy(top_f[:, 0:CAP_S], top_i[:, 0:CAP_S]))
                V.tensor_scalar(top_f[:, CAP_S:CAP], top_i[:, CAP_S:CAP], float(NS), None, ALU.add).then_inc(top_ready, 1)
                dve.wait_ge(topT_tr, l + 1)
                then(V.tensor_copy(gateT[:, 0:NE], bank(3, 0, NE)[0:CAP, :]))
                V.tensor_copy(idxT[:, 0:NE], bank(3, NE, 2 * NE)[0:CAP, :]).then_inc(topT_ready, 1)
                dve.wait_ge(topT_ready, l + 1)
                for b in range(2):
                    V.tensor_copy(idx_g[:, b, 0:1], idxT[:, b:b + 1]).then_inc(idx_ready, 1)

                def exp_then(ins, count):
                    ins.then_inc(exp_step, 1)
                    dve.wait_ge(exp_step, count)

                def rows_mod(b, turned, base):
                    for half in range(2):
                        dve.wait_ge(xe_tr, turned + (half + 1))
                        ks = slice(4 * half, 4 * half + 4)
                        views = []
                        for g, c0, c1 in ((1, 0, CAP_S), (0, CAP_S, CAP)):
                            def wide(t, o):
                                return t[:, o:o + 2 * KD].rearrange("p (k g) -> p k g", g=2)[:, ks, g:g + 1].broadcast_to([P, 4, c1 - c0])
                            views.append((bank(6 + half, 0, 4 * CAP).rearrange("p (k n) -> p k n", k=4)[:, :, c0:c1],
                                          wide(amod, (l * 2 + 1) * KD * 2), wide(modcol, (l * 6 + 3) * KD * 2)))
                        (s0, a0, h0), (s1, a1, h1) = views
                        V.tensor_tensor(s0, s0, a0, ALU.mult)
                        exp_then(V.tensor_tensor(s1, s1, a1, ALU.mult), base + (half + 1))
                        V.tensor_tensor(s0, s0, h0, ALU.add)
                        V.tensor_tensor(s1, s1, h1, ALU.add).then_inc(xe_mod, 1)

                def rows_low(b, highs):
                    for half in range(2):
                        ks = slice(4 * half, 4 * half + 4)
                        dve.wait_ge(xe_high, highs + (half + 1))
                        low_part(xeT[1][:, b, ks, :], bank(6 + half, 0, 4 * CAP), xeT[0][:, b, ks, :], xe_ready)

                def y_half(half, e, used):
                    dve.wait_ge(ring_used, used)
                    return V.scalar_tensor_tensor(out=ybuf[0:CAP, e, half * NW:(half + 1) * NW], in0=bank(4 + half)[0:CAP, :],
                                                  scalar=gate_c[:, e:e + 1], in1=gate2_b[0:CAP, half * NW:(half + 1) * NW],
                                                  op0=ALU.mult, op1=ALU.mult)

                g0 = chunk_no(l, CH_DENSE)

                def expert(e, i, last=False, gather=True):
                    n_exp = i * 2 + (NE * l + e)
                    down = (2 if last else 4) * NQ
                    for j in range(down + 2 * NQ):
                        g = g0 + CH_GATE0 + e * CH_EXP + j
                        if j == 3 and not last:
                            rows_mod(1 - e, n_exp * 2 + 2, n_exp * 2 + 2)
                        if j == 5 and not last:
                            rows_low(1 - e, n_exp * 2 + 2)
                        if j in (NQ, 2 * NQ):
                            half = j // NQ - 1
                            dve.wait_ge(silu_ready, n_exp * 2 + (half + 1))
                            dve.wait_ge(ring_used, i * (2 * CH_EXP) + g)
                            V.tensor_tensor(hid[0:CAP, half * NW:(half + 1) * NW], sil[0:CAP, half, :], bank(2 + half)[0:CAP, :], ALU.mult).then_inc(hid_ready, 1)
                        if j == 6 and gather:
                            V.tensor_copy(idx_g[:, e, 0:1], idxT[:, bass.ds(i * 2 + (e + 2), 1)]).then_inc(idx_ready, 1)
                        if j == 2 * NQ + 1:
                            dve.wait_ge(added, n_exp + (BUF - 1))
                            V.tensor_copy(gate_c[:, e:e + 1], gateT[:, bass.ds(i * 2 + e, 1)])
                            V.tensor_copy(idx_s[:, e, 0:1], idxT[:, bass.ds(i * 2 + e, 1)]).then_inc(gate_set, 1)
                        if j == (2 * NQ if last else 3 * NQ + 2):
                            for half in range(2):
                                ks = slice(4 * half, 4 * half + 4)
                                dve.wait_ge(hidT_high, n_exp * 2 + (half + 1))
                                low_part(hidT[1][:, ks, :], bank(6 + half, 0, 4 * CAP), hidT[0][:, ks, :], hidT_low)
                        if j == down + NQ:
                            dve.wait_ge(gate_set, n_exp + 1)
                            y_half(0, e, i * (2 * CH_EXP) + g)
                        if not by_pool(g + HIGH):
                            dve.wait_ge(high_done, i * (2 * CH_EXP) + (g + HIGH + 1))
                            V.tensor_tensor(low[:, (g + HIGH) % RING, :, :], ring[:, (g + HIGH) % RING, :, :],
                                            high[:, g % HIGH, :, :].bitcast(F32), ALU.subtract).then_inc(low_dve, 1)
                    y_half(1, e, i * (2 * CH_EXP) + (g + 1)).then_inc(y_ready, 1)

                rows_mod(0, 2 * NE * l, 2 * NE * l)
                rows_low(0, 2 * NE * l)
                for j in range(CH_GATE0):
                    split_low(g0 + j + HIGH)
                with dve.Fori(0, LOOPED) as i:
                    expert(0, i)
                    expert(1, i)
                expert(0, LOOPED, gather=False)
                expert(1, LOOPED, last=True, gather=False)

            dve.wait_ge(gfin_in, 16)
            for m in range(T):
                dve.wait_ge(x_in[m], 16 * (2 * L + 1))
                stats(2 * L, m, last=True)

        @block.gpsimd
        def _(pool):
            G = nc.gpsimd
            steps = [0]

            def then(ins):
                steps[0] += 1
                ins.then_inc(pool_step, 1)
                pool.wait_ge(pool_step, steps[0])

            def rope_tile(X, cos, sin, tmp, heads, q):
                t = tmp.rearrange("p (h a j q) -> p h a j q", h=heads, a=2, j=2)
                for j in range(2):
                    s = sin.rearrange("p (o a j q) -> p o a j q", o=1, a=2, j=2)[:, :, :, j, :].broadcast_to([P, heads, 2, q])
                    then(G.tensor_tensor(t[:, :, :, j, :], X[:, :, :, 1 - j, :], s, ALU.mult))
                flat = X.rearrange("p h a j q -> p h (a j q)")
                cc = cos.rearrange("p (o n) -> p o n", o=1).broadcast_to([P, heads, 4 * q])
                then(G.tensor_tensor(flat, flat, cc, ALU.mult))
                return G.tensor_tensor(flat, flat, tmp.rearrange("p (h n) -> p h n", h=heads), ALU.add)

            pool.sem_inc(added, BUF)
            for b in range(2):
                pool.wait_ge(mod_out[b], 16 * (L * N_MOD // 2 + 1))
            pool.wait_ge(const_in, 16 * N_CONST)

            for l in range(L):
                q1, q2 = 2 * l, 2 * l + 1
                if l:
                    pool.wait_ge(y_out, 16 * NE * l)
                    pool.wait_ge(xe_tr, 2 * NE * l)
                for m in range(T):
                    pool.dma_start(xt[:, m, :], tok_in(l, m)).then_inc(x_in[m], 16)

                for m in range(TS):
                    a, d = u_counts(l, 4 * T + m)
                    pool.wait_ge(u_act, a)
                    pool.wait_ge(u_dve, d)
                    for c0, heads, d4, t0 in ((AQ, 16, 8, 0), (CQ, 6, 16, 64)):
                        w = heads * 4 * d4
                        X = u[:, m, c0:c0 + w].rearrange("p (h a j q) -> p h a j q", h=heads, a=2, j=2)
                        ins = rope_tile(X, rope[:, m, t0:t0 + 4 * d4], rope[:, m, t0 + 4 * d4:t0 + 8 * d4], rtmp[:, 0:w], heads, d4)
                        if heads == 16:
                            then(ins)
                    ins.then_inc(rope_a, 1)
                    pool.wait_ge(rope_a, TS * l + m + 1)

                pool.wait_ge(pad_ready, l + 1)
                pool.dma_start(rpb_dram[l], rpad[:, :]).then_inc(pad_out, 16)
                pool.wait_ge(pad_out, 16 * (l + 1))
                for b in range(2):
                    if b:
                        last = UNITS[LAST_UNIT[BLOCKS.index(("B", 0))]]["passes"][-1]
                        pool.wait_ge(s_max, N_PASS * l + last + 1)
                    for h in range(2):
                        for r in range(2):
                            off = ((l * HEADS + 2 * b + h) * 15 + 1 - r) * 127
                            src = bass.AP(rpb_dram.tensor, off, [[1, GRID_W], [127, 14], [1, GRID_W]])
                            pool.dma_start(na_tab[64 * r:64 * r + 64, h, :].rearrange("p (j n) -> p j n", n=GRID_W), src).then_inc(natab_in, 16)

                n = 0
                for q in range(NG_GATE * T):
                    j, m = divmod(q, T)
                    if j % 4 == 0:
                        continue
                    pool.wait_ge(g_mul, NG_GATE * T * l + q + 1)
                    if n >= T:
                        pool.wait_ge(g_add, 6 * T * l + n - T + 1)
                    dst = merged[:, m, (j // 4) * NW:(j // 4 + 1) * NW]
                    G.tensor_tensor(dst, dst, gtmp[:, q % 2, :], ALU.add).then_inc(g_add, 1)
                    n += 1

                pool.wait_ge(g_mul, NG_GATE * T * (l + 1))
                for g in range(2):
                    pool.dma_start(gate1_b[:, g, :], mod_dram[l, g:g + 1, 2 * D:3 * D].broadcast_to([P, D])).then_inc(gate1_in, 16)
                pool.dma_start(gate2_b[0:CAP_S, :], mod_dram[l, 1:2, 5 * D:6 * D].broadcast_to([CAP_S, D])).then_inc(gate2_in, 16)
                pool.dma_start(gate2_b[CAP_S:CAP, :], mod_dram[l, 0:1, 5 * D:6 * D].broadcast_to([CAP_P, D])).then_inc(gate2_in, 16)

                pool.wait_ge(mt_tr, 2 * T * (l + 1))
                for m in range(T):
                    pool.dma_start(xt[:, m, :], tok_in(l, m)).then_inc(x_in[m], 16)
                for m in range(T):
                    pool.wait_ge(x_new, T * l + m + 1)
                    pool.dma_start(x_dram[m * P:(m + 1) * P, :], xt[:, m, :]).then_inc(x_out, 16)
                    pool.wait_ge(xn_ready, T * q2 + m + 1)
                    pool.dma_start(xn_dram[m * P:(m + 1) * P, :], xn_att[:, m % 2, :]).then_inc(xn_out[m % 2], 16)

                pool.wait_ge(x_out, 16 * T * (l + 1))
                for b in range(2):
                    pool.wait_ge(xn_out[b], xn_store(l, 4 - b))

                def gather(b, ready):
                    pool.wait_ge(idx_ready, ready)
                    pool.sem_inc(pool_held, 1)
                    pool.indirect_dma_start(out=xe[0:CAP, b, :], out_offset=None, in_=xn_dram,
                                            in_offset=bass.IndirectOffsetOnAxis(ap=idx_g[:, b, 0:1], axis=0)).then_inc(xe_in[b], 16)

                def split_low(g, i=None):
                    n = g + 1 if i is None else i * (2 * CH_EXP) + (g + 1)
                    pool.wait_ge(high_done, n)
                    G.tensor_tensor(low[:, g % RING, :, :], ring[:, g % RING, :, :], high[:, g % HIGH, :, :].bitcast(F32),
                                    ALU.subtract).then_inc(low_pool, 1)

                g0 = chunk_no(l, CH_DENSE) + HIGH - 1

                def expert(e, i, last=False, rows=True):
                    n_exp = i * 2 + (NE * l + e)
                    at = CH_GATE0 + e * CH_EXP
                    for j in range(2 * HIGH + HIGH, (4 if last else 6) * NQ + 1, HIGH):
                        split_low(g0 + at + j, i)
                        if j == 4 * HIGH and rows:
                            gather(e, i * 2 + (NE * l + e + 3))
                    pool.wait_ge(y_ready, n_exp + 2)
                    pool.sem_inc(pool_held, 1)
                    pool.indirect_dma_start(out=x_dram, out_offset=bass.IndirectOffsetOnAxis(ap=idx_s[:, e, 0:1], axis=0),
                                            in_=ybuf[0:CAP, e, :], in_offset=None, compute_op=ALU.add).then_inc(y_out, 16)
                    if not last:
                        for j in range(HIGH, 2 * HIGH + 1, HIGH):
                            split_low(g0 + at + CH_EXP + j, i)
                    pool.wait_ge(y_out, n_exp * 16 + 16)
                    pool.sem_inc(added, 1)

                split_low(g0)
                gather(0, NE * l + 1)
                gather(1, NE * l + 2)
                pool.wait_ge(gate2_in, 32 * (l + 1))
                for j in range(HIGH, CH_GATE0 + 2 * HIGH + 1, HIGH):
                    split_low(g0 + j)
                with pool.Fori(0, LOOPED) as i:
                    expert(0, i)
                    expert(1, i)
                expert(0, LOOPED, rows=False)
                expert(1, LOOPED, last=True, rows=False)

            pool.dma_start(gfin_b, g_final.rearrange("(a n) -> a n", a=1).broadcast_to([P, D])).then_inc(gfin_in, 16)
            pool.wait_ge(y_out, 16 * NE * L)
            pool.wait_ge(xe_tr, 2 * NE * L)
            q = 2 * L
            for m in range(T):
                pool.dma_start(xt[:, m, :], tok_in(L, m)).then_inc(x_in[m], 16)
            for m in range(T):
                pool.wait_ge(xn_ready, T * q + m + 1)
                dst = y_sample[0, m * P:(m + 1) * P, :] if m < TS else y_prompt[0]
                pool.dma_start(dst, xn_of(q)[:, m % 2, :]).then_inc(y_done[m % 2], 16)
            pool.wait_ge(kv_out, 16 * N_KV * L)
            for b in range(2):
                pool.wait_ge(y_done[b], 16 * (3 - b))


_INS = ["x_prompt", "x_sample", "cache_diff_k", "cache_diff_v", "cache_na_k", "cache_na_v", "cache_swa_k",
        "cache_swa_v", "cache_mla_ckv", "cache_mla_kpe", "c", "c_ctx", "w_mod", "b_mod", "g_norm1", "g_norm2", "w_in",
        "da_lambda", "da_subln", "na_rpb", "sw_sink", "mla_q_norm", "mla_w_uq", "mla_kv_norm", "mla_w_ukv", "w_gate",
        "w_branch", "w_out", "w_router", "w_e_gate", "w_e_up", "w_e_down", "g_final"]
_OUTS = [(1, NP, D), (1, NS, D), (1, L, NP, 4, 64), (1, L, NP, 4, 64), (1, L, NP, 4, 64), (1, L, NP, 4, 64),
         (1, L, NP, 2, 64), (1, L, NP, 2, 64), (1, L, NP, KVR), (1, L, NP, ROPE_D)]


def position_tables():
    t = np.arange(NS)
    parts = []
    for d4 in (8, 16):
        f = np.float32(10000.0) ** (-np.arange(d4, dtype=np.float32) / np.float32(d4))
        cos, sin = [], []
        for pos in (t // GRID_W, t % GRID_W):
            ang = pos.astype(np.float32)[:, None] * f.astype(np.float32)
            cc, s = np.cos(ang), np.sin(ang)
            cos += [cc, cc]
            sin += [-s, s]
        parts += cos + sin
    rope = np.concatenate(parts, axis=1).astype(np.float32)
    qc, kc = np.arange(GRID_W)[:, None], np.arange(GRID_W)[None, :]
    start = np.clip(qc - 8, 0, GRID_W - 16)
    na = np.where((kc >= start) & (kc < start + 16), 0.0, NEG).astype(np.float32)
    q, k = np.arange(P)[:, None], np.arange(P)[None, :]
    sw = np.stack([np.where(k >= q, 0.0, NEG), np.where(k <= q, 0.0, NEG)], axis=1).astype(np.float32)
    return np.eye(P, dtype=np.float32), rope, np.ascontiguousarray(np.concatenate([na, na], axis=0)[:, ::-1]), sw


def kernel(**inputs):
    import concourse.bacc as _bacc
    from concourse.bass_utils import run_bass_kernel_spmd as _run

    nc = _bacc.Bacc("TRN2", target_bir_lowering=False, num_devices=1)
    arrays, args = {}, []
    given = [(n, np.ascontiguousarray(inputs[n])) for n in _INS]
    given += list(zip(["k_ident", "k_rope", "k_mask_na", "k_mask_sw"], position_tables()))
    for name, a in given:
        arrays[f"in_{name}"] = a
        args.append(nc.dram_tensor(f"in_{name}", a.shape, mybir.dt.from_np(a.dtype), kind="ExternalInput").ap())
    for i, shape in enumerate(_OUTS):
        args.append(nc.dram_tensor(f"out_{i}", shape, F32, kind="ExternalOutput").ap())
    hybrid_step(nc, *args)
    r = _run(nc, [arrays], core_ids=[0])
    return tuple(r.results[0][f"out_{i}"] for i in range(len(_OUTS)))
```
